# Optimizing a Trainium2 kernel written in Bass

```python
import math
import jax, jax.numpy as jnp
from jax import lax
import numpy as np

D_MODEL = 1024
BATCH = 1
SEQ = 256
DEPTH = 2
DEC_BATCH = 8
DEC_SEQ = 1
PAST_LEN = 1024
PAGE_SIZE = 128

N_A_LAYERS = DEPTH // 2
N_B_LAYERS = DEPTH - N_A_LAYERS
RET_HEADS = D_MODEL // 256
RET_DK = D_MODEL // RET_HEADS
RET_DV = 2 * RET_DK
RET_CHUNK = 128
ROPE_BASE = 10000.0
FOX_HEADS = D_MODEL // 64
FOX_HD = 64
Q_BLOCK = 128
N_GROUPS = 4
EXPERTS_PER_GROUP = 8
N_EXPERTS = N_GROUPS * EXPERTS_PER_GROUP
TOP_K_INNER = 2
D_EXPERT = D_MODEL // 4
EPS = 1e-6
NEG_INF = -1e30

kernel_name = 'yoco_retnet_fox_hmoe_step'

def rmsnorm(x, g):
    xf = x.astype(jnp.float32)
    y = xf * lax.rsqrt(jnp.mean(xf * xf, axis=-1, keepdims=True) + EPS)
    return (y * g.astype(jnp.float32)).astype(x.dtype)

def adaln(c, w, b, n):
    m = jax.nn.silu(c) @ w + b
    return jnp.split(m[:, None, :], n, axis=-1)

def modulate(h, shift, scale):
    return h * (1.0 + scale) + shift

def rotary(x, pos):
    half = x.shape[-1] // 2
    inv = ROPE_BASE ** (-jnp.arange(half, dtype=jnp.float32) / half)
    ang = pos.astype(jnp.float32)[:, None] * inv[None, :]
    cos = jnp.cos(ang)[None, :, None, :]
    sin = jnp.sin(ang)[None, :, None, :]
    x1, x2 = x[..., :half], x[..., half:]
    return jnp.concatenate([x1 * cos - x2 * sin, x1 * sin + x2 * cos], axis=-1)

def retention_log_gamma():
    return jnp.log(1.0 - 2.0 ** (-5.0 - jnp.arange(RET_HEADS, dtype=jnp.float32)))

def retention_chunk(S, q, k, v, log_gamma):
    L = q.shape[1]
    t = jnp.arange(L, dtype=jnp.float32)
    rel = t[:, None] - t[None, :]
    decay = jnp.where(rel >= 0, jnp.exp(log_gamma[:, None, None] * jnp.maximum(rel, 0.0)), 0.0)
    a = jnp.einsum('bihd,bjhd->bhij', q, k) * decay[None]
    inner = jnp.einsum('bhij,bjhv->bihv', a, v)
    q_dec = jnp.exp((t[:, None] + 1.0) * log_gamma[None, :])
    cross = jnp.einsum('bihd,bhdv->bihv', q * q_dec[None, :, :, None], S)
    k_dec = jnp.exp((L - 1.0 - t)[:, None] * log_gamma[None, :])
    S_new = jnp.exp(L * log_gamma)[None, :, None, None] * S + jnp.einsum('bjhd,bjhv->bhdv', k * k_dec[None, :, :, None], v)
    return inner + cross, S_new

def retention_mixer(h, pos, S0, w_in, w_out):
    B, L, _ = h.shape
    qd = RET_HEADS * RET_DK
    vd = RET_HEADS * RET_DV
    proj = h @ w_in
    q, k, v, g = jnp.split(proj, [qd, 2 * qd, 2 * qd + vd], axis=-1)
    q = rotary(q.reshape(B, L, RET_HEADS, RET_DK).astype(jnp.float32), pos)
    k = rotary(k.reshape(B, L, RET_HEADS, RET_DK).astype(jnp.float32), pos) * (RET_DK ** -0.5)
    v = v.reshape(B, L, RET_HEADS, RET_DV).astype(jnp.float32)
    lg = retention_log_gamma()
    if S0 is None:
        S0 = jnp.zeros((B, RET_HEADS, RET_DK, RET_DV), jnp.float32)
    else:
        S0 = S0.astype(jnp.float32)
    if L > RET_CHUNK and L % RET_CHUNK == 0:
        nc = L // RET_CHUNK

        def to_chunks(t):
            return jnp.moveaxis(t.reshape(B, nc, RET_CHUNK, *t.shape[2:]), 1, 0)

        def step(S, qkv):
            o, S = retention_chunk(S, qkv[0], qkv[1], qkv[2], lg)
            return S, o

        S, o = lax.scan(step, S0, (to_chunks(q), to_chunks(k), to_chunks(v)))
        o = jnp.moveaxis(o, 0, 1).reshape(B, L, RET_HEADS, RET_DV)
    else:
        o, S = retention_chunk(S0, q, k, v, lg)
    o = o * lax.rsqrt(jnp.mean(o * o, axis=-1, keepdims=True) + EPS)
    o = o.reshape(B, L, vd).astype(h.dtype) * jax.nn.silu(g)
    return o @ w_out, S

def fox_block(q, k, v, Fq, Fk, q_pos, k_pos):
    s = jnp.einsum('bqhd,bkhd->bhqk', q, k).astype(jnp.float32) * (FOX_HD ** -0.5)
    s = s + jnp.swapaxes(Fq, 1, 2)[..., :, None] - jnp.swapaxes(Fk, 1, 2)[..., None, :]
    s = jnp.where((k_pos[None, :] <= q_pos[:, None])[None, None], s, NEG_INF)
    p = jax.nn.softmax(s, axis=-1)
    return jnp.einsum('bhqk,bkhd->bqhd', p.astype(v.dtype), v)

def fox_attention(q, k, v, Fq, Fk, q_pos, k_pos):
    B, Lq = q.shape[0], q.shape[1]
    if Lq > Q_BLOCK and Lq % Q_BLOCK == 0:
        nb = Lq // Q_BLOCK
        qb = jnp.moveaxis(q.reshape(B, nb, Q_BLOCK, *q.shape[2:]), 1, 0)
        Fqb = jnp.moveaxis(Fq.reshape(B, nb, Q_BLOCK, Fq.shape[-1]), 1, 0)
        pb = q_pos.reshape(nb, Q_BLOCK)
        out = lax.map(lambda a: fox_block(a[0], k, v, a[1], Fk, a[2], k_pos), (qb, Fqb, pb))
        return jnp.moveaxis(out, 0, 1).reshape(q.shape)
    return fox_block(q, k, v, Fq, Fk, q_pos, k_pos)

def fox_mixer(h, shared, pos, w_q, w_o):
    k_all, v_all, F = shared
    B, L, _ = h.shape
    Lk = k_all.shape[1]
    q = (h @ w_q).reshape(B, L, FOX_HEADS, FOX_HD)
    o = fox_attention(q, k_all, v_all, F[:, Lk - L:], F, pos, jnp.arange(Lk))
    return o.reshape(B, L, FOX_HEADS * FOX_HD) @ w_o

def build_shared_kv(x, c, past, p):
    B, L, _ = x.shape
    sh, sc = adaln(c, p['w_kvmod'], p['b_kvmod'], 2)
    n = modulate(rmsnorm(x, p['g_kv']), sh, sc)
    k, v = jnp.split(n @ p['w_kv'], 2, axis=-1)
    k = k.reshape(B, L, FOX_HEADS, FOX_HD)
    v = v.reshape(B, L, FOX_HEADS, FOX_HD)
    logf = jax.nn.log_sigmoid((n @ p['w_f']).astype(jnp.float32) + p['b_f'].astype(jnp.float32))
    if past is None:
        k_all, v_all, lf_all = k, v, logf
    else:
        k_all = jnp.concatenate([past[0].astype(k.dtype), k], axis=1)
        v_all = jnp.concatenate([past[1].astype(v.dtype), v], axis=1)
        lf_all = jnp.concatenate([past[2].astype(jnp.float32), logf], axis=1)
    F = jnp.cumsum(lf_all, axis=1)
    return (k, v, logf), (k_all, v_all, F)

def hier_moe(h, w_rg, w_re, w_gate, w_up, w_down):
    B, L, _ = h.shape
    lg = (h @ w_rg).astype(jnp.float32)
    pg = jax.nn.softmax(lg, axis=-1)
    _, gi = lax.top_k(lg, 1)
    g_onehot = jax.nn.one_hot(gi[..., 0], N_GROUPS, dtype=jnp.float32)
    p_group = jnp.sum(pg * g_onehot, axis=-1, keepdims=True)
    le = (h @ w_re).astype(jnp.float32).reshape(B, L, N_GROUPS, EXPERTS_PER_GROUP)
    le_sel = jnp.einsum('blge,blg->ble', le, g_onehot)
    tv, ti = lax.top_k(le_sel, TOP_K_INNER)
    w_sel = jax.nn.softmax(tv, axis=-1) * p_group
    ids = gi * EXPERTS_PER_GROUP + ti
    gates = jnp.einsum('blk,blke->ble', w_sel, jax.nn.one_hot(ids, N_EXPERTS, dtype=jnp.float32))
    a = jax.nn.silu(h @ w_gate) * (h @ w_up)
    a = (a.reshape(B, L, N_EXPERTS, D_EXPERT) * gates[..., None].astype(a.dtype)).reshape(B, L, N_EXPERTS * D_EXPERT)
    return a @ w_down

def trunk(x, c, ret_state, past, p):
    B, L, _ = x.shape
    P = 0 if past is None else past[0].shape[1]
    pos = P + jnp.arange(L)
    new_ret = []
    kv_rows = None
    shared = None
    for l in range(DEPTH):
        sh1, sc1, g1, sh2, sc2, g2 = adaln(c, p['w_mod'][l], p['b_mod'][l], 6)
        if l < N_A_LAYERS:
            h = modulate(rmsnorm(x, p['g_mix'][l]), sh1, sc1)
            s0 = None if ret_state is None else ret_state[l]
            o, s_new = retention_mixer(h, pos, s0, p['w_ret_in'][l], p['w_ret_out'][l])
            new_ret.append(s_new)
        else:
            if l == N_A_LAYERS:
                kv_rows, shared = build_shared_kv(x, c, past, p)
            h = modulate(rmsnorm(x, p['g_mix'][l]), sh1, sc1)
            o = fox_mixer(h, shared, pos, p['w_fq'][l - N_A_LAYERS], p['w_fo'][l - N_A_LAYERS])
        x = x + g1 * o
        h = modulate(rmsnorm(x, p['g_ffn'][l]), sh2, sc2)
        x = x + g2 * hier_moe(h, p['w_rg'][l], p['w_re'][l], p['w_e_gate'][l], p['w_e_up'][l], p['w_e_down'][l])
    y = rmsnorm(x, p['g_final'])
    return y, jnp.stack(new_ret, axis=0), kv_rows

def setup_inputs(seed: int = 0) -> dict:
    key = jax.random.key(seed)
    ks = jax.random.split(key, 32)
    D = D_MODEL
    n_pages = PAST_LEN // PAGE_SIZE
    n_used = DEC_BATCH * n_pages
    n_pool = (n_used * 5) // 4
    qd = RET_HEADS * RET_DK
    vd = RET_HEADS * RET_DV
    fd = FOX_HEADS * FOX_HD
    ef = N_EXPERTS * D_EXPERT
    nrm = jax.random.normal
    page_table = jax.random.permutation(ks[9], n_pool)[:n_used].reshape(DEC_BATCH, n_pages).astype(jnp.int32)
    return {
        'x_prompt': nrm(ks[0], (BATCH, SEQ, D), jnp.float32),
        'x_sample': nrm(ks[1], (DEC_BATCH, DEC_SEQ, D), jnp.float32),
        'c_prompt': nrm(ks[2], (BATCH, D), jnp.float32),
        'c_sample': nrm(ks[3], (DEC_BATCH, D), jnp.float32),
        'state_ret': nrm(ks[4], (N_A_LAYERS, DEC_BATCH, RET_HEADS, RET_DK, RET_DV), jnp.float32) * (RET_DK ** -0.5),
        'cache_k': nrm(ks[5], (n_pool, PAGE_SIZE, FOX_HEADS, FOX_HD), jnp.float32),
        'cache_v': nrm(ks[6], (n_pool, PAGE_SIZE, FOX_HEADS, FOX_HD), jnp.float32),
        'cache_logf': jax.nn.log_sigmoid(2.5 + nrm(ks[7], (n_pool, PAGE_SIZE, FOX_HEADS), jnp.float32)),
        'page_table': page_table,
        'w_mod': nrm(ks[10], (DEPTH, D, 6 * D), jnp.float32) * D ** -0.5,
        'b_mod': 0.01 * nrm(ks[11], (DEPTH, 6 * D), jnp.float32),
        'g_mix': 1.0 + 0.01 * nrm(ks[12], (DEPTH, D), jnp.float32),
        'g_ffn': 1.0 + 0.01 * nrm(ks[13], (DEPTH, D), jnp.float32),
        'w_ret_in': nrm(ks[14], (N_A_LAYERS, D, 2 * qd + 2 * vd), jnp.float32) * D ** -0.5,
        'w_ret_out': nrm(ks[15], (N_A_LAYERS, vd, D), jnp.float32) * vd ** -0.5,
        'g_kv': 1.0 + 0.01 * nrm(ks[16], (D,), jnp.float32),
        'w_kvmod': nrm(ks[17], (D, 2 * D), jnp.float32) * D ** -0.5,
        'b_kvmod': 0.01 * nrm(ks[18], (2 * D,), jnp.float32),
        'w_kv': nrm(ks[19], (D, 2 * fd), jnp.float32) * D ** -0.5,
        'w_f': nrm(ks[20], (D, FOX_HEADS), jnp.float32) * D ** -0.5,
        'b_f': jax.random.uniform(ks[21], (FOX_HEADS,), jnp.float32, 1.0, 4.0),
        'w_fq': nrm(ks[22], (N_B_LAYERS, D, fd), jnp.float32) * D ** -0.5,
        'w_fo': nrm(ks[23], (N_B_LAYERS, fd, D), jnp.float32) * fd ** -0.5,
        'w_rg': nrm(ks[24], (DEPTH, D, N_GROUPS), jnp.float32) * D ** -0.5,
        'w_re': nrm(ks[25], (DEPTH, D, N_EXPERTS), jnp.float32) * D ** -0.5,
        'w_e_gate': nrm(ks[26], (DEPTH, D, ef), jnp.float32) * D ** -0.5,
        'w_e_up': nrm(ks[27], (DEPTH, D, ef), jnp.float32) * D ** -0.5,
        'w_e_down': nrm(ks[28], (DEPTH, ef, D), jnp.float32) * D_EXPERT ** -0.5,
        'g_final': 1.0 + 0.01 * nrm(ks[29], (D,), jnp.float32),
    }

def reference(x_prompt, x_sample, c_prompt, c_sample, state_ret, cache_k, cache_v, cache_logf, page_table,
              w_mod, b_mod, g_mix, g_ffn, w_ret_in, w_ret_out, g_kv, w_kvmod, b_kvmod, w_kv, w_f, b_f,
              w_fq, w_fo, w_rg, w_re, w_e_gate, w_e_up, w_e_down, g_final):
    p = dict(w_mod=w_mod, b_mod=b_mod, g_mix=g_mix, g_ffn=g_ffn, w_ret_in=w_ret_in, w_ret_out=w_ret_out,
             g_kv=g_kv, w_kvmod=w_kvmod, b_kvmod=b_kvmod, w_kv=w_kv, w_f=w_f, b_f=b_f, w_fq=w_fq, w_fo=w_fo,
             w_rg=w_rg, w_re=w_re, w_e_gate=w_e_gate, w_e_up=w_e_up, w_e_down=w_e_down, g_final=g_final)
    y_prompt, state_ret_prompt, kv_p = trunk(x_prompt, c_prompt, None, None, p)
    nb, n_pages = page_table.shape
    past_len = n_pages * PAGE_SIZE
    past_k = cache_k[page_table].reshape(nb, past_len, FOX_HEADS, FOX_HD)
    past_v = cache_v[page_table].reshape(nb, past_len, FOX_HEADS, FOX_HD)
    past_lf = cache_logf[page_table].reshape(nb, past_len, FOX_HEADS)
    y_sample, state_ret_sample, kv_s = trunk(x_sample, c_sample, state_ret, (past_k, past_v, past_lf), p)
    k_prompt, v_prompt, logf_prompt = kv_p
    k_sample, v_sample, logf_sample = kv_s
    return (y_prompt, y_sample, state_ret_prompt, state_ret_sample, k_prompt, v_prompt, logf_prompt, k_sample, v_sample, logf_sample)


_drawn_inputs = setup_inputs


def setup_inputs(seed=0):
    import zlib

    import numpy as np

    out = dict(_drawn_inputs(seed))
    spreads = {}
    factors = {'g_kv': 4.602, 'b_kvmod': 3.46, 'g_final': 5.776}
    for name, (base, spread) in spreads.items():
        noise = np.random.default_rng([zlib.crc32(name.encode()), seed]).standard_normal(out[name].shape)
        drawn = base * np.exp(spread * noise) if base else spread * noise
        out[name] = __import__('jax').numpy.asarray(drawn.astype(out[name].dtype))
    for name, factor in factors.items():
        out[name] = (out[name] * factor).astype(out[name].dtype)
    return out
```

```python
from contextlib import ExitStack

import numpy as np

import concourse.bass as bass
from concourse import mybir

F32 = mybir.dt.float32
I32 = mybir.dt.int32
ALU = mybir.AluOpType
ACT = mybir.ActivationFunctionType
AX = mybir.AxisListType.X
ds = bass.ds

P = 128
D = 1024
KT = D // P
TP, NS = 256, 8
T = TP + NS
NC = 1 + NS
RH, RK, RV = 4, 256, 512
RVT = RH * RV // P
FH, HD = 16, 64
PAST, PAGE = 1024, 128
NPG = PAST // PAGE
NPAGES = NS * NPG
NG, EG = 4, 8
NE = NG * EG
FF = D // 4
EPS = 1e-6
NEG = -1e30
R = 6
SW = 2048
S_MOD0, S_RET, S_RO, S_MOE0 = 0, 24, 72, 88
S_KV = S_MOE0 + 3 * NE
S_FQ = S_KV + 8
S_FO = S_FQ + 4
S_MOE1 = S_FO + 4
SLOTS = S_MOE1 + 3 * NE
GAMMA = [1.0 - 2.0 ** (-5.0 - h) for h in range(RH)]

CONST = {}
_at = 0
for _name, _n in (("ident", P), ("ones", P), ("half0", P), ("half1", P), ("cosq", T), ("sinq", T),
                  ("cosk", T), ("sink", T), ("decay", RH * TP), ("kdec", 2 * RH), ("upto", TP),
                  ("causal", 3 * P), ("negeye", FH), ("eps", 1), ("first4", NG), ("first8", EG)):
    CONST[_name] = (_at, _n)
    _at += _n
N_CONST = _at

V_BMOD, V_BKV, V_GAIN, V_BF = 0, 96, 112, 160
N_VEC = 161
G_MIX0, G_MIX1, G_FFN0, G_FFN1, G_KV, G_FINAL = range(6)
SH1, SC1, GT1, SH2, SC2, GT2 = range(6)


class Turns:

    def __init__(self):
        self.count = [0] * 8
        self.at = {}

    def add(self, key, bank):
        self.at[key] = (bank, self.count[bank], 0)
        self.count[bank] += 1

    def loop(self, steps, jobs):
        first = list(self.count)
        per = [sum(b == bank for _, b in jobs) for bank in range(8)]
        for key, bank in jobs:
            self.at[key] = (bank, self.count[bank], per[bank])
            self.count[bank] += 1
        self.count = [f + steps * n for f, n in zip(first, per)]


L = [0, 1, 2, 3]
X0, X1, X2, M = 4, 5, 6, 7


def plan_turns():
    t = Turns()
    t.add(("past", 0), X0)
    t.add(("past", 1), X1)
    t.add("past_total", X2)
    t.add("mod0", M)
    t.add(("rms", 0), X0)
    t.add("mod1", M)
    for i in range(8):
        for m in range(2):
            t.add(("qk", i, m), L[(2 * i + m) % 4])
    for i in range(8):
        for c in range(2):
            t.add(("v", i, c), L[(2 * i + c) % 4])
        t.add(("vs", i), (X0, X1)[i % 2])
    for h in range(RH):
        t.add(("ra", h), X0)
        t.add(("rk", h), X1)
        for v in range(4):
            t.add(("ro", h, v), L[v])
        for s in range(2):
            t.add(("rs", h, s), X2)
    t.add("os", X2)
    for i in range(8):
        for u in range(4):
            t.add(("vb", 4 * i + u), (X0, X1)[u % 2])
        for m in range(2):
            t.add(("g", i, m), L[(2 * i + m) % 4])
    for h in range(RH):
        t.add(("gn", h), L[h])
    t.add("kvmod", M)
    for n in range(4):
        for m in range(2):
            t.add(("rout", n, m), L[(2 * n + m) % 4])

    def moe(l):
        t.add(("rms", 1 + 2 * l), X0)
        t.add(("logits", l), X1)
        t.add(("gatesT", l), X2)
        jobs = []
        for pr in range(2):
            for e in range(2):
                jobs += [(("G", l, pr, e, m), L[m]) for m in range(2)]
                jobs += [(("U", l, pr, e, m), L[2 + m]) for m in range(2)]
            jobs += [(("D", l, pr, k), (X0, X1, X2, M)[k % 4]) for k in range(KT)]
        t.loop(8, jobs)

    moe(0)
    t.add(("rms", 2), X0)
    t.add("flogit", X1)
    t.add("logfT", X2)
    t.add("F", X0)
    for i in range(4):
        for m in range(2):
            t.add(("fk", i, m), L[(2 * i + m) % 4])
    for i in range(4):
        for c in range(2):
            t.add(("fv", i, c), L[(2 * i + c) % 4])
        t.add(("fvs", i), (X0, X1)[i % 2])
    for i in range(4):
        for m in range(2):
            t.add(("fq", i, m), L[(2 * i + m) % 4])
    t.add("own_score", X1)
    t.add("own_F", X2)
    t.loop(NS, [("sc", X0), (("ps", 0), L[0]), (("ps", 1), L[1]), ("mxT", X1), (("pT", 0), L[2]),
                ("mxb", X1), (("pT", 1), L[3]), (("po", 0), M), (("po", 1), M), ("den", X1),
                ("pv", X2)])
    for n in range(4):
        for m in range(2):
            t.add(("fout", n, m), L[(2 * n + m) % 4])
    moe(1)
    t.add(("rms", 4), X0)
    return t.at


class Steps:

    def __init__(self, eng, sem):
        self.eng, self.sem, self.n, self.offset = eng, sem, 0, None

    def step(self, ins):
        ins.then_inc(self.sem, 1)
        self.n += 1

    def wait(self):
        self.eng.wait_ge(self.sem, self.n if self.offset is None else self.offset + self.n)

    def enter(self, it, per):
        self.offset, self.per, self.start = it * per, per, self.n

    def leave(self, steps):
        assert self.n - self.start == self.per, (self.n - self.start, self.per)
        self.n += self.per * (steps - 1)
        self.offset = None


def build(nc, consts, x_in, c_in, vecs, wsmall, wstream, kcache, vcache, lfcache, ptable, state,
          y_out, sp_out, ss_out, k_out, vp_out, vs_out, lf_out):
    at = plan_turns()
    ctx = ExitStack()
    with ctx:
        def sb(name, shape, dt=F32):
            return ctx.enter_context(nc.sbuf_tensor(name, shape, dt))

        def sem(name):
            return ctx.enter_context(nc.semaphore(name))

        gates_dram = nc.dram_tensor("gates_scratch", (2, NE, T), F32, kind="Internal").ap()

        cst = sb("cst", [P, N_CONST])
        vec = sb("vec", [P, N_VEC])
        wsm = sb("wsm", [P, KT * FH + 2 * KT * 36])
        page_ids = sb("page_ids", [1, NPAGES], I32)
        x = sb("x", [P, KT, T])
        xn = sb("xn", [P, KT, T])
        h = sb("h", [P, KT, T])
        cs = sb("cs", [P, KT, NC])
        ring = sb("ring", [P, R, SW])
        mod = [sb(f"mod{l}", [P, 48, NC]) for l in range(2)]
        kvmod = sb("kvmod", [P, 16, NC])
        coef = sb("coef", [P, KT, NC])
        coef2 = sb("coef2", [P, KT, NC])
        root = sb("root", [P, T])
        rstd = sb("rstd", [P, T])
        ms = sb("ms", [P, KT, NS])
        past_F = sb("past_F", [P, NS, NPG * FH])
        past_tot = sb("past_tot", [P, NS * FH])

        arena_cols = 27400
        arena = sb("arena", [P, arena_cols])

        class Region:
            def __init__(self, start):
                self.at = start

            def take(self, *shape, rows=P):
                n = int(np.prod(shape))
                a = arena[0:rows, self.at:self.at + n]
                self.at += n
                assert self.at <= arena_cols, self.at
                if len(shape) == 2:
                    a = a.rearrange("p (a b) -> p a b", a=shape[0])
                if len(shape) == 3:
                    a = a.rearrange("p (a b c) -> p a b c", a=shape[0], b=shape[1])
                return a

        ret = Region(0)
        qk = ret.take(2 * KT, T)
        vtok = ret.take(2, RH * RV)
        vsm = ret.take(RVT, NS)
        gsil = ret.take(RVT, T)
        oret = ret.take(RVT, T)
        st = ret.take(4, 2, RV)
        at_sb = ret.take(2, 3 * P)
        ktok = ret.take(2, 2, RK)
        sp_sb = ret.take(2, RV)
        rot = ret.take(4, T)
        past_lf = gsil.rearrange("p a b -> p (a b)")[:, 0:NS * NPG * FH] \
            .rearrange("p (b g h) -> p b g h", b=NS, g=NPG)
        past_pre = gsil.rearrange("p a b -> p (a b)")[:, NS * NPG * FH:2 * NS * NPG * FH] \
            .rearrange("p (b g h) -> p b g h", b=NS, g=NPG)
        past_sum = gsil.rearrange("p a b -> p (a b)")[:, 2 * NS * NPG * FH:2 * NS * NPG * FH + NS * FH] \
            .rearrange("p (b h) -> p b h", b=NS)

        me = Region(0)
        act_g = me.take(2, T)
        glu = me.take(2, T)
        aff = me.take(4, T)
        gb = me.take(2, 2, T)
        lg = me.take(3, 36)
        r4 = me.take(8, 3, NG)
        r8 = me.take(8, 3, EG)
        r1 = me.take(8, 3)
        le4 = me.take(3, EG, NG)
        gates = me.take(3, NE)
        gatesT = me.take(T, rows=NE)
        fx = Region(0)
        n2 = fx.take(KT, T)
        fq = fx.take(KT, T)
        fk = fx.take(KT, T)
        fo = n2
        fv = fx.take(2, D)
        fvs = fx.take(KT, NS)
        qbd = fx.take(NS, FH)
        own = fx.take(KT, NS)
        s_own = fx.take(NS, FH)
        fz = fx.take(4, T, rows=FH)
        lf_tok = fx.take(2, FH)
        Fsb = fx.take(TP, rows=FH)
        lf_diag = fx.take(NS, FH, rows=FH)
        negF = fx.take(2, TP, rows=FH)
        q_st = fx.take(TP)
        k_st = fx.take(TP)
        v_st = fx.take(2, P)
        s_sb = fx.take(2, 3 * P)
        p_sb = fx.take(2, 3 * P)
        pT_sb = fx.take(2, 3 * P)
        hmax = fx.take(2, 2)
        hneg = fx.take(2, 2)
        hsum = fx.take(2, 2)
        hinv = fx.take(2, 2)
        sF = fx.take(NPG * FH)
        mxp = fx.take(FH)
        mx1 = fx.take(1, rows=FH)
        mxd = fx.take(FH, rows=FH)
        mx = fx.take(FH)
        sM = fx.take(NPG * FH)
        sO = fx.take(FH)
        pD = fx.take(NPG * FH)
        pO = fx.take(FH)
        psm = fx.take(FH)
        den = fx.take(FH)
        dinv = fx.take(FH)
        oO = fx.take(KT)
        oS = fx.take(KT)
        pages = Region(arena_cols - 12 * D)
        assert me.at <= pages.at and fx.at <= pages.at, (me.at, fx.at, pages.at)
        kpg = pages.take(4, D)
        vpg = pages.take(8, D)

        bank = [ctx.enter_context(nc.psum_tensor(f"bank{i}", [P, 512], F32)) for i in range(8)]
        filled = [sem(f"filled{i}") for i in range(8)]
        drained = [sem(f"drained{i}") for i in range(8)]

        consts_in = sem("consts_in")
        x_loaded = sem("x_loaded")
        lf_in = sem("lf_in")
        ids_in = sem("ids_in")
        slot_in = [sem(f"slot_in{r}") for r in range(R)]
        slot_used = sem("slot_used")
        state_in = [sem(f"state_in{r}") for r in range(4)]
        state_out = [sem(f"state_out{r}") for r in range(4)]
        state_scaled = sem("state_scaled")
        state_read = sem("state_read")
        k_in = [sem(f"k_in{r}") for r in range(4)]
        v_in = [sem(f"v_in{r}") for r in range(8)]
        k_used = sem("k_used")
        v_used = sem("v_used")
        gates_out = sem("gates_out")
        gates_in = [sem(f"gates_in{r}") for r in range(2)]
        past_ready = sem("past_ready")
        cond_ready = sem("cond_ready")
        squared = sem("squared")
        h_ready = sem("h_ready")
        x_ready = sem("x_ready")
        o_squared = sem("o_squared")
        o_rooted = sem("o_rooted")
        o_ready = sem("o_ready")
        dve_steps = sem("dve_steps")
        aff_ready = sem("aff_ready")
        route_e = sem("route_e")
        route_x = sem("route_x")
        gates_ready = sem("gates_ready")
        f_exp = sem("f_exp")
        f_neg = sem("f_neg")
        logf_ready = sem("logf_ready")
        qbd_ready = sem("qbd_ready")
        own_ready = sem("own_ready")
        diag_ready = sem("diag_ready")
        staged = sem("staged")
        negF_ready = sem("negF_ready")
        neg_max = sem("neg_max")
        p_raw = sem("p_raw")
        p_ready = sem("p_ready")
        mxp_ready = sem("mxp_ready")
        mxd_ready = sem("mxd_ready")
        shifted = sem("shifted")
        pd_ready = sem("pd_ready")
        psm_ready = sem("psm_ready")
        sample_done = sem("sample_done")
        sp_stored = sem("sp_stored")
        stored = sem("stored")

        def c_(name, rows=P):
            a, n = CONST[name]
            return cst[0:rows, a:a + n]

        ident, ones = c_("ident"), c_("ones")
        gain = [vec[:, V_GAIN + 8 * g:V_GAIN + 8 * g + 8] for g in range(6)]
        w_f = wsm[:, 0:KT * FH].rearrange("p (k n) -> p k n", k=KT)
        w_r = [wsm[:, KT * FH + l * KT * 36:KT * FH + (l + 1) * KT * 36].rearrange("p (k n) -> p k n", k=KT)
               for l in range(2)]

        def slot(n, rows=KT):
            return ring[:, n % R, :].rearrange("p (k c) -> p k c", k=rows)

        def turn(key, it=None):
            b, first, per = at[key]
            return b, first if it is None or per == 0 else it * per + first

        def result(eng, key, it=None):
            b, n = turn(key, it)
            eng.wait_ge(filled[b], n + 1)
            return bank[b]

        def free(key):
            return drained[at[key][0]]

        def moved(eng, key, it=None):
            b, n = turn(key, it)
            eng.wait_ge(drained[b], n + 1)

        def bc(ap, shape):
            return ap.to_broadcast(shape)

        block = ctx.enter_context(nc.Block())

        @block.sync
        def _(sp):
            sp.dma_start(cst[:], consts).then_inc(consts_in, 16)
            sp.dma_start(vec[:], vecs).then_inc(consts_in, 16)
            sp.dma_start(wsm[:], wsmall).then_inc(consts_in, 16)
            sp.dma_start(cs[:], c_in).then_inc(consts_in, 16)
            sp.dma_start(x[:], x_in).then_inc(x_loaded, 16)
            for r in range(R):
                sp.dma_start(ring[:, r, :], wstream[r]).then_inc(slot_in[r], 16)
            with sp.Fori(1, SLOTS // R) as lap:
                for r in range(R):
                    sp.wait_ge(slot_used, lap * R + (r - R + 1))
                    sp.dma_start(ring[:, r, :], wstream[ds(lap * R + r, 1)].rearrange("a p n -> p (a n)")) \
                        .then_inc(slot_in[r], 16)
            for n in range(SLOTS // R * R, SLOTS):
                sp.wait_ge(slot_used, n - R + 1)
                sp.dma_start(ring[:, n % R, :], wstream[n]).then_inc(slot_in[n % R], 16)

        @block.gpsimd
        def _(pool):
            pool.dma_start(page_ids[:], ptable).then_inc(ids_in, 16)
            pool.wait_ge(ids_in, 16)
            with pool.Fori(0, NPAGES) as j:
                page = pool.value_load(page_ids[0:1, ds(j, 1)], min_val=0, max_val=kcache.shape[0] - 1)
                pool.dma_start(past_lf.rearrange("p b g h -> p (b g) h")[:, ds(j, 1), :].rearrange("p a h -> p (a h)"),
                               lfcache[ds(page, 1)].rearrange("a p h -> p (a h)")).then_inc(lf_in, 16)
            for u in range(4):
                pool.dma_start(st[:, u, :, :], state[u]).then_inc(state_in[u], 16)
            for u in range(NS * RH):
                moved(pool, ("vb", u))
                pool.dma_start(ss_out[u], st[:, u % 4, :, :]).then_inc(state_out[u % 4], 16)
                nxt = u + 3
                if 4 <= nxt < NS * RH:
                    pool.wait_ge(state_out[nxt % 4], 16 * (nxt // 4))
                    pool.wait_ge(state_read, nxt - 3)
                    pool.dma_start(st[:, nxt % 4, :, :], state[nxt]).then_inc(state_in[nxt % 4], 16)

            def page_of(j):
                return pool.value_load(page_ids[0:1, ds(j, 1)], min_val=0, max_val=kcache.shape[0] - 1)

            def load_page(ring_, cache, sems, r, page):
                pool.dma_start(ring_[:, r, :], cache[ds(page, 1)].rearrange("a p n -> p (a n)")).then_inc(sems[r], 16)

            for r in range(4):
                pool.wait_ge(state_out[r], 16 * NS * RH // 4)
            pool.wait_ge(x_ready, 1)
            pool.wait_ge(sp_stored, 16 * RH)
            for j in range(4):
                load_page(kpg, kcache, k_in, j, page_of(j))
            for j in range(NPG):
                load_page(vpg, vcache, v_in, j, page_of(j))

            def load_gates(l):
                pool.wait_ge(gates_out, 16 * (l + 1))
                for pr in range(2):
                    if l == 1:
                        pool.wait_ge(aff_ready, 4 * 16)
                    pool.dma_start(gb[:, pr, :, :], gates_dram[l, 2 * pr:2 * pr + 2, :].partition_broadcast(P)) \
                        .then_inc(gates_in[pr], 16)
                with pool.Fori(1, 8) as it:
                    for pr in range(2):
                        pool.wait_ge(aff_ready, it * 8 + (64 * l - 8 + 4 * (pr + 1)))
                        src = gates_dram[l, ds(it * 4 + 2 * pr, 2), :].partition_broadcast(P)
                        pool.dma_start(gb[:, pr, :, :], src).then_inc(gates_in[pr], 16)

            load_gates(0)
            for j in range(4, NPG):
                page = page_of(j)
                pool.wait_ge(k_used, j - 3)
                load_page(kpg, kcache, k_in, j % 4, page)
            with pool.Fori(1, NS) as b:
                for j in range(NPG):
                    page = page_of(b * NPG + j)
                    if j < 3:
                        pool.wait_ge(k_used, b * (NPG - 1) + (j + 5 - (NPG - 1)))
                    elif j == 3:
                        result(pool, "sc", b - 1)
                    else:
                        pool.wait_ge(k_used, b * (NPG - 1) + (j - 3))
                    load_page(kpg, kcache, k_in, j % 4, page)
                for j in range(NPG):
                    page = page_of(b * NPG + j)
                    if j < NPG - 1:
                        pool.wait_ge(v_used, b * (NPG - 1) + (j + 1 - (NPG - 1)))
                    else:
                        result(pool, "pv", b - 1)
                    load_page(vpg, vcache, v_in, j, page)
            load_gates(1)
            for r in range(4):
                pool.wait_ge(state_out[r], 16 * NS * RH // 4)

        @block.tensor
        def _(pe):
            first_of_slot = [False]

            def mm(out, w, rhs, start, stop, done=None):
                ins = nc.tensor.matmul(out, w, rhs, start=start, stop=stop, skip_group_check=True)
                if first_of_slot[0]:
                    ins.then_inc(slot_used, 1)
                    first_of_slot[0] = False
                elif done is not None:
                    ins.then_inc(done, 1)

            def take_slot(n, it=None, laps=1):
                if it is None:
                    pe.wait_ge(slot_in[n % R], 16 * (n // R + 1))
                else:
                    pe.wait_ge(slot_in[n % R], it * (16 * laps) + 16 * (n // R + 1))
                first_of_slot[0] = n > 0

            def begin(key, it=None):
                b, n = turn(key, it)
                if it is not None or n > 0:
                    pe.wait_ge(drained[b], n)
                return bank[b], filled[b]

            def rms(r):
                ps, full = begin(("rms", r))
                pe.wait_ge(squared, r + 1)
                for k in range(KT):
                    mm(ps[:, 0:T], ones, xn[:, k, :], k == 0, k == KT - 1, full if k == KT - 1 else None)

            def columns(key, n, m, src, it=None, k0=0, kn=KT):
                w = slot(n)
                ps, full = begin(key, it)
                for k in range(KT):
                    mm(ps[:, 0:T], w[:, k, m * P:(m + 1) * P], src[:, k, :], k == 0, k == KT - 1,
                       full if k == KT - 1 else None)

            def modulation(n, ps, col, full=None, it=None):
                w = slot(n)
                for m in range(2):
                    for k in range(KT):
                        mm(ps[:, col(m)], w[:, k, m * P:(m + 1) * P], cs[:, k, :], k == 0, k == KT - 1,
                           full if m == 1 and k == KT - 1 else None)

            pe.wait_ge(consts_in, 64)
            pe.wait_ge(past_ready, 1)
            lfv = past_lf.rearrange("p b g h -> p (b g h)")
            prev = past_pre.rearrange("p b g h -> p (b g h)")
            for i in range(2):
                ps, full = begin(("past", i))
                mm(ps[:], c_("upto")[:, 0:P], lfv[:, i * 512:(i + 1) * 512], True, False)
                mm(ps[:], ones, prev[:, i * 512:(i + 1) * 512], False, True, full)
            ps, full = begin("past_total")
            mm(ps[:, 0:NS * FH], ones, past_sum.rearrange("p b h -> p (b h)"), True, True, full)

            pe.wait_ge(cond_ready, 1)
            ps, full = begin("mod0")
            w0 = 24 // R
            for n in range(R):
                take_slot(n)
                modulation(n, ps, lambda m: slice((2 * n + m) * NC, (2 * n + m + 1) * NC))
            with pe.Fori(1, w0) as lap:
                for r in range(R):
                    pe.wait_ge(slot_in[r], lap * 16 + 16)
                    first_of_slot[0] = True
                    modulation(r, ps, lambda m: ds(lap * (2 * R * NC) + (2 * r + m) * NC, NC))
            mm(ps[:, 48 * NC:49 * NC], ones, cs[:, 0, :], True, True, full)

            rms(0)
            pe.wait_ge(h_ready, 1)
            mod1_ps, mod1_full = begin("mod1")

            def mod1_slot(i):
                n = S_RET + 2 * i + 1
                take_slot(n)
                modulation(n, mod1_ps, lambda m: slice((2 * i + m) * NC, (2 * i + m + 1) * NC),
                           mod1_full if i == 23 else None)

            def values(key, skey, n, src, i):
                w = slot(n)
                for c in range(2):
                    ps, full = begin((key, i, c))
                    for k in range(KT):
                        mm(ps[:, 0:256], src[:, k, c * P:(c + 1) * P], w[:, k, :], k == 0, k == KT - 1,
                           full if k == KT - 1 else None)
                ps, full = begin((skey, i))
                for m in range(2):
                    for k in range(KT):
                        mm(ps[:, m * NS:(m + 1) * NS], w[:, k, m * P:(m + 1) * P], src[:, k, TP:T],
                           k == 0, k == KT - 1, full if m == 1 and k == KT - 1 else None)

            for i in range(8):
                take_slot(S_RET + 2 * i)
                for m in range(2):
                    columns(("qk", i, m), S_RET + 2 * i, m, h)
                mod1_slot(i)
            for i in range(8):
                take_slot(S_RET + 2 * (8 + i))
                values("v", "vs", S_RET + 2 * (8 + i), h, i)
                mod1_slot(8 + i)

            def head_scores(hd):
                for s in range(2):
                    moved(pe, ("qk", hd, s))
                    moved(pe, ("qk", 4 + hd, s))
                ps, full = begin(("ra", hd))
                for s in range(2):
                    mm(ps[:, 0:TP], qk[:, 8 + 2 * hd + s, 0:P], qk[:, 2 * hd + s, 0:TP], s == 0, s == 1)
                for s in range(2):
                    mm(ps[:, TP:TP + P], qk[:, 8 + 2 * hd + s, P:TP], qk[:, 2 * hd + s, P:TP], s == 0, s == 1,
                       full if s == 1 else None)
                ps, full = begin(("rk", hd))
                for c in range(2):
                    for s in range(2):
                        ins = nc.tensor.transpose(ps[:, (2 * c + s) * P:(2 * c + s + 1) * P],
                                                  qk[:, 8 + 2 * hd + s, c * P:(c + 1) * P], ident)
                ins.then_inc(full, 1)

            def head_output(hd):
                moved(pe, ("ra", hd))
                for c in range(2):
                    for i in (2 * hd, 2 * hd + 1):
                        moved(pe, ("v", i, c))
                sc = at_sb[:, hd % 2, :]
                for v in range(4):
                    ps, full = begin(("ro", hd, v))
                    col = slice(hd * RV + v * P, hd * RV + (v + 1) * P)
                    mm(ps[:, 0:TP], vtok[:, 0, col], sc[:, 0:TP], True, False)
                    mm(ps[:, P:TP], vtok[:, 1, col], sc[:, TP:TP + P], False, True, full)
                moved(pe, ("rk", hd))
                for s in range(2):
                    ps, full = begin(("rs", hd, s))
                    for c in range(2):
                        mm(ps[:], ktok[:, hd % 2, c, s * P:(s + 1) * P], vtok[:, c, hd * RV:(hd + 1) * RV], c == 0, c == 1,
                           full if c == 1 else None)

            head_scores(0)
            for hd in range(RH):
                if hd + 1 < RH:
                    head_scores(hd + 1)
                head_output(hd)

            def value_rows(u):
                b, hd = u // RH, u % RH
                ps, full = begin(("vb", u))
                for t in range(4):
                    mm(ps[:, t * P:(t + 1) * P], bc(vsm[:, 4 * hd + t, b:b + 1], [P, P]), ident,
                       True, True, full if t == 3 else None)

            for i in range(8):
                moved(pe, ("vs", i))
            os_ps, os_full = begin("os")

            def read_state(u):
                b, hd = u // RH, u % RH
                moved(pe, ("vb", u))
                for t in range(4):
                    for s in range(2):
                        ins = nc.tensor.matmul(os_ps[:, (4 * hd + t) * NS + b:(4 * hd + t) * NS + b + 1],
                                               st[:, u % 4, s, t * P:(t + 1) * P],
                                               qk[:, 2 * hd + s, TP + b:TP + b + 1],
                                               start=s == 0, stop=s == 1, skip_group_check=True)
                ins.then_inc(state_read, 1)

            for i in range(8):
                n = S_RET + 2 * (16 + i)
                value_rows(4 * i)
                value_rows(4 * i + 1)
                take_slot(n)
                columns(("g", i, 0), n, 0, h)
                read_state(4 * i)
                read_state(4 * i + 1)
                value_rows(4 * i + 2)
                value_rows(4 * i + 3)
                columns(("g", i, 1), n, 1, h)
                read_state(4 * i + 2)
                read_state(4 * i + 3)
                mod1_slot(16 + i)
            mm(os_ps[:, RVT * NS:RVT * NS + 1], ones, ones[:, 0:1], True, True, os_full)

            for hd in range(RH):
                pe.wait_ge(o_squared, hd + 1)
                ps, full = begin(("gn", hd))
                for t in range(4):
                    mm(ps[:, 0:T], ones, qk[:, 4 * hd + t, :], t == 0, t == 3, full if t == 3 else None)

            pe.wait_ge(o_ready, RH)
            kv_ps, kv_full = begin("kvmod")
            for n in range(4):
                outs = []
                for half in range(2):
                    j = S_RO + 2 * (2 * n + half)
                    take_slot(j)
                    w = slot(j)
                    for m in range(2):
                        if half == 0:
                            outs.append(begin(("rout", n, m)))
                        ps, full = outs[m]
                        for k in range(KT):
                            mm(ps[:, 0:T], w[:, k, m * P:(m + 1) * P], oret[:, half * KT + k, :],
                               half == 0 and k == 0, half == 1 and k == KT - 1,
                               full if half == 1 and k == KT - 1 else None)
                    take_slot(j + 1)
                    i = 2 * n + half
                    modulation(j + 1, kv_ps, lambda m: slice((2 * i + m) * NC, (2 * i + m + 1) * NC),
                               kv_full if i == 7 else None)

            def moe(l, base):
                rms(1 + 2 * l)
                pe.wait_ge(h_ready, 2 + 3 * l)
                ps, full = begin(("logits", l))
                for c in range(3):
                    rows = slice(c * P, min((c + 1) * P, T))
                    n = rows.stop - rows.start
                    for k in range(KT):
                        mm(ps[0:n, c * 36:(c + 1) * 36], h[:, k, rows], w_r[l][:, k, :], k == 0, k == KT - 1,
                           full if c == 2 and k == KT - 1 else None)
                pe.wait_ge(gates_ready, l + 1)
                ps, full = begin(("gatesT", l))
                for c in range(3):
                    n = min(P, T - c * P)
                    ins = nc.tensor.transpose(ps[0:NE, c * P:c * P + n], gates[0:n, c, :], ident[0:n, 0:n])
                ins.then_inc(full, 1)

                def pair(pr, it):
                    n0 = base + 6 * pr
                    for e in range(2):
                        for what, j in (("G", 0), ("U", 1)):
                            take_slot(n0 + 2 * e + j, it, 2)
                            for m in range(2):
                                columns((what, l, pr, e, m), n0 + 2 * e + j, m, h, it)
                    down = [slot(n0 + 4 + e, 2) for e in range(2)]
                    order = [(k, q) for k in range(4) for q in range(2)] + [(k, 2) for k in range(4)] + \
                            [(k, 3) for k in range(4)] + [(k, q) for k in range(4, KT) for q in range(4)]
                    take_slot(n0 + 4, it, 2)
                    outs, seen = {}, -1
                    for k, q in order:
                        if q > seen:
                            pe.wait_ge(aff_ready, it * 8 + (64 * l + 4 * pr + q + 1))
                            if q == 2:
                                n1 = n0 + 5
                                pe.wait_ge(slot_in[n1 % R], it * 32 + 16 * (n1 // R + 1))
                            seen = q
                        if k not in outs:
                            outs[k] = begin(("D", l, pr, k), it)
                        ps, full = outs[k]
                        mm(ps[:, 0:T], down[q // 2][:, q % 2, k * P:(k + 1) * P], aff[:, q, :], q == 0, q == 3,
                           full if q == 3 else slot_used if (k, q) == (KT - 1, 2) else None)

                with pe.Fori(0, NE // 4) as it:
                    for pr in range(2):
                        pair(pr, it)

            moe(0, S_MOE0)

            rms(2)
            pe.wait_ge(h_ready, 3)
            ps, full = begin("flogit")
            for k in range(KT):
                mm(ps[0:FH, 0:T], w_f[:, k, :], n2[:, k, :], k == 0, k == KT - 1, full if k == KT - 1 else None)
            for i in range(4):
                take_slot(S_KV + i)
                for m in range(2):
                    columns(("fk", i, m), S_KV + i, m, n2)
            pe.wait_ge(logf_ready, 1)
            ps, full = begin("logfT")
            for c in range(2):
                ins = nc.tensor.transpose(ps[:, c * FH:(c + 1) * FH], fz[:, 1, c * P:(c + 1) * P], ident[0:FH, 0:FH])
            ins.then_inc(full, 1)
            for i in range(4):
                take_slot(S_KV + 4 + i)
                if i == 0:
                    moved(pe, "logfT")
                    ps, full = begin("F")
                    nc.tensor.matmul(ps[0:FH, 0:TP], lf_tok[:, 0, :], c_("upto"), start=True, stop=False,
                                     skip_group_check=True)
                    nc.tensor.matmul(ps[0:FH, P:TP], lf_tok[:, 1, :], c_("upto")[:, 0:P], start=False, stop=True,
                                     skip_group_check=True).then_inc(full, 1)
                values("fv", "fvs", S_KV + 4 + i, n2, i)
            pe.wait_ge(h_ready, 4)
            for i in range(4):
                take_slot(S_FQ + i)
                for m in range(2):
                    columns(("fq", i, m), S_FQ + i, m, h)
            pe.wait_ge(diag_ready, 1)
            ps, full = begin("own_F")
            mm(ps[:, 0:NS * FH], ones[0:FH, :], lf_diag.rearrange("p b h -> p (b h)"), True, True, full)
            pe.wait_ge(own_ready, 1)
            ps, full = begin("own_score")
            for r, name in enumerate(("half0", "half1")):
                mm(ps[:, r * 64:(r + 1) * 64], c_(name), own.rearrange("p t b -> p (t b)"), True, True,
                   full if r else None)
            pe.wait_ge(qbd_ready, 1)

            with pe.Fori(0, NS) as b:
                ps, full = begin("sc", b)
                for j in range(NPG):
                    pe.wait_ge(k_in[j % 4], b * 32 + 16 * (j // 4 + 1))
                    for t in range(KT):
                        last = t == KT - 1
                        mm(ps[:, j * FH + 2 * t:j * FH + 2 * t + 2], kpg[:, j % 4, t * P:(t + 1) * P],
                           qbd[:, ds(b, 1), 2 * t:2 * t + 2].rearrange("p a c -> p (a c)"), True, True,
                           (full if j == NPG - 1 else k_used) if last else None)
                pe.wait_ge(staged, b * 3 + 3)
                pe.wait_ge(negF_ready, b + 1)
                for hh in range(2):
                    rows = slice(64 * hh, 64 * hh + 64)
                    ps, full = begin(("ps", hh), b)
                    for c in range(2):
                        cols = slice(0, P) if c == 0 else slice(P, 3 * P)
                        keys = slice(0, (c + 1) * P)
                        mm(ps[:, cols], q_st[rows, c * P:(c + 1) * P], k_st[rows, keys], True, False)
                        mm(ps[:, cols], ones[0:FH, :], negF[:, hh, keys], False, True, full if c else None)
                ps, full = begin("mxT", b)
                pe.wait_ge(mxp_ready, b + 1)
                nc.tensor.transpose(ps[0:FH, 0:P], mxp, ident).then_inc(full, 1)

                def turn_p(hh):
                    ps, full = begin(("pT", hh), b)
                    pe.wait_ge(p_ready, b * 2 + (hh + 1))
                    for i in range(3):
                        ins = nc.tensor.transpose(ps[:, i * P:(i + 1) * P], p_sb[:, hh, i * P:(i + 1) * P], ident)
                    ins.then_inc(full, 1)

                turn_p(0)
                pe.wait_ge(mxd_ready, b + 1)
                ps, full = begin("mxb", b)
                mm(ps[:, 0:FH], ones[0:FH, :], mxd, True, True, full)
                turn_p(1)
                for hh in range(2):
                    moved(pe, ("pT", hh), b)
                    ps, full = begin(("po", hh), b)
                    rows = slice(64 * hh, 64 * hh + 64)
                    mm(ps[rows, 0:TP], v_st[:, 0, rows], pT_sb[:, hh, 0:TP], True, False)
                    mm(ps[rows, P:TP], v_st[:, 1, rows], pT_sb[:, hh, TP:3 * P], False, True, full)
                pe.wait_ge(psm_ready, b + 1)
                ps, full = begin("den", b)
                mm(ps[:, 0:FH], ones, psm, True, True, full)
                ps, full = begin("pv", b)
                for j in range(NPG):
                    pe.wait_ge(v_in[j], b * 16 + 16)
                    for t in range(KT):
                        last = t == KT - 1
                        mm(ps[:, 2 * t:2 * t + 2], vpg[:, j, t * P:(t + 1) * P],
                           pD[:, j * FH + 2 * t:j * FH + 2 * t + 2], j == 0 and t == 0, j == NPG - 1,
                           (full if j == NPG - 1 else v_used) if last else None)

            pe.wait_ge(sample_done, NS)
            for hh in range(2):
                moved(pe, ("po", hh), NS - 1)
            for n in range(4):
                take_slot(S_FO + n)
                for m in range(2):
                    columns(("fout", n, m), S_FO + n, m, fo)
            moe(1, S_MOE1)
            rms(4)

        @block.scalar
        def _(act):
            def copy(out, in_, scale=None):
                if scale is None:
                    return nc.scalar.activation(out, in_, ACT.Copy)
                return nc.scalar.activation(out, in_, ACT.Copy, scale=scale)

            act.wait_ge(consts_in, 64)
            nc.scalar.activation(cs[:], cs[:], ACT.Silu).then_inc(cond_ready, 1)
            eps = c_("eps")

            def rms(r):
                if r == 0:
                    act.wait_ge(x_loaded, 16)
                else:
                    act.wait_ge(x_ready, r)
                nc.scalar.activation(xn[:], x[:], ACT.Square).then_inc(squared, 1)
                ps = result(act, ("rms", r))
                nc.scalar.activation(root[:], ps[:, 0:T], ACT.Sqrt, bias=eps, scale=1.0 / D) \
                    .then_inc(free(("rms", r)), 1)

            rms(0)
            for i in range(8):
                for c in range(2):
                    ps = result(act, ("v", i, c))
                    copy(vtok[:, c, i * 256:(i + 1) * 256], ps[:, 0:256]).then_inc(free(("v", i, c)), 1)
            for hd in range(RH):
                for v in range(4):
                    ps = result(act, ("ro", hd, v))
                    copy(oret[:, 4 * hd + v, 0:TP], ps[:, 0:TP]).then_inc(free(("ro", hd, v)), 1)
                if hd:
                    act.wait_ge(sp_stored, 16 * hd)
                for s in range(2):
                    ps = result(act, ("rs", hd, s))
                    copy(sp_sb[:, s, :], ps[:]).then_inc(free(("rs", hd, s)), 1)
                moved(act, ("rs", hd, 1))
                act.dma_start(sp_out[hd], sp_sb).then_inc(sp_stored, 16)

            def scale_state(u):
                act.wait_ge(state_in[u % 4], 16 * (u // 4 + 1))
                copy(st[:, u % 4, :, :], st[:, u % 4, :, :], GAMMA[u % RH]).then_inc(state_scaled, 1)

            for i in range(8):
                for m in range(2):
                    scale_state(4 * i + 2 * m)
                    scale_state(4 * i + 2 * m + 1)
                    ps = result(act, ("g", i, m))
                    nc.scalar.activation(gsil[:, 2 * i + m, :], ps[:, 0:T], ACT.Silu) \
                        .then_inc(free(("g", i, m)), 1)
            moved(act, "os")
            moved(act, ("ro", RH - 1, 3))
            for hd in range(RH):
                nc.scalar.activation(qk[:, 4 * hd:4 * hd + 4, :], oret[:, 4 * hd:4 * hd + 4, :], ACT.Square) \
                    .then_inc(o_squared, 1)
            for hd in range(RH):
                ps = result(act, ("gn", hd))
                nc.scalar.activation(rot[:, hd, :], ps[:, 0:T], ACT.Sqrt, bias=eps, scale=1.0 / RV) \
                    .then_inc(free(("gn", hd)), 1)

            def moe(l):
                rms(1 + 2 * l)
                act.wait_ge(route_x, l + 1)
                nc.scalar.activation(r4[:, 4, :, :], r4[:, 0, :, :], ACT.Exp)
                nc.scalar.activation(r1[:, 7, :], r1[:, 6, :], ACT.Exp).then_inc(route_e, 1)
                moved(act, ("gatesT", l))
                act.dma_start(gates_dram[l], gatesT).then_inc(gates_out, 16)
                with act.Fori(0, NE // 4) as it:
                    for pr in range(2):
                        for e in range(2):
                            for m in range(2):
                                ps = result(act, ("G", l, pr, e, m), it)
                                b, n = turn(("U", l, pr, e, m), it)
                                act.wait_ge(drained[b], n)
                                nc.scalar.activation(act_g[:, m, :], ps[:, 0:T], ACT.Silu) \
                                    .then_inc(free(("G", l, pr, e, m)), 1)

            moe(0)

            rms(2)
            act.wait_ge(f_neg, 1)
            nc.scalar.activation(fz[:, 2, :], fz[:, 1, :], ACT.Exp).then_inc(f_exp, 1)
            act.wait_ge(f_exp, 1)
            nc.scalar.activation(fz[:, 3, :], fz[:, 2, :], ACT.Ln, bias=1.0).then_inc(f_exp, 1)
            for i in range(4):
                for m in range(2):
                    ps = result(act, ("fk", i, m))
                    copy(fk[:, 2 * i + m, :], ps[:, 0:T]).then_inc(free(("fk", i, m)), 1)
            act.wait_ge(logf_ready, 1)
            act.dma_start(lf_out, fz[:, 1, :]).then_inc(stored, 16)
            moved(act, ("fk", 3, 0))
            moved(act, ("fk", 3, 1))
            act.dma_start(k_out, fk).then_inc(stored, 16)
            for i in range(4):
                for c in range(2):
                    ps = result(act, ("fv", i, c))
                    copy(fv[:, c, i * 256:(i + 1) * 256], ps[:, 0:256]).then_inc(free(("fv", i, c)), 1)
            moved(act, ("fv", 3, 0))
            moved(act, ("fv", 3, 1))
            act.dma_start(vp_out, fv).then_inc(stored, 16)
            moved(act, ("fvs", 2))
            moved(act, ("fvs", 3))
            act.dma_start(vs_out, fvs).then_inc(stored, 16)
            for i in range(4):
                for m in range(2):
                    ps = result(act, ("fq", i, m))
                    copy(fq[:, 2 * i + m, :], ps[:, 0:T], HD ** -0.5).then_inc(free(("fq", i, m)), 1)
            moved(act, ("fq", 3, 0))
            moved(act, ("fq", 3, 1))

            with act.Fori(0, NS) as b:
                copy(q_st, fq[:, ds(b, 1), 0:TP].rearrange("p a n -> p (a n)")).then_inc(staged, 1)
                copy(k_st, fk[:, ds(b, 1), 0:TP].rearrange("p a n -> p (a n)")).then_inc(staged, 1)
                copy(v_st, fv[:, :, ds(b * P, P)]).then_inc(staged, 1)
                for hh in range(2):
                    act.wait_ge(neg_max, b * 2 + (hh + 1))
                    nc.scalar.activation(p_sb[:, hh, 0:P], s_sb[:, hh, 0:P], ACT.Exp, bias=hneg[:, hh, 0:1],
                                         accum_out=hsum[:, hh, 0:1])
                    nc.scalar.activation(p_sb[:, hh, P:3 * P], s_sb[:, hh, P:3 * P], ACT.Exp,
                                         bias=hneg[:, hh, 1:2], accum_out=hsum[:, hh, 1:2]).then_inc(p_raw, 1)

                def move_pT(hh):
                    ps = result(act, ("pT", hh), b)
                    copy(pT_sb[:, hh, :], ps[:, 0:3 * P]).then_inc(free(("pT", hh)), 1)

                move_pT(0)
                act.wait_ge(shifted, b + 1)
                nc.scalar.activation(pD, sM, ACT.Exp)
                nc.scalar.activation(pO, sO, ACT.Exp).then_inc(pd_ready, 1)
                move_pT(1)
                for hh in range(2):
                    rows = slice(64 * hh, 64 * hh + 64)
                    ps = result(act, ("po", hh), b)
                    copy(fo[rows, ds(b, 1), 0:TP].rearrange("p a n -> p (a n)"), ps[rows, 0:TP]) \
                        .then_inc(free(("po", hh)), 1)

            moe(1)
            rms(4)
            act.wait_ge(h_ready, 6)
            act.dma_start(y_out, h[:]).then_inc(stored, 16)
            act.wait_ge(stored, 16 * 5)

        @block.vector
        def _(dve):
            own_steps = Steps(dve, dve_steps)
            step, wait = own_steps.step, own_steps.wait
            tt, stt, tsc = nc.vector.tensor_tensor, nc.vector.scalar_tensor_tensor, nc.vector.tensor_scalar

            dve.wait_ge(consts_in, 64)
            step(nc.vector.memset(past_pre[:, :, 0, :], 0.0))
            dve.wait_ge(lf_in, 16 * NPAGES)
            for g in range(1, NPG):
                wait()
                step(tt(past_pre[:, :, g, :], past_pre[:, :, g - 1, :], past_lf[:, :, g - 1, :], ALU.add))
            wait()
            tt(past_sum, past_pre[:, :, NPG - 1, :], past_lf[:, :, NPG - 1, :], ALU.add).then_inc(past_ready, 1)
            flat_F = past_F[:, :, :].rearrange("p b c -> p (b c)")
            for i in range(2):
                ps = result(dve, ("past", i))
                nc.vector.tensor_copy(flat_F[:, i * 512:(i + 1) * 512], ps[:]).then_inc(free(("past", i)), 1)
            ps = result(dve, "past_total")
            nc.vector.tensor_copy(past_tot[:], ps[:, 0:NS * FH]).then_inc(free("past_total"), 1)

            def add_bias(key, out, tiles, v0):
                ps = result(dve, key)
                tt(out, ps[:, 0:tiles * NC].rearrange("p (t c) -> p t c", c=NC),
                   bc(vec[:, v0:v0 + tiles].unsqueeze(2), [P, tiles, NC]), ALU.add).then_inc(free(key), 1)

            add_bias("mod0", mod[0][:], 48, V_BMOD)

            def normalise(r):
                moved(dve, ("rms", r))
                step(nc.vector.reciprocal(rstd[:], root[:]))
                wait()
                step(tt(xn[:], x[:], bc(rstd[:].unsqueeze(1), [P, KT, T]), ALU.mult))

            def modulate(out, cf, g, table, shift, scale):
                sh, sc = table[:, 8 * shift:8 * shift + 8, :], table[:, 8 * scale:8 * scale + 8, :]
                step(stt(cf[:], sc, 1.0, bc(gain[g].unsqueeze(2), [P, KT, NC]), ALU.add, ALU.mult))
                wait()
                step(tt(out[:, :, TP:T], xn[:, :, TP:T], cf[:, :, 1:NC], ALU.mult))
                for k in range(KT):
                    tsc(out[:, k, 0:TP], xn[:, k, 0:TP], cf[:, k, 0:1], sh[:, k, 0:1], ALU.mult, ALU.add)
                wait()
                tt(out[:, :, TP:T], out[:, :, TP:T], sh[:, :, 1:NC], ALU.add).then_inc(h_ready, 1)

            moved(dve, "mod0")
            normalise(0)
            modulate(h, coef, G_MIX0, mod[0], SH1, SC1)

            for i in range(8):
                cos, sin = (c_("cosq"), c_("sinq")) if i < 4 else (c_("cosk"), c_("sink"))
                ps0 = result(dve, ("qk", i, 0))
                ps1 = result(dve, ("qk", i, 1))
                if i:
                    moved(dve, ("qk", i - 1, 0))
                    moved(dve, ("qk", i - 1, 1))
                step(tt(rot[:, 0, :], ps0[:, 0:T], cos, ALU.mult))
                step(tt(rot[:, 1, :], ps1[:, 0:T], sin, ALU.mult))
                step(tt(rot[:, 2, :], ps0[:, 0:T], sin, ALU.mult))
                step(tt(rot[:, 3, :], ps1[:, 0:T], cos, ALU.mult))
                wait()
                tt(qk[:, 2 * i, :], rot[:, 0, :], rot[:, 1, :], ALU.subtract).then_inc(free(("qk", i, 0)), 1)
                tt(qk[:, 2 * i + 1, :], rot[:, 2, :], rot[:, 3, :], ALU.add).then_inc(free(("qk", i, 1)), 1)
            for i in range(8):
                ps = result(dve, ("vs", i))
                nc.vector.tensor_copy(vsm[:, 2 * i:2 * i + 2, :],
                                      ps[:, 0:2 * NS].rearrange("p (m b) -> p m b", m=2)) \
                    .then_inc(free(("vs", i)), 1)
            for hd in range(RH):
                ps = result(dve, ("ra", hd))
                dec = c_("decay")[:, hd * TP:(hd + 1) * TP]
                tt(at_sb[:, hd % 2, 0:TP], ps[:, 0:TP], dec, ALU.mult)
                tt(at_sb[:, hd % 2, TP:TP + P], ps[:, TP:TP + P], dec[:, 0:P], ALU.mult) \
                    .then_inc(free(("ra", hd)), 1)
                ps = result(dve, ("rk", hd))
                for c in range(2):
                    kd = c_("kdec")[:, c * RH + hd:c * RH + hd + 1]
                    ins = tsc(ktok[:, hd % 2, c, :], ps[:, c * RK:(c + 1) * RK], kd, None, ALU.mult)
                ins.then_inc(free(("rk", hd)), 1)
            for u in range(NS * RH):
                b, hd = u // RH, u % RH
                ps = result(dve, ("vb", u))
                dve.wait_ge(state_scaled, u + 1)
                for s in range(2):
                    ins = stt(st[:, u % 4, s, :], ps[:], qk[:, 8 + 2 * hd + s, TP + b:TP + b + 1],
                              st[:, u % 4, s, :], ALU.mult, ALU.add)
                ins.then_inc(free(("vb", u)), 1)
            ps = result(dve, "os")
            nc.vector.tensor_copy(oret[:, :, TP:T], ps[:, 0:RVT * NS].rearrange("p (t b) -> p t b", b=NS)) \
                .then_inc(free("os"), 1)
            add_bias("mod1", mod[1][:], 48, V_BMOD + 48)
            moved(dve, ("g", 7, 0))
            moved(dve, ("g", 7, 1))
            for hd in range(RH):
                tiles = slice(4 * hd, 4 * hd + 4)
                moved(dve, ("gn", hd))
                step(nc.vector.reciprocal(rot[:, hd, :], rot[:, hd, :]))
                wait()
                step(tt(oret[:, tiles, :], oret[:, tiles, :], bc(rot[:, hd:hd + 1, :], [P, 4, T]), ALU.mult))
                wait()
                tt(oret[:, tiles, :], oret[:, tiles, :], gsil[:, tiles, :], ALU.mult).then_inc(o_ready, 1)

            def residual(name, gate):
                for n in range(4):
                    for m in range(2):
                        t = 2 * n + m
                        ps = result(dve, (name, n, m))
                        stt(x[:, t, 0:TP], ps[:, 0:TP], gate[:, t, 0:1], x[:, t, 0:TP], ALU.mult, ALU.add)
                        tt(ms[:, t, :], ps[:, TP:T], gate[:, t, 1:NC], ALU.mult).then_inc(free((name, n, m)), 1)
                moved(dve, (name, 3, 0))
                moved(dve, (name, 3, 1))
                tt(x[:, :, TP:T], x[:, :, TP:T], ms[:], ALU.add).then_inc(x_ready, 1)

            residual("rout", mod[0][:, 8 * GT1:8 * GT1 + 8, :])
            add_bias("kvmod", kvmod[:], 16, V_BKV)

            def first_max(v, most, is_max, weight, first, best):
                n = v.shape[2]
                step(nc.vector.tensor_reduce(best[0], v, AX, ALU.max))
                wait()
                step(tt(is_max, v, bc(best[0].unsqueeze(2), [P, 3, n]), ALU.is_equal))
                wait()
                step(tt(weight, is_max, bc(first.unsqueeze(1), [P, 3, n]), ALU.mult))
                wait()
                step(nc.vector.tensor_reduce(best[1], weight, AX, ALU.max))
                wait()
                step(tt(most, weight, bc(best[1].unsqueeze(2), [P, 3, n]), ALU.is_equal))
                wait()

            def moe(l):
                normalise(1 + 2 * l)
                step(nc.vector.memset(lg, 0.0))
                modulate(h, coef, G_FFN0 + l, mod[l], SH2, SC2)
                dve.wait_ge(h_ready, 2 + 3 * l)
                step(nc.vector.memset(xn[:], 0.0))
                ps = result(dve, ("logits", l))
                nc.vector.tensor_copy(lg[:, 0:2, :], ps[:, 0:72].rearrange("p (c n) -> p c n", c=2))
                nc.vector.tensor_copy(lg[0:NS, 2, :], ps[0:NS, 72:108]).then_inc(free(("logits", l)), 1)
                moved(dve, ("logits", l))
                grp = lg[:, :, 0:NG]
                le = lg[:, :, NG:36]
                group = r4[:, 3, :, :]
                first_max(grp, group, r4[:, 1, :, :], r4[:, 2, :, :], c_("first4"), (r1[:, 0, :], r1[:, 1, :]))
                step(tt(r4[:, 0, :, :], grp, bc(r1[:, 0, :].unsqueeze(2), [P, 3, NG]), ALU.subtract))
                for c in range(3):
                    step(tt(le4[:, c, :, :], le[:, c, :].rearrange("p (g e) -> p e g", g=NG),
                            bc(group[:, c:c + 1, :], [P, EG, NG]), ALU.mult))
                wait()
                sel = r8[:, 0, :, :]
                step(nc.vector.tensor_reduce(sel, le4, AX, ALU.add))
                wait()
                one, two = r8[:, 3, :, :], r8[:, 7, :, :]
                first_max(sel, one, r8[:, 1, :, :], r8[:, 2, :, :], c_("first8"), (r1[:, 2, :], r1[:, 3, :]))
                step(stt(r8[:, 4, :, :], one, NEG, sel, ALU.mult, ALU.add))
                wait()
                first_max(r8[:, 4, :, :], two, r8[:, 5, :, :], r8[:, 6, :, :], c_("first8"),
                          (r1[:, 4, :], r1[:, 5, :]))
                tt(r1[:, 6, :], r1[:, 4, :], r1[:, 2, :], ALU.subtract).then_inc(route_x, 1)
                dve.wait_ge(route_e, l + 1)
                step(nc.vector.tensor_reduce(r1[:, 0, :], r4[:, 4, :, :], AX, ALU.add))
                wait()
                step(stt(r1[:, 1, :], r1[:, 7, :], 1.0, r1[:, 0, :], ALU.add, ALU.mult))
                wait()
                step(nc.vector.reciprocal(r1[:, 2, :], r1[:, 1, :]))
                wait()
                step(tt(r1[:, 3, :], r1[:, 2, :], r1[:, 7, :], ALU.mult))
                step(tt(r8[:, 1, :, :], one, bc(r1[:, 2, :].unsqueeze(2), [P, 3, EG]), ALU.mult))
                wait()
                step(tt(r8[:, 2, :, :], two, bc(r1[:, 3, :].unsqueeze(2), [P, 3, EG]), ALU.mult))
                wait()
                step(tt(r8[:, 4, :, :], r8[:, 1, :, :], r8[:, 2, :, :], ALU.add))
                wait()
                for c in range(3):
                    ins = tt(gates[:, c, :].rearrange("p (g e) -> p g e", g=NG),
                             bc(group[:, c, :].unsqueeze(2), [P, NG, EG]),
                             bc(r8[:, 4, c:c + 1, :], [P, NG, EG]), ALU.mult)
                ins.then_inc(gates_ready, 1)
                ps = result(dve, ("gatesT", l))
                nc.vector.tensor_copy(gatesT, ps[0:NE, 0:T]).then_inc(free(("gatesT", l)), 1)

                with dve.Fori(0, NE // 4) as it:
                    for pr in range(2):
                        for e in range(2):
                            for m in range(2):
                                moved(dve, ("G", l, pr, e, m), it)
                                ps = result(dve, ("U", l, pr, e, m), it)
                                tt(glu[:, m, :], ps[:, 0:T], act_g[:, m, :], ALU.mult) \
                                    .then_inc(free(("U", l, pr, e, m)), 1)
                                moved(dve, ("U", l, pr, e, m), it)
                                if e == 0 and m == 0:
                                    dve.wait_ge(gates_in[pr], it * 16 + (128 * l + 16))
                                tt(aff[:, 2 * e + m, :], glu[:, m, :], gb[:, pr, e, :], ALU.mult) \
                                    .then_inc(aff_ready, 1)
                        for k in range(KT):
                            ps = result(dve, ("D", l, pr, k), it)
                            tt(xn[:, k, :], ps[:, 0:T], xn[:, k, :], ALU.add).then_inc(free(("D", l, pr, k)), 1)
                for k in range(4, KT):
                    moved(dve, ("D", l, 1, k), NE // 4 - 1)
                gate = mod[l][:, 8 * GT2:8 * GT2 + 8, :]
                step(tt(ms[:], xn[:, :, TP:T], gate[:, :, 1:NC], ALU.mult))
                for t in range(KT):
                    stt(x[:, t, 0:TP], xn[:, t, 0:TP], gate[:, t, 0:1], x[:, t, 0:TP], ALU.mult, ALU.add)
                wait()
                tt(x[:, :, TP:T], x[:, :, TP:T], ms[:], ALU.add).then_inc(x_ready, 1)

            moe(0)

            normalise(2)
            modulate(n2, coef, G_KV, kvmod, 0, 1)
            modulate(h, coef2, G_MIX1, mod[1], SH1, SC1)
            step(nc.vector.memset(qbd, 0.0))
            ps = result(dve, "flogit")
            tsc(fz[:, 0, :], ps[0:FH, 0:T], vec[0:FH, V_BF:V_BF + 1], None, ALU.add).then_inc(free("flogit"), 1)
            moved(dve, "flogit")
            stt(fz[:, 1, :], fz[:, 0, :], -1.0, fz[:, 0, :], ALU.mult, ALU.min).then_inc(f_neg, 1)
            dve.wait_ge(f_exp, 2)
            stt(fz[:, 1, :], fz[:, 0, :], 0.0, fz[:, 3, :], ALU.min, ALU.subtract).then_inc(logf_ready, 1)
            dve.wait_ge(logf_ready, 1)
            tt(lf_diag, bc(ident[0:FH, 0:FH].unsqueeze(1), [FH, NS, FH]),
               bc(fz[:, 1, TP:T].unsqueeze(2), [FH, NS, FH]), ALU.mult).then_inc(diag_ready, 1)
            ps = result(dve, "logfT")
            nc.vector.tensor_copy(lf_tok, ps[:, 0:2 * FH].rearrange("p (c n) -> p c n", c=2)) \
                .then_inc(free("logfT"), 1)
            ps = result(dve, "F")
            nc.vector.tensor_copy(Fsb, ps[0:FH, 0:TP]).then_inc(free("F"), 1)
            for i in range(4):
                ps = result(dve, ("fvs", i))
                nc.vector.tensor_copy(fvs[:, 2 * i:2 * i + 2, :],
                                      ps[:, 0:2 * NS].rearrange("p (m b) -> p m b", m=2)) \
                    .then_inc(free(("fvs", i)), 1)
            moved(dve, ("fk", 3, 0))
            moved(dve, ("fk", 3, 1))
            moved(dve, ("fq", 3, 0))
            moved(dve, ("fq", 3, 1))
            tt(own, fq[:, :, TP:T], fk[:, :, TP:T], ALU.mult).then_inc(own_ready, 1)
            wait()
            for r in range(2):
                rows = slice(64 * r, 64 * r + 64)
                ins = nc.vector.tensor_copy(qbd[rows].rearrange("p b (t r) -> p r t b", r=2)[:, r, :, :],
                                            fq[rows, :, TP:T])
            ins.then_inc(qbd_ready, 1)
            ps = result(dve, "own_F")
            tt(s_own, ps[:, 0:NS * FH].rearrange("p (b h) -> p b h", b=NS),
               past_tot[:].rearrange("p (b h) -> p b h", b=NS), ALU.add).then_inc(free("own_F"), 1)
            moved(dve, "own_F")
            ps = result(dve, "own_score")
            for r in range(2):
                view = s_own.rearrange("p b (t r) -> p r b t", r=2)[:, r, :, :]
                ins = tt(view, ps[:, r * 64:(r + 1) * 64].rearrange("p (t b) -> p b t", t=KT), view, ALU.subtract)
            ins.then_inc(free("own_score"), 1)
            moved(dve, "own_score")
            moved(dve, "F")

            with dve.Fori(0, NS) as b:
                own_steps.enter(b, 7)
                for hh in range(2):
                    ins = tsc(negF[:, hh, :], Fsb, c_("negeye", FH)[:, ds(b * 2 + hh, 1)], None, ALU.mult)
                ins.then_inc(negF_ready, 1)
                ps = result(dve, "sc", b)
                tt(sF, ps[:, 0:NPG * FH], past_F[:, ds(b, 1), :].rearrange("p a c -> p (a c)"), ALU.subtract) \
                    .then_inc(free("sc"), 1)
                moved(dve, "sc", b)
                nc.vector.tensor_reduce(mxp, sF.rearrange("p (g h) -> p h g", g=NPG), AX, ALU.max) \
                    .then_inc(mxp_ready, 1)
                for hh in range(2):
                    ps = result(dve, ("ps", hh), b)
                    tt(s_sb[:, hh, :], ps[:, 0:3 * P], c_("causal"), ALU.add).then_inc(free(("ps", hh)), 1)
                    moved(dve, ("ps", hh), b)
                    nc.vector.tensor_reduce(hmax[:, hh, 0:1], s_sb[:, hh, 0:P], AX, ALU.max)
                    step(nc.vector.tensor_reduce(hmax[:, hh, 1:2], s_sb[:, hh, P:3 * P], AX, ALU.max))
                    wait()
                    tsc(hneg[:, hh, :], hmax[:, hh, :], -1.0, None, ALU.mult).then_inc(neg_max, 1)
                ps = result(dve, "mxT", b)
                nc.vector.tensor_reduce(mx1, ps[0:FH, 0:P], AX, ALU.max).then_inc(free("mxT"), 1)
                moved(dve, "mxT", b)
                tsc(mxd, ident[0:FH, 0:FH], mx1, None, ALU.mult).then_inc(mxd_ready, 1)

                def norm_p(hh):
                    dve.wait_ge(p_raw, b * 2 + (hh + 1))
                    step(nc.vector.reciprocal(hinv[:, hh, :], hsum[:, hh, :]))
                    wait()
                    tsc(p_sb[:, hh, 0:P], p_sb[:, hh, 0:P], hinv[:, hh, 0:1], None, ALU.mult)
                    tsc(p_sb[:, hh, P:3 * P], p_sb[:, hh, P:3 * P], hinv[:, hh, 1:2], None, ALU.mult) \
                        .then_inc(p_ready, 1)

                norm_p(0)
                ps = result(dve, "mxb", b)
                own_b = s_own[:, ds(b, 1), :].rearrange("p a h -> p (a h)")
                tt(mx, ps[:, 0:FH], own_b, ALU.max).then_inc(free("mxb"), 1)
                moved(dve, "mxb", b)
                tt(sM.rearrange("p (g h) -> p g h", g=NPG), sF.rearrange("p (g h) -> p g h", g=NPG),
                   bc(mx.unsqueeze(1), [P, NPG, FH]), ALU.subtract)
                tt(sO, own_b, mx, ALU.subtract).then_inc(shifted, 1)
                norm_p(1)
                dve.wait_ge(pd_ready, b + 1)
                nc.vector.tensor_reduce(psm, pD.rearrange("p (g h) -> p h g", g=NPG), AX, ALU.add) \
                    .then_inc(psm_ready, 1)
                ps = result(dve, "den", b)
                tt(den, ps[:, 0:FH], pO, ALU.add).then_inc(free("den"), 1)
                moved(dve, "den", b)
                step(nc.vector.reciprocal(dinv, den))
                half = [slice(64 * r, 64 * r + 64) for r in range(2)]
                by_half = lambda a, r: a[half[r]].rearrange("p (t r) -> p r t", r=2)[:, r, :]
                for r in range(2):
                    step(tt(oO[half[r]], by_half(pO, r),
                            fvs[half[r], :, ds(b, 1)].rearrange("p t a -> p (t a)"), ALU.mult))
                ps = result(dve, "pv", b)
                wait()
                for r in range(2):
                    ins = tt(oS[half[r]], by_half(ps[:, 0:FH], r), oO[half[r]], ALU.add)
                ins.then_inc(free("pv"), 1)
                moved(dve, "pv", b)
                for r in range(2):
                    ins = tt(fo[half[r], :, ds(b + TP, 1)].rearrange("p t a -> p (t a)"), oS[half[r]],
                             by_half(dinv, r), ALU.mult)
                ins.then_inc(sample_done, 1)
                own_steps.leave(NS)

            residual("fout", mod[1][:, 8 * GT1:8 * GT1 + 8, :])
            moe(1)
            normalise(4)
            wait()
            tt(h[:], xn[:], bc(gain[G_FINAL].unsqueeze(2), [P, KT, T]), ALU.mult).then_inc(h_ready, 1)


def constants():
    c = np.zeros((P, N_CONST), np.float32)

    def put(name, value):
        a, n = CONST[name]
        c[:, a:a + n] = value

    i = np.arange(P)
    put("ident", np.eye(P))
    put("ones", 1.0)
    put("half0", (i < 64)[:, None])
    put("half1", (i >= 64)[:, None])
    inv = np.float32(10000.0) ** (-i.astype(np.float32) / np.float32(P))
    pos = np.concatenate([np.arange(TP), np.full(NS, PAST)]).astype(np.float32)
    angle = (pos[None, :] * inv.astype(np.float32)[:, None]).astype(np.float32).astype(np.float64)
    for name, f in (("cos", np.cos), ("sin", np.sin)):
        put(name + "q", f(angle))
        put(name + "k", f(angle).astype(np.float32) * np.float32(RK ** -0.5))
    log_gamma = np.log(np.array(GAMMA, np.float32)).astype(np.float64)
    rel = np.arange(TP)[None, :] - i[:, None]
    for hd in range(RH):
        a = CONST["decay"][0] + hd * TP
        c[:, a:a + TP] = np.where(rel >= 0, np.exp(log_gamma[hd] * np.maximum(rel, 0)), 0.0)
        for k in range(2):
            c[:, CONST["kdec"][0] + k * RH + hd] = np.exp(log_gamma[hd] * (TP - 1 - k * P - i))
    put("upto", rel >= 0)
    future = np.where(i[None, :] <= i[:, None], 0.0, NEG)
    put("causal", np.concatenate([future, np.zeros((P, P)), future], 1))
    c[0:FH, CONST["negeye"][0]:CONST["negeye"][0] + FH] = -np.eye(FH)
    put("eps", EPS)
    put("first4", NG - np.arange(NG))
    put("first8", EG - np.arange(EG))
    return c


def features(a):
    return np.ascontiguousarray(a.reshape(a.shape[0], -1, P).transpose(2, 1, 0))


def column_slots(w):
    return w.reshape(KT, P, -1, 256).transpose(2, 1, 0, 3).reshape(-1, P, SW)


def weight_stream(w_mod, w_kvmod, w_ret_in, w_ret_out, w_kv, w_fq, w_fo, w_gate, w_up, w_down):
    s = np.empty((SLOTS, P, SW), np.float32)
    s[S_MOD0:S_MOD0 + 24] = column_slots(w_mod[0])
    s[S_RET:S_RET + 48:2] = column_slots(w_ret_in)
    s[S_RET + 1:S_RET + 48:2] = column_slots(w_mod[1])
    s[S_RO:S_RO + 16:2] = w_ret_out.reshape(2, KT, P, 4, 256).transpose(3, 0, 2, 1, 4).reshape(8, P, SW)
    s[S_RO + 1:S_RO + 16:2] = column_slots(w_kvmod)
    s[S_KV:S_KV + 8] = column_slots(w_kv)
    s[S_FQ:S_FQ + 4] = column_slots(w_fq)
    s[S_FO:S_FO + 4] = column_slots(w_fo)
    for l, base in ((0, S_MOE0), (1, S_MOE1)):
        m = s[base:base + 3 * NE].reshape(NE // 2, 6, P, SW)
        for j, w in ((0, w_gate), (1, w_up)):
            m[:, j:4:2] = column_slots(w[l]).reshape(NE // 2, 2, P, SW)
        m[:, 4:6] = w_down[l].reshape(NE // 2, 2, 2, P, D).transpose(0, 1, 3, 2, 4).reshape(NE // 2, 2, P, SW)
    return s


def kernel(x_prompt, x_sample, c_prompt, c_sample, state_ret, cache_k, cache_v, cache_logf, page_table,
           w_mod, b_mod, g_mix, g_ffn, w_ret_in, w_ret_out, g_kv, w_kvmod, b_kvmod, w_kv, w_f, b_f,
           w_fq, w_fo, w_rg, w_re, w_e_gate, w_e_up, w_e_down, g_final):
    import concourse.bacc as bacc
    from concourse.bass_utils import run_bass_kernel_spmd

    a = {k: np.asarray(v) for k, v in locals().items() if k not in ("bacc", "run_bass_kernel_spmd")}
    pool = a["cache_k"].shape[0]
    vectors = np.zeros((P, N_VEC), np.float32)
    vectors[:, V_BMOD:V_BMOD + 96] = a["b_mod"].reshape(96, P).T
    vectors[:, V_BKV:V_BKV + 16] = a["b_kvmod"].reshape(16, P).T
    gains = (a["g_mix"][0], a["g_mix"][1], a["g_ffn"][0], a["g_ffn"][1], a["g_kv"], a["g_final"])
    vectors[:, V_GAIN:V_GAIN + 48] = np.concatenate(gains).reshape(48, P).T
    vectors[0:FH, V_BF] = a["b_f"]
    small = [a["w_f"].reshape(KT, P, FH).transpose(1, 0, 2).reshape(P, -1)]
    for l in range(2):
        both = np.concatenate([a["w_rg"][l], a["w_re"][l]], 1)
        small.append(both.reshape(KT, P, 36).transpose(1, 0, 2).reshape(P, -1))
    ins = {
        "consts": constants(),
        "x_in": features(np.concatenate([a["x_prompt"][0], a["x_sample"][:, 0]])),
        "c_in": features(np.concatenate([a["c_prompt"], a["c_sample"]])),
        "vecs": vectors,
        "wsmall": np.concatenate(small, 1),
        "wstream": weight_stream(a["w_mod"], a["w_kvmod"], a["w_ret_in"][0], a["w_ret_out"][0], a["w_kv"],
                                 a["w_fq"][0], a["w_fo"][0], a["w_e_gate"], a["w_e_up"], a["w_e_down"]),
        "kcache": a["cache_k"].reshape(pool, PAGE, KT, P).transpose(0, 3, 2, 1).reshape(pool, P, D),
        "vcache": a["cache_v"].reshape(pool, PAGE, D),
        "lfcache": a["cache_logf"],
        "ptable": a["page_table"].reshape(1, NPAGES),
        "state": a["state_ret"].reshape(NS * RH, 2, P, RV).transpose(0, 2, 1, 3),
    }
    outs = {
        "y_out": (P, KT, T), "sp_out": (RH, P, 2, RV), "ss_out": (NS * RH, P, 2, RV), "k_out": (P, KT, T),
        "vp_out": (P, 2, D), "vs_out": (P, KT, NS), "lf_out": (FH, T),
    }
    nc = bacc.Bacc("TRN2", target_bir_lowering=False, num_devices=1)
    arrays, args = {}, []
    for name, v in ins.items():
        v = np.ascontiguousarray(v)
        arrays[name] = v
        args.append(nc.dram_tensor(name, v.shape, mybir.dt.from_np(v.dtype), kind="ExternalInput").ap())
    for name, shape in outs.items():
        args.append(nc.dram_tensor(name, shape, F32, kind="ExternalOutput").ap())
    build(nc, *args)
    r = run_bass_kernel_spmd(nc, [arrays], core_ids=[0]).results[0]

    y = r["y_out"].transpose(2, 1, 0).reshape(T, D)
    k = r["k_out"].transpose(2, 1, 0).reshape(T, FH, HD)
    vp = r["vp_out"].transpose(1, 0, 2).reshape(1, TP, FH, HD)
    vs = r["vs_out"].transpose(2, 1, 0).reshape(NS, 1, FH, HD)
    lf = r["lf_out"].T
    sp = r["sp_out"].transpose(0, 2, 1, 3).reshape(1, 1, RH, RK, RV)
    ss = r["ss_out"].transpose(0, 2, 1, 3).reshape(1, NS, RH, RK, RV)
    return (y[None, :TP], y[TP:, None], sp, ss, k[None, :TP], vp, lf[None, :TP], k[TP:, None], vs, lf[TP:, None])
```

```python
from contextlib import ExitStack

import numpy as np

import concourse.bass as bass
from concourse import mybir

F32 = mybir.dt.float32
I32 = mybir.dt.int32
ALU = mybir.AluOpType
ACT = mybir.ActivationFunctionType
AX = mybir.AxisListType.X
ds = bass.ds

P = 128
D = 1024
KT = D // P
TP, NS = 256, 8
T = TP + NS
NC = 1 + NS
RH, RK, RV = 4, 256, 512
RVT = RH * RV // P
FH, HD = 16, 64
PAST, PAGE = 1024, 128
NPG = PAST // PAGE
NPAGES = NS * NPG
NG, EG = 4, 8
NE = NG * EG
FF = D // 4
EPS = 1e-6
NEG = -1e30
R = 6
SW = 2048
S_MOD0, S_RET, S_RO, S_MOE0 = 0, 24, 72, 88
S_KV = S_MOE0 + 3 * NE
S_FQ = S_KV + 8
S_FO = S_FQ + 4
S_MOE1 = S_FO + 4
SLOTS = S_MOE1 + 3 * NE
GAMMA = [1.0 - 2.0 ** (-5.0 - h) for h in range(RH)]

CONST = {}
_at = 0
for _name, _n in (("ident", P), ("ones", P), ("half0", P), ("half1", P), ("cosq", T), ("sinq", T),
                  ("cosk", T), ("sink", T), ("decay", RH * TP), ("kdec", 2 * RH), ("upto", TP),
                  ("causal", 3 * P), ("negeye", FH), ("eps", 1), ("first4", NG), ("first8", EG)):
    CONST[_name] = (_at, _n)
    _at += _n
N_CONST = _at

V_BMOD, V_BKV, V_GAIN, V_BF = 0, 96, 112, 160
N_VEC = 161
G_MIX0, G_MIX1, G_FFN0, G_FFN1, G_KV, G_FINAL = range(6)
SH1, SC1, GT1, SH2, SC2, GT2 = range(6)


class Turns:

    def __init__(self):
        self.count = [0] * 8
        self.at = {}

    def add(self, key, bank):
        self.at[key] = (bank, self.count[bank], 0)
        self.count[bank] += 1

    def loop(self, steps, jobs):
        first = list(self.count)
        per = [sum(b == bank for _, b in jobs) for bank in range(8)]
        for key, bank in jobs:
            self.at[key] = (bank, self.count[bank], per[bank])
            self.count[bank] += 1
        self.count = [f + steps * n for f, n in zip(first, per)]


L = [0, 1, 2, 3]
X0, X1, X2, M = 4, 5, 6, 7


def plan_turns():
    t = Turns()
    t.loop(24 // R, [(("row0", r), (X1, X2)[r % 2]) for r in range(R)] + [("mod0", M)])
    t.add(("rms", 0), X0)
    t.add("mod1", M)
    for i in range(8):
        for m in range(2):
            t.add(("qk", i, m), L[(2 * i + m) % 4])
    for i in range(8):
        for c in range(2):
            t.add(("v", i, c), L[(2 * i + c) % 4])
        t.add(("vs", i), (X0, X1)[i % 2])
    t.add(("past", 0), X0)
    t.add(("past", 1), X1)
    t.add("past_total", X0)
    for i in range(16):
        t.add(("row1", i), X2)
    for h in range(RH):
        t.add(("ra", h), X0)
        t.add(("rk", h), X1)
        for v in range(4):
            t.add(("ro", h, v), L[v])
        for s in range(2):
            t.add(("rs", h, s), X2)
    for i in range(8):
        for u in range(4):
            t.add(("vb", 4 * i + u), X0)
        for m in range(2):
            t.add(("g", i, m), L[(2 * i + m) % 4])
        t.add(("row1", 16 + i), X2)
    for h in range(RH):
        t.add(("os", h), X1)
        t.add(("osT", h), X1)
    for h in range(RH):
        t.add(("gn", h), L[h])
    t.add("kvmod", M)
    for i in range(8):
        t.add(("row2", i), X2)
    for n in range(4):
        for m in range(2):
            t.add(("rout", n, m), L[(2 * n + m) % 4])

    def moe(l):
        t.add(("rms", 1 + 2 * l), X0)
        t.add(("logits", l), X1)
        t.add(("logitsT", l), X1)
        t.add(("gatesT", l), X2)
        jobs = []
        for pr in range(2):
            for e in range(2):
                jobs += [(("G", l, pr, e, m), L[m]) for m in range(2)]
                jobs += [(("U", l, pr, e, m), L[2 + m]) for m in range(2)]
            jobs += [(("D", l, pr, k), (X0, X1, X2, M)[k % 4]) for k in range(KT)]
        t.loop(8, jobs)

    moe(0)
    t.add(("rms", 2), X0)
    t.add("flogit", X1)
    t.add("logfT", X2)
    t.add("F", X0)
    for i in range(4):
        for m in range(2):
            t.add(("fk", i, m), L[(2 * i + m) % 4])
    for i in range(4):
        for c in range(2):
            t.add(("fv", i, c), L[(2 * i + c) % 4])
        t.add(("fvs", i), (X0, X1)[i % 2])
    for i in range(4):
        for m in range(2):
            t.add(("fq", i, m), L[(2 * i + m) % 4])
    t.add("own_score", X1)
    t.add("own_F", X2)
    t.add("fvsT", X0)
    t.add(("qrow", 0), X1)
    t.add(("qrow", 1), X2)
    t.add(("qb", 0, "pre"), X0)
    t.add(("qb", 1, "pre"), X1)

    def window(tag):
        values = [(("pv", 0, tag), X2), (("pv", 1, tag), M)]
        heads = [(("ps", 0, tag), L[0]), (("ps", 1, tag), L[1]), (("pT", 0, tag), L[2]), (("pT", 1, tag), L[3]),
                 (("po", 0, tag), L[0]), (("po", 1, tag), L[1])]
        scores = [(("mxT", tag), X0), (("mxb", tag), X1), (("qb", 0, tag), X0), (("qb", 1, tag), X1),
                  (("den", tag), X0)]
        turned = [(("oT", tag), X1)]
        return {"first": heads + scores, "mid": values + heads + scores + turned, "last": values + turned}[tag]

    for key, bank in window("first"):
        t.add(key, bank)
    t.loop(NS - 1, window("mid"))
    for key, bank in window("last"):
        t.add(key, bank)
    for n in range(4):
        for m in range(2):
            t.add(("fout", n, m), L[(2 * n + m) % 4])
    moe(1)
    t.add(("rms", 4), X0)
    return t.at


class Steps:

    def __init__(self, eng, sem):
        self.eng, self.sem, self.n, self.offset = eng, sem, 0, None

    def step(self, ins):
        ins.then_inc(self.sem, 1)
        self.n += 1

    def wait(self):
        self.eng.wait_ge(self.sem, self.n if self.offset is None else self.offset + self.n)

    def enter(self, it, per):
        self.offset, self.per, self.start = it * per, per, self.n

    def leave(self, steps):
        assert self.n - self.start == self.per, (self.n - self.start, self.per)
        self.n += self.per * (steps - 1)
        self.offset = None


def build(nc, consts, x_in, c_in, vecs, wsmall, wstream, kcache, vcache, lfcache, ptable, state,
          y_out, sp_out, ss_out, k_out, vp_out, vs_out, lf_out):
    at = plan_turns()
    ctx = ExitStack()
    with ctx:
        def sb(name, shape, dt=F32):
            return ctx.enter_context(nc.sbuf_tensor(name, shape, dt))

        def sem(name):
            return ctx.enter_context(nc.semaphore(name))

        gates_dram = nc.dram_tensor("gates_scratch", (2, NE, T), F32, kind="Internal").ap()

        cst = sb("cst", [P, N_CONST])
        vec = sb("vec", [P, N_VEC])
        wsm = sb("wsm", [P, KT * FH + 2 * KT * 36])
        page_ids = sb("page_ids", [1, NPAGES], I32)
        x = sb("x", [P, KT, T])
        xn = sb("xn", [P, KT, T])
        h = sb("h", [P, KT, T])
        cs = sb("cs", [P, KT, NC])
        ring = sb("ring", [P, R, SW])
        mod = [sb(f"mod{l}", [P, 48, NC]) for l in range(2)]
        kvmod = sb("kvmod", [P, 16, NC])
        coef = sb("coef", [P, KT, NC])
        coef2 = sb("coef2", [P, KT, NC])
        root = sb("root", [P, T])
        rstd = sb("rstd", [P, T])
        ms = sb("ms", [P, KT, NS])
        past_F = sb("past_F", [P, NS, NPG * FH])
        past_tot = sb("past_tot", [P, NS * FH])

        arena_cols = 27400
        arena = sb("arena", [P, arena_cols])

        class Region:
            def __init__(self, start):
                self.at = start

            def take(self, *shape, rows=P):
                n = int(np.prod(shape))
                a = arena[0:rows, self.at:self.at + n]
                self.at += n
                assert self.at <= arena_cols, self.at
                if len(shape) == 2:
                    a = a.rearrange("p (a b) -> p a b", a=shape[0])
                if len(shape) == 3:
                    a = a.rearrange("p (a b c) -> p a b c", a=shape[0], b=shape[1])
                return a

        ret = Region(0)
        qk = ret.take(2 * KT, T)
        vtok = ret.take(2, RH * RV)
        vrow = xn[0:NS].rearrange("p a b -> p (a b)")[:, 0:RH * RV]
        mrow = ret.take(2, 256)
        qz = ret.take(2, RH, NS * NS)
        osb = ret.take(RV)
        gsil = ret.take(RVT, T)
        oret = ret.take(RVT, T)
        st = ret.take(4, 2, RV)
        at_sb = ret.take(2, 3 * P)
        ktok = ret.take(2, 2, RK)
        sp_sb = ret.take(2, RV)
        rot = ret.take(4, T)
        past_lf = gsil.rearrange("p a b -> p (a b)")[:, 0:NS * NPG * FH] \
            .rearrange("p (b g h) -> p b g h", b=NS, g=NPG)
        past_pre = gsil.rearrange("p a b -> p (a b)")[:, NS * NPG * FH:2 * NS * NPG * FH] \
            .rearrange("p (b g h) -> p b g h", b=NS, g=NPG)
        past_sum = gsil.rearrange("p a b -> p (a b)")[:, 2 * NS * NPG * FH:2 * NS * NPG * FH + NS * FH] \
            .rearrange("p (b h) -> p b h", b=NS)

        me = Region(0)
        act_g = me.take(2, T)
        glu = me.take(2, T)
        aff = me.take(4, T)
        gb = me.take(2, 2, T)
        lg = me.take(3, 36)
        lgT = me.take(T, rows=36)
        r4 = me.take(8, 3, NG)
        r8 = me.take(8, 3, EG)
        r1 = me.take(8, 3)
        le4 = me.take(3, EG, NG)
        gates = me.take(3, NE)
        gatesT = me.take(T, rows=NE)
        fx = Region(0)
        n2 = fx.take(KT, T)
        fq = fx.take(KT, T)
        fk = fx.take(KT, T)
        fo = n2
        fv = fx.take(2, D)
        fvs = fx.take(KT, NS)
        own = fx.take(KT, NS)
        s_own = fx.take(NS, FH)
        fz = fx.take(4, T, rows=FH)
        lf_tok = fx.take(2, FH)
        Fsb = fx.take(TP, rows=FH)
        q_row = fx.take(D, rows=NS)
        q_one = fx.take(D, rows=NS)
        lf_diag = fx.take(NS, FH, rows=FH)
        negF = fx.take(2, TP, rows=FH)
        q_st = fx.take(TP)
        k_st = fx.take(TP)
        v_st = fx.take(2, P)
        s_sb = fx.take(2, 3 * P)
        p_sb = fx.take(2, 3 * P)
        pT_sb = fx.take(2, 3 * P)
        hmax = fx.take(2, 2)
        hneg = fx.take(2, 2)
        hsum = fx.take(2, 2)
        hinv = fx.take(2, 2)
        sF = fx.take(NPG * FH)
        mxp = fx.take(FH)
        mx1 = fx.take(1, rows=FH)
        mxd = fx.take(FH, rows=FH)
        mx = fx.take(FH)
        sM = fx.take(NPG * FH)
        sO = fx.take(FH)
        pD = fx.take(NPG * FH)
        pO = fx.take(FH)
        psm = fx.take(FH)
        den = fx.take(FH)
        dinv = fx.take(FH)
        dinv1 = fx.take(FH)
        pO1 = fx.take(FH)
        pE = fx.take(NPG * FH)
        sc = fx.take(NPG * FH)
        oO = fx.take(KT)
        oS = fx.take(KT)
        pages = Region(arena_cols - 8 * D)
        assert me.at <= pages.at and fx.at <= pages.at, (me.at, fx.at, pages.at)
        kpg = pages.take(4, D)
        vpg = pages.take(4, D)
        flat = lambda a: a[:, :, :].rearrange("p a b -> p (a b)")
        qb = flat(xn)[:, 0:D]
        o_row = flat(xn)[0:FH, D:2 * D]
        prod = flat(h)[:, 0:2 * D].rearrange("p (r n) -> p r n", r=2)

        bank = [ctx.enter_context(nc.psum_tensor(f"bank{i}", [P, 512], F32)) for i in range(8)]
        filled = [sem(f"filled{i}") for i in range(8)]
        drained = [sem(f"drained{i}") for i in range(8)]

        consts_in = sem("consts_in")
        x_loaded = sem("x_loaded")
        lf_in = sem("lf_in")
        ids_in = sem("ids_in")
        slot_in = [sem(f"slot_in{r}") for r in range(R)]
        slot_used = sem("slot_used")
        state_in = [sem(f"state_in{r}") for r in range(4)]
        state_out = [sem(f"state_out{r}") for r in range(4)]
        state_scaled = sem("state_scaled")
        state_read = sem("state_read")
        k_in = [sem(f"k_in{r}") for r in range(4)]
        v_in = [sem(f"v_in{r}") for r in range(4)]
        k_used = sem("k_used")
        v_used = sem("v_used")
        gates_out = sem("gates_out")
        gates_in = [sem(f"gates_in{r}") for r in range(2)]
        past_ready = sem("past_ready")
        cond_ready = sem("cond_ready")
        squared = sem("squared")
        h_ready = sem("h_ready")
        x_ready = sem("x_ready")
        o_squared = sem("o_squared")
        o_rooted = sem("o_rooted")
        o_ready = sem("o_ready")
        dve_steps = sem("dve_steps")
        aff_ready = sem("aff_ready")
        route_e = sem("route_e")
        route_x = sem("route_x")
        gates_ready = sem("gates_ready")
        f_exp = sem("f_exp")
        f_neg = sem("f_neg")
        logf_ready = sem("logf_ready")
        one_ready = sem("one_ready")
        pE_ready = sem("pE_ready")
        lf_stored = sem("lf_stored")
        vs_stored = sem("vs_stored")
        qz_ready = sem("qz_ready")
        own_ready = sem("own_ready")
        diag_ready = sem("diag_ready")
        staged = sem("staged")
        negF_ready = sem("negF_ready")
        neg_max = sem("neg_max")
        p_raw = sem("p_raw")
        p_ready = sem("p_ready")
        mxp_ready = sem("mxp_ready")
        mxd_ready = sem("mxd_ready")
        shifted = sem("shifted")
        pd_ready = sem("pd_ready")
        psm_ready = sem("psm_ready")
        sample_done = sem("sample_done")
        sp_stored = sem("sp_stored")
        stored = sem("stored")

        def c_(name, rows=P):
            a, n = CONST[name]
            return cst[0:rows, a:a + n]

        ident, ones = c_("ident"), c_("ones")
        gain = [vec[:, V_GAIN + 8 * g:V_GAIN + 8 * g + 8] for g in range(6)]
        w_f = wsm[:, 0:KT * FH].rearrange("p (k n) -> p k n", k=KT)
        w_r = [wsm[:, KT * FH + l * KT * 36:KT * FH + (l + 1) * KT * 36].rearrange("p (k n) -> p k n", k=KT)
               for l in range(2)]

        def slot(n, rows=KT):
            return ring[:, n % R, :].rearrange("p (k c) -> p k c", k=rows)

        def turn(key, it=None):
            b, first, per = at[key]
            return b, first if it is None or per == 0 else it * per + first

        def result(eng, key, it=None):
            b, n = turn(key, it)
            eng.wait_ge(filled[b], n + 1)
            return bank[b]

        def free(key):
            return drained[at[key][0]]

        def moved(eng, key, it=None):
            b, n = turn(key, it)
            eng.wait_ge(drained[b], n + 1)

        def bc(ap, shape):
            return ap.to_broadcast(shape)

        block = ctx.enter_context(nc.Block())

        @block.sync
        def _(sp):
            sp.dma_start(cst[:], consts).then_inc(consts_in, 16)
            sp.dma_start(vec[:], vecs).then_inc(consts_in, 16)
            sp.dma_start(wsm[:], wsmall).then_inc(consts_in, 16)
            sp.dma_start(cs[:], c_in).then_inc(consts_in, 16)
            sp.dma_start(x[:], x_in).then_inc(x_loaded, 16)
            for r in range(R):
                sp.dma_start(ring[:, r, :], wstream[r]).then_inc(slot_in[r], 16)
            with sp.Fori(1, SLOTS // R) as lap:
                for r in range(R):
                    sp.wait_ge(slot_used, lap * R + (r - R + 1))
                    sp.dma_start(ring[:, r, :], wstream[ds(lap * R + r, 1)].rearrange("a p n -> p (a n)")) \
                        .then_inc(slot_in[r], 16)
            for n in range(SLOTS // R * R, SLOTS):
                sp.wait_ge(slot_used, n - R + 1)
                sp.dma_start(ring[:, n % R, :], wstream[n]).then_inc(slot_in[n % R], 16)

        @block.gpsimd
        def _(pool):
            pool.dma_start(page_ids[:], ptable).then_inc(ids_in, 16)
            pool.wait_ge(ids_in, 16)
            with pool.Fori(0, NPAGES) as j:
                page = pool.value_load(page_ids[0:1, ds(j, 1)], min_val=0, max_val=kcache.shape[0] - 1)
                pool.dma_start(past_lf.rearrange("p b g h -> p (b g) h")[:, ds(j, 1), :].rearrange("p a h -> p (a h)"),
                               lfcache[ds(page, 1)].rearrange("a p h -> p (a h)")).then_inc(lf_in, 16)
            def state_of(u):
                return u % NS * RH + u // NS

            for u in range(4):
                pool.dma_start(st[:, u, :, :], state[state_of(u)]).then_inc(state_in[u], 16)
            for u in range(NS * RH):
                moved(pool, ("vb", u))
                pool.dma_start(ss_out[state_of(u)], st[:, u % 4, :, :]).then_inc(state_out[u % 4], 16)
                nxt = u + 3
                if 4 <= nxt < NS * RH:
                    pool.wait_ge(state_out[nxt % 4], 16 * (nxt // 4))
                    old = nxt - 4
                    if old % NS == NS - 1:
                        result(pool, ("os", old // NS))
                    else:
                        pool.wait_ge(state_read, old // NS * (NS - 1) + old % NS + 1)
                    pool.dma_start(st[:, nxt % 4, :, :], state[state_of(nxt)]).then_inc(state_in[nxt % 4], 16)

            def page_of(j):
                return pool.value_load(page_ids[0:1, ds(j, 1)], min_val=0, max_val=kcache.shape[0] - 1)

            def load_page(ring_, cache, sems, r, page):
                pool.dma_start(ring_[:, r, :], cache[ds(page, 1)].rearrange("a p n -> p (a n)")).then_inc(sems[r], 16)

            for r in range(4):
                pool.wait_ge(state_out[r], 16 * NS * RH // 4)
            pool.wait_ge(x_ready, 1)
            pool.wait_ge(sp_stored, 16 * RH)
            for j in range(4):
                load_page(kpg, kcache, k_in, j, page_of(j))
            for j in range(4):
                load_page(vpg, vcache, v_in, j, page_of(j))

            def load_gates(l):
                pool.wait_ge(gates_out, 16 * (l + 1))
                for pr in range(2):
                    if l == 1:
                        pool.wait_ge(aff_ready, 4 * 16)
                    pool.dma_start(gb[:, pr, :, :], gates_dram[l, 2 * pr:2 * pr + 2, :].partition_broadcast(P)) \
                        .then_inc(gates_in[pr], 16)
                with pool.Fori(1, 8) as it:
                    for pr in range(2):
                        pool.wait_ge(aff_ready, it * 8 + (64 * l - 8 + 4 * (pr + 1)))
                        src = gates_dram[l, ds(it * 4 + 2 * pr, 2), :].partition_broadcast(P)
                        pool.dma_start(gb[:, pr, :, :], src).then_inc(gates_in[pr], 16)

            load_gates(0)
            for j in range(4, NPG):
                page = page_of(j)
                pool.wait_ge(k_used, j - 3)
                load_page(kpg, kcache, k_in, j % 4, page)
            def values_of(b, j, tag=None, it=None):
                page = page_of(b * NPG + j)
                if j >= 4:
                    pool.wait_ge(v_used, b * (NPG - 1) + (j - 3))
                elif j < 3:
                    pool.wait_ge(v_used, b * (NPG - 1) + (j + 5 - (NPG - 1)))
                else:
                    result(pool, ("pv", 1, tag), it)
                load_page(vpg, vcache, v_in, j % 4, page)

            with pool.Fori(0, NS - 1) as it:
                b = it + 1
                for j in range(NPG):
                    page = page_of(b * NPG + j)
                    pool.wait_ge(k_used, b * NPG + (j - 3))
                    load_page(kpg, kcache, k_in, j % 4, page)
                    if j < 4:
                        values_of(it, 4 + j)
                    else:
                        values_of(b, j - 4, "mid", it)
            for j in range(4, NPG):
                values_of(NS - 1, j)
            load_gates(1)
            for r in range(4):
                pool.wait_ge(state_out[r], 16 * NS * RH // 4)

        @block.tensor
        def _(pe):
            first_of_slot = [False]

            def mm(out, w, rhs, start, stop, done=None):
                ins = nc.tensor.matmul(out, w, rhs, start=start, stop=stop, skip_group_check=True)
                if first_of_slot[0]:
                    ins.then_inc(slot_used, 1)
                    first_of_slot[0] = False
                elif done is not None:
                    ins.then_inc(done, 1)

            def turned(out, rows, n, waits, done=None):
                if waits:
                    ins = nc.tensor.matmul(out, rows, ident[0:n, 0:n], start=True, stop=True)
                else:
                    ins = nc.tensor.transpose(out, rows, ident[0:n, 0:n])
                if done is not None:
                    ins.then_inc(done, 1)

            def take_slot(n, it=None, laps=1):
                if it is None:
                    pe.wait_ge(slot_in[n % R], 16 * (n // R + 1))
                else:
                    pe.wait_ge(slot_in[n % R], it * (16 * laps) + 16 * (n // R + 1))
                first_of_slot[0] = n > 0

            def begin(key, it=None):
                b, n = turn(key, it)
                if it is not None or n > 0:
                    pe.wait_ge(drained[b], n)
                return bank[b], filled[b]

            def rms(r):
                ps, full = begin(("rms", r))
                pe.wait_ge(squared, r + 1)
                for k in range(KT):
                    mm(ps[:, 0:T], ones, xn[:, k, :], k == 0, k == KT - 1, full if k == KT - 1 else None)

            def columns(key, n, m, src, it=None, k0=0, kn=KT):
                w = slot(n)
                ps, full = begin(key, it)
                for k in range(KT):
                    mm(ps[:, 0:T], w[:, k, m * P:(m + 1) * P], src[:, k, :], k == 0, k == KT - 1,
                       full if k == KT - 1 else None)

            def mod_rows(key, n, it=None, blocks=range(KT)):
                w = slot(n)
                b, _ = turn(key, it)
                ps, full = begin(key, it) if blocks[0] == 0 else (bank[b], filled[b])
                for k in blocks:
                    mm(ps[0:NC, 0:256], cs[:, k, :], w[:, k, :], k == 0, k == KT - 1,
                       full if k == KT - 1 else None)

            def mod_turn(key, buf, ps, tile, done=None, it=None):
                moved(pe, key, it)
                for m in range(2):
                    turned(ps[:, (tile + m) * NC:(tile + m + 1) * NC], mrow[0:NC, buf, m * P:(m + 1) * P], NC,
                           m == 0, done if m else None)

            pe.wait_ge(consts_in, 64)
            pe.wait_ge(cond_ready, 1)

            def mod0_lap(it):
                for r in range(R):
                    pe.wait_ge(slot_in[r], it * 16 + 16)
                    first_of_slot[0] = not (isinstance(it, int) and r == 0)
                    mod_rows(("row0", r), r, it)
                    if r == 0:
                        ps, full = begin("mod0", it)
                    else:
                        mod_turn(("row0", r - 1), (r - 1) % 2, ps, 2 * (r - 1), None, it)
                mod_turn(("row0", R - 1), (R - 1) % 2, ps, 2 * (R - 1), full, it)

            mod0_lap(0)
            with pe.Fori(1, 24 // R) as it:
                mod0_lap(it)

            rms(0)
            pe.wait_ge(h_ready, 1)
            mod1_ps, mod1_full = begin("mod1")

            def mod1_slot(i):
                take_slot(S_RET + 2 * i + 1)
                mod_rows(("row1", i), S_RET + 2 * i + 1)
                if i:
                    mod1_turn(i - 1)

            def mod1_turn(i):
                mod_turn(("row1", i), i % 2, mod1_ps, 2 * i, mod1_full if i == 23 else None)

            def values(key, skey, n, src, i):
                w = slot(n)
                for c in range(2):
                    ps, full = begin((key, i, c))
                    for k in range(KT):
                        mm(ps[:, 0:256], src[:, k, c * P:(c + 1) * P], w[:, k, :], k == 0, k == KT - 1,
                           full if k == KT - 1 else None)
                ps, full = begin((skey, i))
                for k in range(KT):
                    mm(ps[0:NS, 0:256], src[:, k, TP:T], w[:, k, :], k == 0, k == KT - 1,
                       full if k == KT - 1 else None)

            for i in range(8):
                take_slot(S_RET + 2 * i)
                for m in range(2):
                    columns(("qk", i, m), S_RET + 2 * i, m, h)
                mod1_slot(i)
            for i in range(8):
                take_slot(S_RET + 2 * (8 + i))
                values("v", "vs", S_RET + 2 * (8 + i), h, i)
                mod1_slot(8 + i)

            pe.wait_ge(past_ready, 1)
            lfv = past_lf.rearrange("p b g h -> p (b g h)")
            prev = past_pre.rearrange("p b g h -> p (b g h)")
            for i in range(2):
                ps, full = begin(("past", i))
                mm(ps[:], c_("upto")[:, 0:P], lfv[:, i * 512:(i + 1) * 512], True, False)
                mm(ps[:], ones, prev[:, i * 512:(i + 1) * 512], False, True, full)
            ps, full = begin("past_total")
            mm(ps[:, 0:NS * FH], ones, past_sum.rearrange("p b h -> p (b h)"), True, True, full)

            def head_scores(hd):
                for s in range(2):
                    moved(pe, ("qk", hd, s))
                    moved(pe, ("qk", 4 + hd, s))
                ps, full = begin(("ra", hd))
                for s in range(2):
                    mm(ps[:, 0:TP], qk[:, 8 + 2 * hd + s, 0:P], qk[:, 2 * hd + s, 0:TP], s == 0, s == 1)
                for s in range(2):
                    mm(ps[:, TP:TP + P], qk[:, 8 + 2 * hd + s, P:TP], qk[:, 2 * hd + s, P:TP], s == 0, s == 1,
                       full if s == 1 else None)
                ps, full = begin(("rk", hd))
                for c in range(2):
                    for s in range(2):
                        ins = nc.tensor.transpose(ps[:, (2 * c + s) * P:(2 * c + s + 1) * P],
                                                  qk[:, 8 + 2 * hd + s, c * P:(c + 1) * P], ident)
                ins.then_inc(full, 1)

            def head_output(hd):
                moved(pe, ("ra", hd))
                for c in range(2):
                    for i in (2 * hd, 2 * hd + 1):
                        moved(pe, ("v", i, c))
                sc = at_sb[:, hd % 2, :]
                for v in range(4):
                    ps, full = begin(("ro", hd, v))
                    col = slice(hd * RV + v * P, hd * RV + (v + 1) * P)
                    mm(ps[:, 0:TP], vtok[:, 0, col], sc[:, 0:TP], True, False)
                    mm(ps[:, P:TP], vtok[:, 1, col], sc[:, TP:TP + P], False, True, full)
                moved(pe, ("rk", hd))
                for s in range(2):
                    ps, full = begin(("rs", hd, s))
                    for c in range(2):
                        mm(ps[:], ktok[:, hd % 2, c, s * P:(s + 1) * P], vtok[:, c, hd * RV:(hd + 1) * RV], c == 0, c == 1,
                           full if c == 1 else None)

            head_scores(0)
            for hd in range(RH):
                if hd + 1 < RH:
                    head_scores(hd + 1)
                head_output(hd)

            def value_rows(u):
                hd, b = u // NS, u % NS
                ps, full = begin(("vb", u))
                mm(ps[:], bc(ident[0:NS, b:b + 1], [NS, P]), vrow[:, hd * RV:(hd + 1) * RV], True, True, full)

            for i in range(8):
                moved(pe, ("vs", i))
            pe.wait_ge(qz_ready, 1)

            def read_state(u):
                hd, b = u // NS, u % NS
                if b == 0:
                    begin(("os", hd))
                ps, full = bank[X1], filled[X1]
                moved(pe, ("vb", u))
                for s in range(2):
                    mm(ps[0:NS, :], qz[:, s, hd, b * NS:(b + 1) * NS], st[:, u % 4, s, :], b == 0 and s == 0,
                       b == NS - 1 and s == 1, None if s == 0 else full if b == NS - 1 else state_read)

            def outputs_turn(hd):
                moved(pe, ("os", hd))
                ps, full = begin(("osT", hd))
                for t in range(4):
                    ins = nc.tensor.transpose(ps[:, t * NS:(t + 1) * NS], osb[0:NS, t * P:(t + 1) * P],
                                              ident[0:NS, 0:NS])
                ins.then_inc(full, 1)

            for i in range(8):
                n = S_RET + 2 * (16 + i)
                value_rows(4 * i)
                take_slot(n)
                columns(("g", i, 0), n, 0, h)
                if i and i % 2 == 0:
                    outputs_turn(i // 2 - 1)
                read_state(4 * i)
                value_rows(4 * i + 1)
                columns(("g", i, 1), n, 1, h)
                read_state(4 * i + 1)
                value_rows(4 * i + 2)
                take_slot(n + 1)
                mod_rows(("row1", 16 + i), n + 1, None, range(0, 4))
                read_state(4 * i + 2)
                value_rows(4 * i + 3)
                mod_rows(("row1", 16 + i), n + 1, None, range(4, 8))
                mod1_turn(15 + i)
                read_state(4 * i + 3)
            mod1_turn(23)
            outputs_turn(RH - 1)

            for hd in range(RH):
                pe.wait_ge(o_squared, hd + 1)
                ps, full = begin(("gn", hd))
                for t in range(4):
                    mm(ps[:, 0:T], ones, qk[:, 4 * hd + t, :], t == 0, t == 3, full if t == 3 else None)

            pe.wait_ge(o_ready, RH)
            kv_ps, kv_full = begin("kvmod")
            for n in range(4):
                outs = []
                for half in range(2):
                    j = S_RO + 2 * (2 * n + half)
                    take_slot(j)
                    w = slot(j)
                    for m in range(2):
                        if half == 0:
                            outs.append(begin(("rout", n, m)))
                        ps, full = outs[m]
                        for k in range(KT):
                            mm(ps[:, 0:T], w[:, k, m * P:(m + 1) * P], oret[:, half * KT + k, :],
                               half == 0 and k == 0, half == 1 and k == KT - 1,
                               full if half == 1 and k == KT - 1 else None)
                    take_slot(j + 1)
                    i = 2 * n + half
                    mod_rows(("row2", i), j + 1)
                    if i:
                        mod_turn(("row2", i - 1), (i - 1) % 2, kv_ps, 2 * (i - 1))
            mod_turn(("row2", 7), 1, kv_ps, 14, kv_full)

            def moe(l, base):
                rms(1 + 2 * l)
                pe.wait_ge(h_ready, 2 + 3 * l)
                ps, full = begin(("logits", l))
                for k in range(KT):
                    mm(ps[0:36, 0:T], w_r[l][:, k, :], h[:, k, :], k == 0, k == KT - 1,
                       full if k == KT - 1 else None)
                moved(pe, ("logits", l))
                ps, full = begin(("logitsT", l))
                for c in range(3):
                    n = min(P, T - c * P)
                    ins = nc.tensor.transpose(ps[0:n, c * 36:(c + 1) * 36], lgT[:, c * P:c * P + n],
                                              ident[0:36, 0:36])
                ins.then_inc(full, 1)
                pe.wait_ge(gates_ready, l + 1)
                ps, full = begin(("gatesT", l))
                for c in range(3):
                    n = min(P, T - c * P)
                    ins = nc.tensor.transpose(ps[0:NE, c * P:c * P + n], gates[0:n, c, :], ident[0:n, 0:n])
                ins.then_inc(full, 1)

                def pair(pr, it):
                    n0 = base + 6 * pr
                    for e in range(2):
                        for what, j in (("G", 0), ("U", 1)):
                            take_slot(n0 + 2 * e + j, it, 2)
                            for m in range(2):
                                columns((what, l, pr, e, m), n0 + 2 * e + j, m, h, it)
                    down = [slot(n0 + 4 + e, 2) for e in range(2)]
                    order = [(k, q) for k in range(4) for q in range(2)] + [(k, 2) for k in range(4)] + \
                            [(k, 3) for k in range(4)] + [(k, q) for k in range(4, KT) for q in range(4)]
                    take_slot(n0 + 4, it, 2)
                    outs, seen = {}, -1
                    for k, q in order:
                        if q > seen:
                            pe.wait_ge(aff_ready, it * 8 + (64 * l + 4 * pr + q + 1))
                            if q == 2:
                                n1 = n0 + 5
                                pe.wait_ge(slot_in[n1 % R], it * 32 + 16 * (n1 // R + 1))
                            seen = q
                        if k not in outs:
                            outs[k] = begin(("D", l, pr, k), it)
                        ps, full = outs[k]
                        mm(ps[:, 0:T], down[q // 2][:, q % 2, k * P:(k + 1) * P], aff[:, q, :], q == 0, q == 3,
                           full if q == 3 else slot_used if (k, q) == (KT - 1, 2) else None)

                with pe.Fori(0, NE // 4) as it:
                    for pr in range(2):
                        pair(pr, it)

            moe(0, S_MOE0)

            rms(2)
            pe.wait_ge(h_ready, 3)
            ps, full = begin("flogit")
            for k in range(KT):
                mm(ps[0:FH, 0:T], w_f[:, k, :], n2[:, k, :], k == 0, k == KT - 1, full if k == KT - 1 else None)
            for i in range(4):
                take_slot(S_KV + i)
                for m in range(2):
                    columns(("fk", i, m), S_KV + i, m, n2)
            pe.wait_ge(logf_ready, 1)
            ps, full = begin("logfT")
            for c in range(2):
                ins = nc.tensor.transpose(ps[:, c * FH:(c + 1) * FH], fz[:, 1, c * P:(c + 1) * P], ident[0:FH, 0:FH])
            ins.then_inc(full, 1)
            for i in range(4):
                take_slot(S_KV + 4 + i)
                if i == 0:
                    moved(pe, "logfT")
                    ps, full = begin("F")
                    nc.tensor.matmul(ps[0:FH, 0:TP], lf_tok[:, 0, :], c_("upto"), start=True, stop=False,
                                     skip_group_check=True)
                    nc.tensor.matmul(ps[0:FH, P:TP], lf_tok[:, 1, :], c_("upto")[:, 0:P], start=False, stop=True,
                                     skip_group_check=True).then_inc(full, 1)
                values("fv", "fvs", S_KV + 4 + i, n2, i)
            pe.wait_ge(h_ready, 4)
            for i in range(4):
                take_slot(S_FQ + i)
                for m in range(2):
                    columns(("fq", i, m), S_FQ + i, m, h)
            pe.wait_ge(diag_ready, 1)
            ps, full = begin("own_F")
            mm(ps[:, 0:NS * FH], ones[0:FH, :], lf_diag.rearrange("p b h -> p (b h)"), True, True, full)
            pe.wait_ge(own_ready, 1)
            ps, full = begin("own_score")
            for r, name in enumerate(("half0", "half1")):
                mm(ps[:, r * 64:(r + 1) * 64], c_(name), own.rearrange("p t b -> p (t b)"), True, True,
                   full if r else None)
            for i in range(4):
                moved(pe, ("fvs", i))
            ps, full = begin("fvsT")
            for t in range(KT):
                ins = nc.tensor.transpose(ps[:, t * NS:(t + 1) * NS], q_one[:, t * P:(t + 1) * P],
                                          ident[0:NS, 0:NS])
            ins.then_inc(full, 1)
            for i in range(2):
                ps, full = begin(("qrow", i))
                for t in range(4):
                    ins = nc.tensor.transpose(ps[0:NS, t * P:(t + 1) * P], fq[:, 4 * i + t, TP:T], ident)
                ins.then_inc(full, 1)

            def query_everywhere(tag, b, it=None):
                pe.wait_ge(one_ready, b + 1)
                for i in range(2):
                    ps, full = begin(("qb", i, tag), it)
                    mm(ps[:], ones[0:NS, :], q_one[:, i * 512:(i + 1) * 512], True, True, full)

            query_everywhere("pre", 0)

            def window(tag, b, it=None):
                def value_page(j):
                    if tag == "first":
                        return
                    if j == 0:
                        pe.wait_ge(pd_ready, b)
                        begin(("pv", 0, tag), it)
                        begin(("pv", 1, tag), it)
                    pe.wait_ge(v_in[j % 4], b * 32 + (16 * (j // 4 + 1) - 32))
                    for i in range(2):
                        bk = at[("pv", i, tag)][0]
                        mm(bank[bk][0:FH, :], pD[:, j * FH:(j + 1) * FH], vpg[:, j % 4, i * 512:(i + 1) * 512],
                           j == 0, j == NPG - 1, filled[bk] if j == NPG - 1 else v_used if i else None)

                def head_scores(hh):
                    if tag == "last":
                        return
                    pe.wait_ge(staged, b * 3 + 3)
                    pe.wait_ge(negF_ready, b + 1)
                    rows = slice(64 * hh, 64 * hh + 64)
                    ps, full = begin(("ps", hh, tag), it)
                    for c in range(2):
                        cols = slice(0, P) if c == 0 else slice(P, 3 * P)
                        keys = slice(0, (c + 1) * P)
                        mm(ps[:, cols], q_st[rows, c * P:(c + 1) * P], k_st[rows, keys], True, False)
                        mm(ps[:, cols], ones[0:FH, :], negF[:, hh, keys], False, True, full if c else None)

                def head_turn(hh):
                    if tag == "last":
                        return
                    ps, full = begin(("pT", hh, tag), it)
                    pe.wait_ge(p_ready, b * 2 + (hh + 1))
                    for i in range(3):
                        ins = nc.tensor.transpose(ps[:, i * P:(i + 1) * P], p_sb[:, hh, i * P:(i + 1) * P], ident)
                    ins.then_inc(full, 1)

                def head_values(hh):
                    if tag == "last":
                        return
                    moved(pe, ("pT", hh, tag), it)
                    ps, full = begin(("po", hh, tag), it)
                    rows = slice(64 * hh, 64 * hh + 64)
                    mm(ps[rows, 0:TP], v_st[:, 0, rows], pT_sb[:, hh, 0:TP], True, False)
                    mm(ps[rows, P:TP], v_st[:, 1, rows], pT_sb[:, hh, TP:3 * P], False, True, full)

                value_page(0)
                head_scores(0)
                value_page(1)
                head_scores(1)
                value_page(2)
                value_page(3)
                head_turn(0)
                value_page(4)
                head_turn(1)
                head_values(0)
                value_page(5)
                head_values(1)
                value_page(6)
                value_page(7)
                if tag != "last":
                    ps, full = begin(("mxT", tag), it)
                    pe.wait_ge(mxp_ready, b + 1)
                    nc.tensor.transpose(ps[0:FH, 0:P], mxp, ident).then_inc(full, 1)
                    pe.wait_ge(mxd_ready, b + 1)
                    ps, full = begin(("mxb", tag), it)
                    mm(ps[:, 0:FH], ones[0:FH, :], mxd, True, True, full)
                    query_everywhere(tag, b + 1, it)
                    pe.wait_ge(psm_ready, b + 1)
                    ps, full = begin(("den", tag), it)
                    mm(ps[:, 0:FH], ones, psm, True, True, full)
                if tag != "first":
                    moved(pe, ("pv", 0, tag), it)
                    moved(pe, ("pv", 1, tag), it)
                    ps, full = begin(("oT", tag), it)
                    for t in range(KT):
                        turned(ps[:, t * FH:(t + 1) * FH], o_row[:, t * P:(t + 1) * P], FH, t == 0,
                               full if t == KT - 1 else None)

            window("first", 0)
            with pe.Fori(0, NS - 1) as it:
                window("mid", it + 1, it)
            window("last", NS)

            pe.wait_ge(sample_done, NS)
            for hh in range(2):
                moved(pe, ("po", hh, "mid"), NS - 2)
            for n in range(4):
                take_slot(S_FO + n)
                for m in range(2):
                    columns(("fout", n, m), S_FO + n, m, fo)
            moe(1, S_MOE1)
            rms(4)

        @block.scalar
        def _(act):
            def copy(out, in_, scale=None):
                if scale is None:
                    return nc.scalar.activation(out, in_, ACT.Copy)
                return nc.scalar.activation(out, in_, ACT.Copy, scale=scale)

            act.wait_ge(consts_in, 64)
            nc.scalar.activation(cs[:], cs[:], ACT.Silu).then_inc(cond_ready, 1)
            eps = c_("eps")

            def mod_rows(key, buf, it=None):
                ps = result(act, key, it)
                copy(mrow[0:NC, buf, :], ps[0:NC, 0:256]).then_inc(free(key), 1)

            with act.Fori(0, 24 // R) as it:
                for r in range(R):
                    mod_rows(("row0", r), r % 2, it)

            def rms(r):
                if r == 0:
                    act.wait_ge(x_loaded, 16)
                else:
                    act.wait_ge(x_ready, r)
                nc.scalar.activation(xn[:], x[:], ACT.Square).then_inc(squared, 1)
                ps = result(act, ("rms", r))
                nc.scalar.activation(root[:], ps[:, 0:T], ACT.Sqrt, bias=eps, scale=1.0 / D) \
                    .then_inc(free(("rms", r)), 1)

            rms(0)
            for i in range(8):
                mod_rows(("row1", i), i % 2)
            for i in range(8):
                for c in range(2):
                    ps = result(act, ("v", i, c))
                    copy(vtok[:, c, i * 256:(i + 1) * 256], ps[:, 0:256]).then_inc(free(("v", i, c)), 1)
                mod_rows(("row1", 8 + i), i % 2)
            for hd in range(RH):
                for v in range(4):
                    ps = result(act, ("ro", hd, v))
                    copy(oret[:, 4 * hd + v, 0:TP], ps[:, 0:TP]).then_inc(free(("ro", hd, v)), 1)
                if hd:
                    act.wait_ge(sp_stored, 16 * hd)
                for s in range(2):
                    ps = result(act, ("rs", hd, s))
                    copy(sp_sb[:, s, :], ps[:]).then_inc(free(("rs", hd, s)), 1)
                moved(act, ("rs", hd, 1))
                act.dma_start(sp_out[hd], sp_sb).then_inc(sp_stored, 16)

            def scale_state(u):
                act.wait_ge(state_in[u % 4], 16 * (u // 4 + 1))
                copy(st[:, u % 4, :, :], st[:, u % 4, :, :], GAMMA[u // NS]).then_inc(state_scaled, 1)

            for i in range(8):
                for m in range(2):
                    scale_state(4 * i + 2 * m)
                    scale_state(4 * i + 2 * m + 1)
                    ps = result(act, ("g", i, m))
                    nc.scalar.activation(gsil[:, 2 * i + m, :], ps[:, 0:T], ACT.Silu) \
                        .then_inc(free(("g", i, m)), 1)
                mod_rows(("row1", 16 + i), i % 2)
                if i % 2:
                    ps = result(act, ("os", i // 2))
                    copy(osb[0:NS, :], ps[0:NS, :]).then_inc(free(("os", i // 2)), 1)
            moved(act, ("osT", RH - 1))
            moved(act, ("ro", RH - 1, 3))
            for hd in range(RH):
                nc.scalar.activation(qk[:, 4 * hd:4 * hd + 4, :], oret[:, 4 * hd:4 * hd + 4, :], ACT.Square) \
                    .then_inc(o_squared, 1)
            for hd in range(RH):
                ps = result(act, ("gn", hd))
                nc.scalar.activation(rot[:, hd, :], ps[:, 0:T], ACT.Sqrt, bias=eps, scale=1.0 / RV) \
                    .then_inc(free(("gn", hd)), 1)

            for i in range(8):
                mod_rows(("row2", i), i % 2)

            def moe(l):
                rms(1 + 2 * l)
                ps = result(act, ("logits", l))
                copy(lgT, ps[0:36, 0:T]).then_inc(free(("logits", l)), 1)
                act.wait_ge(route_x, l + 1)
                nc.scalar.activation(r4[:, 4, :, :], r4[:, 0, :, :], ACT.Exp)
                nc.scalar.activation(r1[:, 7, :], r1[:, 6, :], ACT.Exp).then_inc(route_e, 1)
                moved(act, ("gatesT", l))
                act.dma_start(gates_dram[l], gatesT).then_inc(gates_out, 16)
                with act.Fori(0, NE // 4) as it:
                    for pr in range(2):
                        for e in range(2):
                            for m in range(2):
                                ps = result(act, ("G", l, pr, e, m), it)
                                b, n = turn(("U", l, pr, e, m), it)
                                act.wait_ge(drained[b], n)
                                nc.scalar.activation(act_g[:, m, :], ps[:, 0:T], ACT.Silu) \
                                    .then_inc(free(("G", l, pr, e, m)), 1)

            moe(0)

            rms(2)
            act.wait_ge(f_neg, 1)
            nc.scalar.activation(fz[:, 2, :], fz[:, 1, :], ACT.Exp).then_inc(f_exp, 1)
            act.wait_ge(f_exp, 1)
            nc.scalar.activation(fz[:, 3, :], fz[:, 2, :], ACT.Ln, bias=1.0).then_inc(f_exp, 1)
            for i in range(4):
                for m in range(2):
                    ps = result(act, ("fk", i, m))
                    copy(fk[:, 2 * i + m, :], ps[:, 0:T]).then_inc(free(("fk", i, m)), 1)
            act.wait_ge(logf_ready, 1)
            act.dma_start(lf_out, fz[:, 1, :]).then_inc(lf_stored, 16)
            moved(act, ("fk", 3, 0))
            moved(act, ("fk", 3, 1))
            act.dma_start(k_out, fk).then_inc(stored, 16)
            for i in range(4):
                for c in range(2):
                    ps = result(act, ("fv", i, c))
                    copy(fv[:, c, i * 256:(i + 1) * 256], ps[:, 0:256]).then_inc(free(("fv", i, c)), 1)
            moved(act, ("fv", 3, 0))
            moved(act, ("fv", 3, 1))
            act.dma_start(vp_out, fv).then_inc(stored, 16)
            moved(act, ("fvs", 2))
            moved(act, ("fvs", 3))
            act.dma_start(vs_out, q_one).then_inc(vs_stored, 16)
            for i in range(4):
                for m in range(2):
                    ps = result(act, ("fq", i, m))
                    copy(fq[:, 2 * i + m, :], ps[:, 0:T], HD ** -0.5).then_inc(free(("fq", i, m)), 1)
            moved(act, ("fq", 3, 0))
            moved(act, ("fq", 3, 1))

            def query_everywhere(tag, it=None):
                for i in range(2):
                    ps = result(act, ("qb", i, tag), it)
                    copy(qb[:, i * 512:(i + 1) * 512], ps[:]).then_inc(free(("qb", i, tag)), 1)

            query_everywhere("pre")

            def window(tag, b, it=None):
                if tag != "last":
                    copy(q_st, fq[:, ds(b, 1), 0:TP].rearrange("p a n -> p (a n)")).then_inc(staged, 1)
                    copy(k_st, fk[:, ds(b, 1), 0:TP].rearrange("p a n -> p (a n)")).then_inc(staged, 1)
                    copy(v_st, fv[:, :, ds(b * P, P)]).then_inc(staged, 1)
                    for hh in range(2):
                        act.wait_ge(neg_max, b * 2 + (hh + 1))
                        nc.scalar.activation(p_sb[:, hh, 0:P], s_sb[:, hh, 0:P], ACT.Exp, bias=hneg[:, hh, 0:1],
                                             accum_out=hsum[:, hh, 0:1])
                        nc.scalar.activation(p_sb[:, hh, P:3 * P], s_sb[:, hh, P:3 * P], ACT.Exp,
                                             bias=hneg[:, hh, 1:2], accum_out=hsum[:, hh, 1:2]).then_inc(p_raw, 1)
                    for hh in range(2):
                        ps = result(act, ("pT", hh, tag), it)
                        copy(pT_sb[:, hh, :], ps[:, 0:3 * P]).then_inc(free(("pT", hh, tag)), 1)
                    for hh in range(2):
                        rows = slice(64 * hh, 64 * hh + 64)
                        ps = result(act, ("po", hh, tag), it)
                        copy(fo[rows, ds(b, 1), 0:TP].rearrange("p a n -> p (a n)"), ps[rows, 0:TP]) \
                            .then_inc(free(("po", hh, tag)), 1)
                if tag != "last":
                    act.wait_ge(shifted, b + 1)
                    nc.scalar.activation(pE, sF, ACT.Exp)
                    nc.scalar.activation(pO, sO, ACT.Exp).then_inc(pE_ready, 1)
                    query_everywhere(tag, it)
                if tag != "first":
                    for i in range(2):
                        ps = result(act, ("pv", i, tag), it)
                        copy(o_row[:, i * 512:(i + 1) * 512], ps[0:FH, :]).then_inc(free(("pv", i, tag)), 1)
                if tag != "last":
                    act.wait_ge(pE_ready, b + 1)
                    copy(pD, pE).then_inc(pd_ready, 1)

            window("first", 0)
            with act.Fori(0, NS - 1) as it:
                window("mid", it + 1, it)
            window("last", NS)

            moe(1)
            rms(4)
            act.wait_ge(h_ready, 6)
            act.dma_start(y_out, h[:]).then_inc(stored, 16)
            act.wait_ge(stored, 16 * 3)
            act.wait_ge(lf_stored, 16)

        @block.vector
        def _(dve):
            own_steps = Steps(dve, dve_steps)
            step, wait = own_steps.step, own_steps.wait
            tt, stt, tsc = nc.vector.tensor_tensor, nc.vector.scalar_tensor_tensor, nc.vector.tensor_scalar

            dve.wait_ge(consts_in, 64)
            def add_bias(key, out, tiles, v0):
                ps = result(dve, key)
                tt(out, ps[:, 0:tiles * NC].rearrange("p (t c) -> p t c", c=NC),
                   bc(vec[:, v0:v0 + tiles].unsqueeze(2), [P, tiles, NC]), ALU.add).then_inc(free(key), 1)

            with dve.Fori(0, 24 // R) as it:
                ps = result(dve, "mod0", it)
                tiles = 2 * R
                tt(mod[0][:, ds(it * tiles, tiles), :], ps[:, 0:tiles * NC].rearrange("p (t c) -> p t c", c=NC),
                   bc(vec[:, ds(it * tiles, tiles)].unsqueeze(2), [P, tiles, NC]), ALU.add) \
                    .then_inc(free("mod0"), 1)

            def normalise(r):
                moved(dve, ("rms", r))
                step(nc.vector.reciprocal(rstd[:], root[:]))
                wait()
                step(tt(xn[:], x[:], bc(rstd[:].unsqueeze(1), [P, KT, T]), ALU.mult))

            def modulate(out, cf, g, table, shift, scale):
                sh, sc = table[:, 8 * shift:8 * shift + 8, :], table[:, 8 * scale:8 * scale + 8, :]
                step(stt(cf[:], sc, 1.0, bc(gain[g].unsqueeze(2), [P, KT, NC]), ALU.add, ALU.mult))
                wait()
                step(tt(out[:, :, TP:T], xn[:, :, TP:T], cf[:, :, 1:NC], ALU.mult))
                for k in range(KT):
                    tsc(out[:, k, 0:TP], xn[:, k, 0:TP], cf[:, k, 0:1], sh[:, k, 0:1], ALU.mult, ALU.add)
                wait()
                tt(out[:, :, TP:T], out[:, :, TP:T], sh[:, :, 1:NC], ALU.add).then_inc(h_ready, 1)

            moved(dve, "mod0", 24 // R - 1)
            normalise(0)
            modulate(h, coef, G_MIX0, mod[0], SH1, SC1)

            for i in range(8):
                cos, sin = (c_("cosq"), c_("sinq")) if i < 4 else (c_("cosk"), c_("sink"))
                ps0 = result(dve, ("qk", i, 0))
                ps1 = result(dve, ("qk", i, 1))
                if i:
                    moved(dve, ("qk", i - 1, 0))
                    moved(dve, ("qk", i - 1, 1))
                step(tt(rot[:, 0, :], ps0[:, 0:T], cos, ALU.mult))
                step(tt(rot[:, 1, :], ps1[:, 0:T], sin, ALU.mult))
                step(tt(rot[:, 2, :], ps0[:, 0:T], sin, ALU.mult))
                step(tt(rot[:, 3, :], ps1[:, 0:T], cos, ALU.mult))
                wait()
                tt(qk[:, 2 * i, :], rot[:, 0, :], rot[:, 1, :], ALU.subtract).then_inc(free(("qk", i, 0)), 1)
                tt(qk[:, 2 * i + 1, :], rot[:, 2, :], rot[:, 3, :], ALU.add).then_inc(free(("qk", i, 1)), 1)
            for i in range(8):
                ps = result(dve, ("vs", i))
                nc.vector.tensor_copy(vrow[:, i * 256:(i + 1) * 256], ps[0:NS, 0:256]) \
                    .then_inc(free(("vs", i)), 1)
            step(nc.vector.memset(past_pre[:, :, 0, :], 0.0))
            dve.wait_ge(lf_in, 16 * NPAGES)
            for g in range(1, NPG):
                wait()
                step(tt(past_pre[:, :, g, :], past_pre[:, :, g - 1, :], past_lf[:, :, g - 1, :], ALU.add))
            wait()
            tt(past_sum, past_pre[:, :, NPG - 1, :], past_lf[:, :, NPG - 1, :], ALU.add).then_inc(past_ready, 1)
            flat_F = past_F[:, :, :].rearrange("p b c -> p (b c)")
            for i in range(2):
                ps = result(dve, ("past", i))
                nc.vector.tensor_copy(flat_F[:, i * 512:(i + 1) * 512], ps[:]).then_inc(free(("past", i)), 1)
            ps = result(dve, "past_total")
            nc.vector.tensor_copy(past_tot[:], ps[:, 0:NS * FH]).then_inc(free("past_total"), 1)
            step(nc.vector.memset(qz, 0.0))
            wait()
            for hd in range(RH):
                for s in range(2):
                    ins = nc.vector.tensor_copy(qz[:, s, hd, 0:NS * NS:NS + 1], qk[:, 2 * hd + s, TP:T])
            ins.then_inc(qz_ready, 1)
            for hd in range(RH):
                ps = result(dve, ("ra", hd))
                dec = c_("decay")[:, hd * TP:(hd + 1) * TP]
                tt(at_sb[:, hd % 2, 0:TP], ps[:, 0:TP], dec, ALU.mult)
                tt(at_sb[:, hd % 2, TP:TP + P], ps[:, TP:TP + P], dec[:, 0:P], ALU.mult) \
                    .then_inc(free(("ra", hd)), 1)
                ps = result(dve, ("rk", hd))
                for c in range(2):
                    kd = c_("kdec")[:, c * RH + hd:c * RH + hd + 1]
                    ins = tsc(ktok[:, hd % 2, c, :], ps[:, c * RK:(c + 1) * RK], kd, None, ALU.mult)
                ins.then_inc(free(("rk", hd)), 1)
            def samples_out(hd):
                ps = result(dve, ("osT", hd))
                nc.vector.tensor_copy(oret[:, 4 * hd:4 * hd + 4, TP:T],
                                      ps[:, 0:4 * NS].rearrange("p (t b) -> p t b", b=NS)) \
                    .then_inc(free(("osT", hd)), 1)

            for u in range(NS * RH):
                hd, b = u // NS, u % NS
                if hd and b == 1:
                    samples_out(hd - 1)
                ps = result(dve, ("vb", u))
                dve.wait_ge(state_scaled, u + 1)
                for s in range(2):
                    ins = stt(st[:, u % 4, s, :], ps[:], qk[:, 8 + 2 * hd + s, TP + b:TP + b + 1],
                              st[:, u % 4, s, :], ALU.mult, ALU.add)
                ins.then_inc(free(("vb", u)), 1)
            samples_out(RH - 1)
            add_bias("mod1", mod[1][:], 48, V_BMOD + 48)
            moved(dve, ("g", 7, 0))
            moved(dve, ("g", 7, 1))
            for hd in range(RH):
                tiles = slice(4 * hd, 4 * hd + 4)
                moved(dve, ("gn", hd))
                step(nc.vector.reciprocal(rot[:, hd, :], rot[:, hd, :]))
                wait()
                step(tt(oret[:, tiles, :], oret[:, tiles, :], bc(rot[:, hd:hd + 1, :], [P, 4, T]), ALU.mult))
                wait()
                tt(oret[:, tiles, :], oret[:, tiles, :], gsil[:, tiles, :], ALU.mult).then_inc(o_ready, 1)

            def residual(name, gate):
                for n in range(4):
                    for m in range(2):
                        t = 2 * n + m
                        ps = result(dve, (name, n, m))
                        stt(x[:, t, 0:TP], ps[:, 0:TP], gate[:, t, 0:1], x[:, t, 0:TP], ALU.mult, ALU.add)
                        tt(ms[:, t, :], ps[:, TP:T], gate[:, t, 1:NC], ALU.mult).then_inc(free((name, n, m)), 1)
                moved(dve, (name, 3, 0))
                moved(dve, (name, 3, 1))
                tt(x[:, :, TP:T], x[:, :, TP:T], ms[:], ALU.add).then_inc(x_ready, 1)

            residual("rout", mod[0][:, 8 * GT1:8 * GT1 + 8, :])
            add_bias("kvmod", kvmod[:], 16, V_BKV)

            def first_max(v, most, is_max, weight, first, best):
                n = v.shape[2]
                step(nc.vector.tensor_reduce(best[0], v, AX, ALU.max))
                wait()
                step(tt(is_max, v, bc(best[0].unsqueeze(2), [P, 3, n]), ALU.is_equal))
                wait()
                step(tt(weight, is_max, bc(first.unsqueeze(1), [P, 3, n]), ALU.mult))
                wait()
                step(nc.vector.tensor_reduce(best[1], weight, AX, ALU.max))
                wait()
                step(tt(most, weight, bc(best[1].unsqueeze(2), [P, 3, n]), ALU.is_equal))
                wait()

            def moe(l):
                normalise(1 + 2 * l)
                step(nc.vector.memset(lg, 0.0))
                modulate(h, coef, G_FFN0 + l, mod[l], SH2, SC2)
                dve.wait_ge(h_ready, 2 + 3 * l)
                step(nc.vector.memset(xn[:], 0.0))
                ps = result(dve, ("logitsT", l))
                nc.vector.tensor_copy(lg[:, 0:2, :], ps[:, 0:72].rearrange("p (c n) -> p c n", c=2))
                nc.vector.tensor_copy(lg[0:NS, 2, :], ps[0:NS, 72:108]).then_inc(free(("logitsT", l)), 1)
                moved(dve, ("logitsT", l))
                grp = lg[:, :, 0:NG]
                le = lg[:, :, NG:36]
                group = r4[:, 3, :, :]
                first_max(grp, group, r4[:, 1, :, :], r4[:, 2, :, :], c_("first4"), (r1[:, 0, :], r1[:, 1, :]))
                step(tt(r4[:, 0, :, :], grp, bc(r1[:, 0, :].unsqueeze(2), [P, 3, NG]), ALU.subtract))
                for c in range(3):
                    step(tt(le4[:, c, :, :], le[:, c, :].rearrange("p (g e) -> p e g", g=NG),
                            bc(group[:, c:c + 1, :], [P, EG, NG]), ALU.mult))
                wait()
                sel = r8[:, 0, :, :]
                step(nc.vector.tensor_reduce(sel, le4, AX, ALU.add))
                wait()
                one, two = r8[:, 3, :, :], r8[:, 7, :, :]
                first_max(sel, one, r8[:, 1, :, :], r8[:, 2, :, :], c_("first8"), (r1[:, 2, :], r1[:, 3, :]))
                step(stt(r8[:, 4, :, :], one, NEG, sel, ALU.mult, ALU.add))
                wait()
                first_max(r8[:, 4, :, :], two, r8[:, 5, :, :], r8[:, 6, :, :], c_("first8"),
                          (r1[:, 4, :], r1[:, 5, :]))
                tt(r1[:, 6, :], r1[:, 4, :], r1[:, 2, :], ALU.subtract).then_inc(route_x, 1)
                dve.wait_ge(route_e, l + 1)
                step(nc.vector.tensor_reduce(r1[:, 0, :], r4[:, 4, :, :], AX, ALU.add))
                wait()
                step(stt(r1[:, 1, :], r1[:, 7, :], 1.0, r1[:, 0, :], ALU.add, ALU.mult))
                wait()
                step(nc.vector.reciprocal(r1[:, 2, :], r1[:, 1, :]))
                wait()
                step(tt(r1[:, 3, :], r1[:, 2, :], r1[:, 7, :], ALU.mult))
                step(tt(r8[:, 1, :, :], one, bc(r1[:, 2, :].unsqueeze(2), [P, 3, EG]), ALU.mult))
                wait()
                step(tt(r8[:, 2, :, :], two, bc(r1[:, 3, :].unsqueeze(2), [P, 3, EG]), ALU.mult))
                wait()
                step(tt(r8[:, 4, :, :], r8[:, 1, :, :], r8[:, 2, :, :], ALU.add))
                wait()
                for c in range(3):
                    ins = tt(gates[:, c, :].rearrange("p (g e) -> p g e", g=NG),
                             bc(group[:, c, :].unsqueeze(2), [P, NG, EG]),
                             bc(r8[:, 4, c:c + 1, :], [P, NG, EG]), ALU.mult)
                ins.then_inc(gates_ready, 1)
                ps = result(dve, ("gatesT", l))
                nc.vector.tensor_copy(gatesT, ps[0:NE, 0:T]).then_inc(free(("gatesT", l)), 1)

                with dve.Fori(0, NE // 4) as it:
                    for pr in range(2):
                        for e in range(2):
                            for m in range(2):
                                moved(dve, ("G", l, pr, e, m), it)
                                ps = result(dve, ("U", l, pr, e, m), it)
                                tt(glu[:, m, :], ps[:, 0:T], act_g[:, m, :], ALU.mult) \
                                    .then_inc(free(("U", l, pr, e, m)), 1)
                                moved(dve, ("U", l, pr, e, m), it)
                                if e == 0 and m == 0:
                                    dve.wait_ge(gates_in[pr], it * 16 + (128 * l + 16))
                                tt(aff[:, 2 * e + m, :], glu[:, m, :], gb[:, pr, e, :], ALU.mult) \
                                    .then_inc(aff_ready, 1)
                        for k in range(KT):
                            ps = result(dve, ("D", l, pr, k), it)
                            tt(xn[:, k, :], ps[:, 0:T], xn[:, k, :], ALU.add).then_inc(free(("D", l, pr, k)), 1)
                for k in range(4, KT):
                    moved(dve, ("D", l, 1, k), NE // 4 - 1)
                gate = mod[l][:, 8 * GT2:8 * GT2 + 8, :]
                step(tt(ms[:], xn[:, :, TP:T], gate[:, :, 1:NC], ALU.mult))
                for t in range(KT):
                    stt(x[:, t, 0:TP], xn[:, t, 0:TP], gate[:, t, 0:1], x[:, t, 0:TP], ALU.mult, ALU.add)
                wait()
                tt(x[:, :, TP:T], x[:, :, TP:T], ms[:], ALU.add).then_inc(x_ready, 1)

            moe(0)

            normalise(2)
            modulate(n2, coef, G_KV, kvmod, 0, 1)
            modulate(h, coef2, G_MIX1, mod[1], SH1, SC1)
            ps = result(dve, "flogit")
            tsc(fz[:, 0, :], ps[0:FH, 0:T], vec[0:FH, V_BF:V_BF + 1], None, ALU.add).then_inc(free("flogit"), 1)
            moved(dve, "flogit")
            stt(fz[:, 1, :], fz[:, 0, :], -1.0, fz[:, 0, :], ALU.mult, ALU.min).then_inc(f_neg, 1)
            dve.wait_ge(f_exp, 2)
            stt(fz[:, 1, :], fz[:, 0, :], 0.0, fz[:, 3, :], ALU.min, ALU.subtract).then_inc(logf_ready, 1)
            dve.wait_ge(logf_ready, 1)
            tt(lf_diag, bc(ident[0:FH, 0:FH].unsqueeze(1), [FH, NS, FH]),
               bc(fz[:, 1, TP:T].unsqueeze(2), [FH, NS, FH]), ALU.mult).then_inc(diag_ready, 1)
            ps = result(dve, "logfT")
            nc.vector.tensor_copy(lf_tok, ps[:, 0:2 * FH].rearrange("p (c n) -> p c n", c=2)) \
                .then_inc(free("logfT"), 1)
            ps = result(dve, "F")
            nc.vector.tensor_copy(Fsb, ps[0:FH, 0:TP]).then_inc(free("F"), 1)
            for i in range(4):
                ps = result(dve, ("fvs", i))
                nc.vector.tensor_copy(q_one[:, i * 256:(i + 1) * 256], ps[0:NS, 0:256]) \
                    .then_inc(free(("fvs", i)), 1)
            moved(dve, ("fk", 3, 0))
            moved(dve, ("fk", 3, 1))
            moved(dve, ("fq", 3, 0))
            moved(dve, ("fq", 3, 1))
            tt(own, fq[:, :, TP:T], fk[:, :, TP:T], ALU.mult).then_inc(own_ready, 1)
            ps = result(dve, "own_F")
            tt(s_own, ps[:, 0:NS * FH].rearrange("p (b h) -> p b h", b=NS),
               past_tot[:].rearrange("p (b h) -> p b h", b=NS), ALU.add).then_inc(free("own_F"), 1)
            moved(dve, "own_F")
            ps = result(dve, "own_score")
            for r in range(2):
                view = s_own.rearrange("p b (t r) -> p r b t", r=2)[:, r, :, :]
                ins = tt(view, ps[:, r * 64:(r + 1) * 64].rearrange("p (t b) -> p b t", t=KT), view, ALU.subtract)
            ins.then_inc(free("own_score"), 1)
            ps = result(dve, "fvsT")
            nc.vector.tensor_copy(fvs, ps[:, 0:KT * NS].rearrange("p (t b) -> p t b", b=NS)) \
                .then_inc(free("fvsT"), 1)
            for i in range(2):
                ps = result(dve, ("qrow", i))
                nc.vector.tensor_copy(q_row[:, i * 512:(i + 1) * 512], ps[0:NS, :]).then_inc(free(("qrow", i)), 1)
            for key in ("own_score", "F", "fvsT", ("qrow", 0), ("qrow", 1)):
                moved(dve, key)
            dve.wait_ge(vs_stored, 16)

            def one_query(b):
                tsc(q_one, q_row, ident[0:NS, ds(b, 1)], None, ALU.mult).then_inc(one_ready, 1)

            one_query(0)
            moved(dve, ("qb", 0, "pre"))
            moved(dve, ("qb", 1, "pre"))

            half = [slice(64 * r, 64 * r + 64) for r in range(2)]

            def by_half(a, r):
                return a[half[r]].rearrange("p (t r) -> p r t", r=2)[:, r, :]

            def window(tag, b, it=None):
                if tag != "first":
                    dve.wait_ge(pd_ready, b)
                    wait()
                    step(nc.vector.tensor_copy(pO1, pO))
                    wait()
                    step(nc.vector.tensor_copy(dinv1, dinv))
                if tag != "last":
                    for hh in range(2):
                        ins = tsc(negF[:, hh, :], Fsb, c_("negeye", FH)[:, ds(b * 2 + hh, 1)], None, ALU.mult)
                    ins.then_inc(negF_ready, 1)

                def multiply(j):
                    dve.wait_ge(k_in[j % 4], b * 32 + 16 * (j // 4 + 1))
                    tt(prod[:, j % 2, :], kpg[:, j % 4, :], qb, ALU.mult).then_inc(k_used, 1)

                def add_up(j):
                    dve.wait_ge(k_used, b * NPG + (j + 1))
                    step(nc.vector.tensor_reduce(sc[:, j * FH:(j + 1) * FH],
                                                 prod[:, j % 2, :].rearrange("p (h d) -> p h d", h=FH), AX, ALU.add))

                def head_max(hh):
                    ps = result(dve, ("ps", hh, tag), it)
                    tt(s_sb[:, hh, :], ps[:, 0:3 * P], c_("causal"), ALU.add).then_inc(free(("ps", hh, tag)), 1)
                    moved(dve, ("ps", hh, tag), it)
                    nc.vector.tensor_reduce(hmax[:, hh, 0:1], s_sb[:, hh, 0:P], AX, ALU.max)
                    step(nc.vector.tensor_reduce(hmax[:, hh, 1:2], s_sb[:, hh, P:3 * P], AX, ALU.max))
                    wait()
                    tsc(hneg[:, hh, :], hmax[:, hh, :], -1.0, None, ALU.mult).then_inc(neg_max, 1)

                def norm_p(hh):
                    dve.wait_ge(p_raw, b * 2 + (hh + 1))
                    step(nc.vector.reciprocal(hinv[:, hh, :], hsum[:, hh, :]))
                    wait()
                    tsc(p_sb[:, hh, 0:P], p_sb[:, hh, 0:P], hinv[:, hh, 0:1], None, ALU.mult)
                    tsc(p_sb[:, hh, P:3 * P], p_sb[:, hh, P:3 * P], hinv[:, hh, 1:2], None, ALU.mult) \
                        .then_inc(p_ready, 1)

                if tag != "last":
                    multiply(0)
                    for j in range(1, NPG + 1):
                        if j < NPG:
                            if j > 1:
                                wait()
                            multiply(j)
                        add_up(j - 1)
                        if j in (2, 3):
                            head_max(j - 2)
                        if j in (4, 5):
                            norm_p(j - 4)
                    one_query(b + 1)
                    wait()
                    step(tt(sF, sc, past_F[:, ds(b, 1), :].rearrange("p a c -> p (a c)"), ALU.subtract))
                    wait()
                    nc.vector.tensor_reduce(mxp, sF.rearrange("p (g h) -> p h g", g=NPG), AX, ALU.max) \
                        .then_inc(mxp_ready, 1)
                    ps = result(dve, ("mxT", tag), it)
                    nc.vector.tensor_reduce(mx1, ps[0:FH, 0:P], AX, ALU.max).then_inc(free(("mxT", tag)), 1)
                    moved(dve, ("mxT", tag), it)
                    tsc(mxd, ident[0:FH, 0:FH], mx1, None, ALU.mult).then_inc(mxd_ready, 1)
                    ps = result(dve, ("mxb", tag), it)
                    own_b = s_own[:, ds(b, 1), :].rearrange("p a h -> p (a h)")
                    tt(mx, ps[:, 0:FH], own_b, ALU.max).then_inc(free(("mxb", tag)), 1)
                    moved(dve, ("mxb", tag), it)
                    tt(sF.rearrange("p (g h) -> p g h", g=NPG), sF.rearrange("p (g h) -> p g h", g=NPG),
                       bc(mx.unsqueeze(1), [P, NPG, FH]), ALU.subtract)
                    tt(sO, own_b, mx, ALU.subtract).then_inc(shifted, 1)
                    dve.wait_ge(pE_ready, b + 1)
                    nc.vector.tensor_reduce(psm, pE.rearrange("p (g h) -> p h g", g=NPG), AX, ALU.add) \
                        .then_inc(psm_ready, 1)
                    ps = result(dve, ("den", tag), it)
                    tt(den, ps[:, 0:FH], pO, ALU.add).then_inc(free(("den", tag)), 1)
                    moved(dve, ("den", tag), it)
                    step(nc.vector.reciprocal(dinv, den))
                if tag != "first":
                    for r in range(2):
                        step(tt(oO[half[r]], by_half(pO1, r),
                                fvs[half[r], :, ds(b - 1, 1)].rearrange("p t a -> p (t a)"), ALU.mult))
                    ps = result(dve, ("oT", tag), it)
                    wait()
                    for r in range(2):
                        ins = tt(oS[half[r]], ps[half[r], r:r + (FH + 2) * (KT - 1) + 1:FH + 2], oO[half[r]], ALU.add)
                    ins.then_inc(free(("oT", tag)), 1)
                    moved(dve, ("oT", tag), it)
                    for r in range(2):
                        ins = tt(fo[half[r], :, ds(b + (TP - 1), 1)].rearrange("p t a -> p (t a)"), oS[half[r]],
                                 by_half(dinv1, r), ALU.mult)
                    ins.then_inc(sample_done, 1)

            window("first", 0)
            with dve.Fori(0, NS - 1) as it:
                own_steps.enter(it, 18)
                window("mid", it + 1, it)
                own_steps.leave(NS - 1)
            window("last", NS)

            residual("fout", mod[1][:, 8 * GT1:8 * GT1 + 8, :])
            moe(1)
            normalise(4)
            wait()
            tt(h[:], xn[:], bc(gain[G_FINAL].unsqueeze(2), [P, KT, T]), ALU.mult).then_inc(h_ready, 1)


def constants():
    c = np.zeros((P, N_CONST), np.float32)

    def put(name, value):
        a, n = CONST[name]
        c[:, a:a + n] = value

    i = np.arange(P)
    put("ident", np.eye(P))
    put("ones", 1.0)
    put("half0", (i < 64)[:, None])
    put("half1", (i >= 64)[:, None])
    inv = np.float32(10000.0) ** (-i.astype(np.float32) / np.float32(P))
    pos = np.concatenate([np.arange(TP), np.full(NS, PAST)]).astype(np.float32)
    angle = (pos[None, :] * inv.astype(np.float32)[:, None]).astype(np.float32).astype(np.float64)
    for name, f in (("cos", np.cos), ("sin", np.sin)):
        put(name + "q", f(angle))
        put(name + "k", f(angle).astype(np.float32) * np.float32(RK ** -0.5))
    log_gamma = np.log(np.array(GAMMA, np.float32)).astype(np.float64)
    rel = np.arange(TP)[None, :] - i[:, None]
    for hd in range(RH):
        a = CONST["decay"][0] + hd * TP
        c[:, a:a + TP] = np.where(rel >= 0, np.exp(log_gamma[hd] * np.maximum(rel, 0)), 0.0)
        for k in range(2):
            c[:, CONST["kdec"][0] + k * RH + hd] = np.exp(log_gamma[hd] * (TP - 1 - k * P - i))
    put("upto", rel >= 0)
    future = np.where(i[None, :] <= i[:, None], 0.0, NEG)
    put("causal", np.concatenate([future, np.zeros((P, P)), future], 1))
    c[0:FH, CONST["negeye"][0]:CONST["negeye"][0] + FH] = -np.eye(FH)
    put("eps", EPS)
    put("first4", NG - np.arange(NG))
    put("first8", EG - np.arange(EG))
    return c


def features(a):
    return np.ascontiguousarray(a.reshape(a.shape[0], -1, P).transpose(2, 1, 0))


def column_slots(w):
    return w.reshape(KT, P, -1, 256).transpose(2, 1, 0, 3).reshape(-1, P, SW)


def weight_stream(w_mod, w_kvmod, w_ret_in, w_ret_out, w_kv, w_fq, w_fo, w_gate, w_up, w_down):
    s = np.empty((SLOTS, P, SW), np.float32)
    s[S_MOD0:S_MOD0 + 24] = column_slots(w_mod[0])
    s[S_RET:S_RET + 48:2] = column_slots(w_ret_in)
    s[S_RET + 1:S_RET + 48:2] = column_slots(w_mod[1])
    s[S_RO:S_RO + 16:2] = w_ret_out.reshape(2, KT, P, 4, 256).transpose(3, 0, 2, 1, 4).reshape(8, P, SW)
    s[S_RO + 1:S_RO + 16:2] = column_slots(w_kvmod)
    s[S_KV:S_KV + 8] = column_slots(w_kv)
    s[S_FQ:S_FQ + 4] = column_slots(w_fq)
    s[S_FO:S_FO + 4] = column_slots(w_fo)
    for l, base in ((0, S_MOE0), (1, S_MOE1)):
        m = s[base:base + 3 * NE].reshape(NE // 2, 6, P, SW)
        for j, w in ((0, w_gate), (1, w_up)):
            m[:, j:4:2] = column_slots(w[l]).reshape(NE // 2, 2, P, SW)
        m[:, 4:6] = w_down[l].reshape(NE // 2, 2, 2, P, D).transpose(0, 1, 3, 2, 4).reshape(NE // 2, 2, P, SW)
    return s


def kernel(x_prompt, x_sample, c_prompt, c_sample, state_ret, cache_k, cache_v, cache_logf, page_table,
           w_mod, b_mod, g_mix, g_ffn, w_ret_in, w_ret_out, g_kv, w_kvmod, b_kvmod, w_kv, w_f, b_f,
           w_fq, w_fo, w_rg, w_re, w_e_gate, w_e_up, w_e_down, g_final):
    import concourse.bacc as bacc
    from concourse.bass_utils import run_bass_kernel_spmd

    a = {k: np.asarray(v) for k, v in locals().items() if k not in ("bacc", "run_bass_kernel_spmd")}
    pool = a["cache_k"].shape[0]
    vectors = np.zeros((P, N_VEC), np.float32)
    vectors[:, V_BMOD:V_BMOD + 96] = a["b_mod"].reshape(96, P).T
    vectors[:, V_BKV:V_BKV + 16] = a["b_kvmod"].reshape(16, P).T
    gains = (a["g_mix"][0], a["g_mix"][1], a["g_ffn"][0], a["g_ffn"][1], a["g_kv"], a["g_final"])
    vectors[:, V_GAIN:V_GAIN + 48] = np.concatenate(gains).reshape(48, P).T
    vectors[0:FH, V_BF] = a["b_f"]
    small = [a["w_f"].reshape(KT, P, FH).transpose(1, 0, 2).reshape(P, -1)]
    for l in range(2):
        both = np.concatenate([a["w_rg"][l], a["w_re"][l]], 1)
        small.append(both.reshape(KT, P, 36).transpose(1, 0, 2).reshape(P, -1))
    ins = {
        "consts": constants(),
        "x_in": features(np.concatenate([a["x_prompt"][0], a["x_sample"][:, 0]])),
        "c_in": features(np.concatenate([a["c_prompt"], a["c_sample"]])),
        "vecs": vectors,
        "wsmall": np.concatenate(small, 1),
        "wstream": weight_stream(a["w_mod"], a["w_kvmod"], a["w_ret_in"][0], a["w_ret_out"][0], a["w_kv"],
                                 a["w_fq"][0], a["w_fo"][0], a["w_e_gate"], a["w_e_up"], a["w_e_down"]),
        "kcache": a["cache_k"].reshape(pool, PAGE, D),
        "vcache": a["cache_v"].reshape(pool, PAGE, D),
        "lfcache": a["cache_logf"],
        "ptable": a["page_table"].reshape(1, NPAGES),
        "state": a["state_ret"].reshape(NS * RH, 2, P, RV).transpose(0, 2, 1, 3),
    }
    outs = {
        "y_out": (P, KT, T), "sp_out": (RH, P, 2, RV), "ss_out": (NS * RH, P, 2, RV), "k_out": (P, KT, T),
        "vp_out": (P, 2, D), "vs_out": (NS, D), "lf_out": (FH, T),
    }
    nc = bacc.Bacc("TRN2", target_bir_lowering=False, num_devices=1)
    arrays, args = {}, []
    for name, v in ins.items():
        v = np.ascontiguousarray(v)
        arrays[name] = v
        args.append(nc.dram_tensor(name, v.shape, mybir.dt.from_np(v.dtype), kind="ExternalInput").ap())
    for name, shape in outs.items():
        args.append(nc.dram_tensor(name, shape, F32, kind="ExternalOutput").ap())
    build(nc, *args)
    r = run_bass_kernel_spmd(nc, [arrays], core_ids=[0]).results[0]

    y = r["y_out"].transpose(2, 1, 0).reshape(T, D)
    k = r["k_out"].transpose(2, 1, 0).reshape(T, FH, HD)
    vp = r["vp_out"].transpose(1, 0, 2).reshape(1, TP, FH, HD)
    vs = r["vs_out"].reshape(NS, 1, FH, HD)
    lf = r["lf_out"].T
    sp = r["sp_out"].transpose(0, 2, 1, 3).reshape(1, 1, RH, RK, RV)
    ss = r["ss_out"].transpose(0, 2, 1, 3).reshape(1, NS, RH, RK, RV)
    return (y[None, :TP], y[TP:, None], sp, ss, k[None, :TP], vp, lf[None, :TP], k[TP:, None], vs, lf[TP:, None])
```

```python
from contextlib import ExitStack

import numpy as np

import concourse.bass as bass
from concourse import mybir

F32 = mybir.dt.float32
I32 = mybir.dt.int32
ALU = mybir.AluOpType
ACT = mybir.ActivationFunctionType
AX = mybir.AxisListType.X
ds = bass.ds

P = 128
D = 1024
KT = D // P
TP, NS = 256, 8
T = TP + NS
NC = 1 + NS
RH, RK, RV = 4, 256, 512
RVT = RH * RV // P
FH, HD = 16, 64
PAST, PAGE = 1024, 128
NPG = PAST // PAGE
NPAGES = NS * NPG
NG, EG = 4, 8
NE = NG * EG
FF = D // 4
EPS = 1e-6
NEG = -1e30
R = 6
SW = 2048
PICKS = 2 * T
WIN = 128
XW = PICKS // (WIN + 1)
NW = NE + XW
PC = -(-PICKS // P)
PROWS = [min(P, PICKS - c * P) for c in range(PC)]
TROWS = [min(P, T - c * P) for c in range(3)]
S_MOD0, S_RET, S_RO, S_MOE0 = 0, 24, 72, 88
S_KV = S_MOE0 + 3 * NE
S_FQ = S_KV + 8
S_FO = S_FQ + 4
S_MOE1 = S_FO + 4
SLOTS = S_MOE1 + 3 * NE
GAMMA = [1.0 - 2.0 ** (-5.0 - h) for h in range(RH)]

CONST = {}
_at = 0
for _name, _n in (("ident", P), ("ones", P), ("half0", P), ("half1", P), ("cosq", T), ("sinq", T),
                  ("cosk", T), ("sink", T), ("decay", RH * TP), ("kdec", 2 * RH), ("upto", TP),
                  ("causal", 3 * P), ("negeye", FH), ("eps", 1), ("first4", NG), ("first8", EG),
                  ("place", PICKS), ("before", 2 * NE), ("back", 4 * NE)):
    CONST[_name] = (_at, _n)
    _at += _n
N_CONST = _at

GU_SLOT = [6 * (e // 2) + 2 * (e % 2) for e in range(NE)]
DN_SLOT = [6 * (e // 2) + 4 + e % 2 for e in range(NE)]
GU_LAST, DN_LAST = GU_SLOT[-1], DN_SLOT[-1]

V_BMOD, V_BKV, V_GAIN, V_BF = 0, 96, 112, 160
N_VEC = 161
G_MIX0, G_MIX1, G_FFN0, G_FFN1, G_KV, G_FINAL = range(6)
SH1, SC1, GT1, SH2, SC2, GT2 = range(6)


class Turns:

    def __init__(self):
        self.count = [0] * 8
        self.at = {}

    def add(self, key, bank):
        self.at[key] = (bank, self.count[bank], 0)
        self.count[bank] += 1

    def loop(self, steps, jobs):
        first = list(self.count)
        per = [sum(b == bank for _, b in jobs) for bank in range(8)]
        for key, bank in jobs:
            self.at[key] = (bank, self.count[bank], per[bank])
            self.count[bank] += 1
        self.count = [f + steps * n for f, n in zip(first, per)]


L = [0, 1, 2, 3]
X0, X1, X2, M = 4, 5, 6, 7


def plan_turns():
    t = Turns()
    t.loop(24 // R, [(("row0", r), (X1, X2)[r % 2]) for r in range(R)] + [("mod0", M)])
    t.add(("rms", 0), X0)
    t.add("mod1", M)
    for i in range(8):
        for m in range(2):
            t.add(("qk", i, m), L[(2 * i + m) % 4])
    for i in range(8):
        for c in range(2):
            t.add(("v", i, c), L[(2 * i + c) % 4])
        t.add(("vs", i), (X0, X1)[i % 2])
    t.add(("past", 0), X0)
    t.add(("past", 1), X1)
    t.add("past_total", X0)
    for i in range(16):
        t.add(("row1", i), X2)
    for h in range(RH):
        t.add(("ra", h), X0)
        t.add(("rk", h), X1)
        for v in range(4):
            t.add(("ro", h, v), L[v])
        for s in range(2):
            t.add(("rs", h, s), X2)
    for i in range(8):
        for u in range(4):
            t.add(("vb", 4 * i + u), X0)
        for m in range(2):
            t.add(("g", i, m), L[(2 * i + m) % 4])
        t.add(("row1", 16 + i), X2)
    for h in range(RH):
        t.add(("os", h), X1)
        t.add(("osT", h), X1)
    for h in range(RH):
        t.add(("gn", h), L[h])
    t.add("kvmod", M)
    for i in range(8):
        t.add(("row2", i), X2)
    for n in range(4):
        for m in range(2):
            t.add(("rout", n, m), L[(2 * n + m) % 4])

    def moe(l):
        t.add(("rms", 1 + 2 * l), X0)
        t.add(("logits", l), X1)
        t.add(("logitsT", l), X1)
        t.add(("count", l), X2)
        for c in range(3):
            for i in range(2):
                t.add(("ht", l, c, i), L[(2 * c + i) % 4])
        t.add(("place", l), X0)
        for k in range(KT):
            for i in range(2):
                t.add(("sorted", l, k, i), (2 * k + i) % 8)
        t.loop(NE // 2, [(("GU", l, 0), L[0]), (("GU", l, 1), L[1]), (("aT", l, 0), L[2]), (("aT", l, 1), L[3])] +
               [(("Y", l, e, i), (X0, X1, X2, M)[2 * e + i]) for e in range(2) for i in range(2)])
        for c in range(PC):
            t.add(("gT", l, c), L[c % 4])
        for k in range(KT):
            t.add(("sum", l, k), k)

    moe(0)
    t.add(("rms", 2), X0)
    t.add("flogit", X1)
    t.add("logfT", X2)
    t.add("F", X0)
    for i in range(4):
        for m in range(2):
            t.add(("fk", i, m), L[(2 * i + m) % 4])
    for i in range(4):
        for c in range(2):
            t.add(("fv", i, c), L[(2 * i + c) % 4])
        t.add(("fvs", i), (X0, X1)[i % 2])
    for i in range(4):
        for m in range(2):
            t.add(("fq", i, m), L[(2 * i + m) % 4])
    t.add("own_score", X1)
    t.add("own_F", X2)
    t.add("fvsT", X0)
    t.add(("qrow", 0), X1)
    t.add(("qrow", 1), X2)
    t.add(("qb", 0, "pre"), X0)
    t.add(("qb", 1, "pre"), X1)

    def window(tag):
        values = [(("pv", 0, tag), X2), (("pv", 1, tag), M)]
        heads = [(("ps", 0, tag), L[0]), (("ps", 1, tag), L[1]), (("pT", 0, tag), L[2]), (("pT", 1, tag), L[3]),
                  (("po", 0, tag), L[0]), (("po", 1, tag), L[1]), (("qb", 0, tag), L[2]), (("qb", 1, tag), L[3])]
        scores = [(("mxT", tag), X0), (("mxb", tag), X1), (("den", tag), X0)]
        turned = [(("oT", tag), X1)]
        return {"first": heads + scores, "mid": values + heads + scores + turned,
                "end": values + heads + scores + turned, "last": values + turned}[tag]

    for key, bank in window("first"):
        t.add(key, bank)
    t.loop(NS - 2, window("mid"))
    for key, bank in window("end") + window("last"):
        t.add(key, bank)
    for n in range(4):
        for m in range(2):
            t.add(("fout", n, m), L[(2 * n + m) % 4])
    moe(1)
    t.add(("rms", 4), X0)
    return t.at


class Steps:

    def __init__(self, eng, sem):
        self.eng, self.sem, self.n, self.offset = eng, sem, 0, None

    def step(self, ins):
        ins.then_inc(self.sem, 1)
        self.n += 1

    def wait(self):
        self.eng.wait_ge(self.sem, self.n if self.offset is None else self.offset + self.n)

    def enter(self, it, per):
        self.offset, self.per, self.start = it * per, per, self.n

    def leave(self, steps):
        assert self.n - self.start == self.per, (self.n - self.start, self.per)
        self.n += self.per * (steps - 1)
        self.offset = None


def build(nc, consts, x_in, c_in, vecs, wsmall, wstream, kcache, vcache, lfcache, ptable, state,
          y_out, sp_out, ss_out, k_out, vp_out, vs_out, lf_out):
    at = plan_turns()
    ctx = ExitStack()
    with ctx:
        def sb(name, shape, dt=F32):
            return ctx.enter_context(nc.sbuf_tensor(name, shape, dt))

        def sem(name):
            return ctx.enter_context(nc.semaphore(name))

        y_rows = nc.dram_tensor("y_rows", (PICKS + WIN, D), F32, kind="Internal").ap()

        cst = sb("cst", [P, N_CONST])
        vec = sb("vec", [P, N_VEC])
        wsm = sb("wsm", [P, KT * FH + 2 * KT * 36])
        page_ids = sb("page_ids", [1, NPAGES], I32)
        start_ids = sb("start_ids", [1, NW], I32)
        extra_ids = sb("extra_ids", [1, 2 * XW + 1], I32)
        x = sb("x", [P, KT, T])
        xn = sb("xn", [P, KT, T])
        h = sb("h", [P, KT, T])
        cs = sb("cs", [P, KT, NC])
        ring = sb("ring", [P, R, SW])
        mod = [sb(f"mod{l}", [P, 48, NC]) for l in range(2)]
        kvmod = sb("kvmod", [P, 16, NC])
        coef = sb("coef", [P, KT, NC])
        coef2 = sb("coef2", [P, KT, NC])
        root = sb("root", [P, T])
        rstd = sb("rstd", [P, T])
        ms = sb("ms", [P, KT, NS])
        past_F = sb("past_F", [P, NS, NPG * FH])
        past_tot = sb("past_tot", [P, NS * FH])

        arena_cols = 26600
        arena = sb("arena", [P, arena_cols])

        class Region:
            def __init__(self, start):
                self.at = start

            def take(self, *shape, rows=P):
                n = int(np.prod(shape))
                a = arena[0:rows, self.at:self.at + n]
                self.at += n
                assert self.at <= arena_cols, self.at
                if len(shape) == 2:
                    a = a.rearrange("p (a b) -> p a b", a=shape[0])
                if len(shape) == 3:
                    a = a.rearrange("p (a b c) -> p a b c", a=shape[0], b=shape[1])
                return a

        ret = Region(0)
        qk = ret.take(2 * KT, T)
        vtok = ret.take(2, RH * RV)
        vrow = xn[0:NS].rearrange("p a b -> p (a b)")[:, 0:RH * RV]
        mrow = ret.take(2, 256)
        qz = ret.take(2, RH, NS * NS)
        osb = ret.take(RV)
        gsil = ret.take(RVT, T)
        oret = ret.take(RVT, T)
        st = ret.take(4, 2, RV)
        at_sb = ret.take(2, 3 * P)
        ktok = ret.take(2, 2, RK)
        sp_sb = ret.take(2, RV)
        rot = ret.take(4, T)
        past_lf = gsil.rearrange("p a b -> p (a b)")[:, 0:NS * NPG * FH] \
            .rearrange("p (b g h) -> p b g h", b=NS, g=NPG)
        past_pre = gsil.rearrange("p a b -> p (a b)")[:, NS * NPG * FH:2 * NS * NPG * FH] \
            .rearrange("p (b g h) -> p b g h", b=NS, g=NPG)
        past_sum = gsil.rearrange("p a b -> p (a b)")[:, 2 * NS * NPG * FH:2 * NS * NPG * FH + NS * FH] \
            .rearrange("p (b h) -> p b h", b=NS)

        me = Region(0)
        act_g = me.take(2, FF)
        aff = me.take(2, FF)
        aff_T = me.take(2, 2, P)
        xw = me.take(2, KT, WIN)
        x_sorted = me.take(KT, PICKS + WIN)
        y_sorted = x_sorted.rearrange("p a b -> p (a b)")[:, 0:PC * D].rearrange("p (c n) -> p c n", c=PC)
        h_tok = me.take(3, D)
        y_sb = h_tok[:, 0:2, :]
        pick = me.take(3, PICKS)
        pick_g = me.take(3, PICKS)
        pick_two = h_tok.rearrange("p a b -> p (a b)")[:, 0:3 * PICKS].rearrange("p (c n) -> p c n", c=3)
        pick_gT = me.take(PC, T)
        lg = me.take(3, 36)
        lgT = me.take(T, rows=36)
        r4 = me.take(8, 3, NG)
        r8 = me.take(8, 3, EG)
        r1 = me.take(8, 3)
        le4 = me.take(3, EG, NG)
        chosen = me.take(3, 3, NE)
        place = me.take(3, NE)
        where = me.take(2, 3, NE)
        place_of = me.take(2, 3)
        count_T = me.take(P, rows=NE)
        first_n = me.take(2 * NE, rows=1)
        over = me.take(2 * NE, rows=1)
        rest = me.take(2 * NE, rows=1)
        keys = me.take(3, 2 * NE, rows=1)
        top = me.take(3, 8, rows=1)
        starts = me.take(NW, rows=1)
        extra = me.take(2 * XW + 1, rows=1)
        fx = Region(0)
        n2 = fx.take(KT, T)
        fq = fx.take(KT, T)
        fk = fx.take(KT, T)
        fo = n2
        fv = fx.take(2, D)
        fvs = fx.take(KT, NS)
        own = fx.take(KT, NS)
        s_own = fx.take(NS, FH)
        fz = fx.take(4, T, rows=FH)
        lf_tok = fx.take(2, FH)
        Fsb = fx.take(TP, rows=FH)
        q_row = fx.take(D, rows=NS)
        q_one = fx.take(D, rows=NS)
        lf_diag = fx.take(NS, FH, rows=FH)
        negF = fx.take(2, TP, rows=FH)
        q_st = fx.take(TP)
        k_st = fx.take(TP)
        v_st = fx.take(2, P)
        s_sb = fx.take(2, 3 * P)
        p_sb = fx.take(2, 3 * P)
        pT_sb = fx.take(2, 3 * P)
        hmax = fx.take(2, 2)
        hneg = fx.take(2, 2)
        hsum = fx.take(2, 2)
        hinv = fx.take(2, 2)
        sF = fx.take(NPG * FH)
        mxp = fx.take(FH)
        mx1 = fx.take(1, rows=FH)
        mxd = fx.take(FH, rows=FH)
        mx = fx.take(FH)
        sM = fx.take(NPG * FH)
        sO = fx.take(FH)
        pD = fx.take(NPG * FH)
        pO = fx.take(FH)
        psm = fx.take(FH)
        den = fx.take(FH)
        dinv = fx.take(FH)
        dinv1 = fx.take(FH)
        pO1 = fx.take(FH)
        pE = fx.take(NPG * FH)
        sc = fx.take(NPG * FH)
        oO = fx.take(KT)
        oS = fx.take(KT)
        pages = Region(arena_cols - 8 * D)
        assert me.at <= pages.at and fx.at <= pages.at, (me.at, fx.at, pages.at)
        kpg = pages.take(4, D)
        vpg = pages.take(4, D)
        flat = lambda a: a[:, :, :].rearrange("p a b -> p (a b)")
        qb = flat(xn)[:, 0:D]
        o_row = flat(xn)[0:FH, D:2 * D]
        prod = flat(h)[:, 0:2 * D].rearrange("p (r n) -> p r n", r=2)

        bank = [ctx.enter_context(nc.psum_tensor(f"bank{i}", [P, 512], F32)) for i in range(8)]
        filled = [sem(f"filled{i}") for i in range(8)]
        drained = [sem(f"drained{i}") for i in range(8)]

        cond_in = sem("cond_in")
        consts_in = sem("consts_in")
        x_loaded = sem("x_loaded")
        lf_in = sem("lf_in")
        ids_in = sem("ids_in")
        slot_in = [sem(f"slot_in{r}") for r in range(R)]
        slot_used = sem("slot_used")
        state_in = [sem(f"state_in{r}") for r in range(4)]
        state_out = [sem(f"state_out{r}") for r in range(4)]
        state_scaled = sem("state_scaled")
        state_read = sem("state_read")
        k_in = [sem(f"k_in{r}") for r in range(4)]
        v_in = [sem(f"v_in{r}") for r in range(4)]
        k_used = sem("k_used")
        v_used = sem("v_used")
        chosen_ready = sem("chosen_ready")
        pick_ready = sem("pick_ready")
        pick_g_ready = sem("pick_g_ready")
        windows_ready = sem("windows_ready")
        xw_ready = sem("xw_ready")
        silu_ready = sem("silu_ready")
        y_stored = [sem(f"y_stored{e}") for e in range(2)]
        y_in = [sem(f"y_in{c}") for c in range(PC)]
        far_in = [sem(f"far_in{l}") for l in range(2)]
        far_product = [sem(f"far_product{l}") for l in range(2)]
        far_silu = [sem(f"far_silu{l}") for l in range(2)]
        far_moved = [sem(f"far_moved{l}") for l in range(2)]
        far_stored = [sem(f"far_stored{l}") for l in range(2)]
        past_ready = sem("past_ready")
        cond_ready = sem("cond_ready")
        squared = sem("squared")
        h_ready = sem("h_ready")
        x_ready = sem("x_ready")
        o_squared = sem("o_squared")
        o_rooted = sem("o_rooted")
        o_ready = sem("o_ready")
        dve_steps = sem("dve_steps")
        route_e = sem("route_e")
        route_x = sem("route_x")
        f_exp = sem("f_exp")
        f_neg = sem("f_neg")
        logf_ready = sem("logf_ready")
        one_ready = sem("one_ready")
        pE_ready = sem("pE_ready")
        lf_stored = sem("lf_stored")
        vs_stored = sem("vs_stored")
        qz_ready = sem("qz_ready")
        own_ready = sem("own_ready")
        diag_ready = sem("diag_ready")
        staged = sem("staged")
        negF_ready = sem("negF_ready")
        neg_max = sem("neg_max")
        p_raw = sem("p_raw")
        p_ready = sem("p_ready")
        mxp_ready = sem("mxp_ready")
        mxd_ready = sem("mxd_ready")
        shifted = sem("shifted")
        pd_ready = sem("pd_ready")
        psm_ready = sem("psm_ready")
        sample_done = sem("sample_done")
        sp_stored = sem("sp_stored")
        stored = sem("stored")

        def c_(name, rows=P):
            a, n = CONST[name]
            return cst[0:rows, a:a + n]

        ident, ones = c_("ident"), c_("ones")
        gain = [vec[:, V_GAIN + 8 * g:V_GAIN + 8 * g + 8] for g in range(6)]
        w_f = wsm[:, 0:KT * FH].rearrange("p (k n) -> p k n", k=KT)
        w_r = [wsm[:, KT * FH + l * KT * 36:KT * FH + (l + 1) * KT * 36].rearrange("p (k n) -> p k n", k=KT)
               for l in range(2)]

        def slot(n, rows=KT):
            return ring[:, n % R, :].rearrange("p (k c) -> p k c", k=rows)

        def turn(key, it=None):
            b, first, per = at[key]
            return b, first if it is None or per == 0 else it * per + first

        def result(eng, key, it=None):
            b, n = turn(key, it)
            eng.wait_ge(filled[b], n + 1)
            return bank[b]

        def free(key):
            return drained[at[key][0]]

        def moved(eng, key, it=None):
            b, n = turn(key, it)
            eng.wait_ge(drained[b], n + 1)

        def further(eng, l):
            eng.wait_ge(windows_ready, l + 1)
            return eng.value_load(extra_ids[0:1, 2 * XW:2 * XW + 1], min_val=0, max_val=PICKS)

        far_w = [flat(h)[:, 0:SW], flat(xn)[:, 0:SW]]

        def bc(ap, shape):
            return ap.to_broadcast(shape)

        block = ctx.enter_context(nc.Block())

        @block.sync
        def _(sp):
            sp.dma_start(cs[:], c_in).then_inc(cond_in, 16)
            for r in range(R):
                sp.dma_start(ring[:, r, :], wstream[r]).then_inc(slot_in[r], 16)
                if r == 0:
                    sp.dma_start(cst[:], consts).then_inc(consts_in, 16)
                    sp.dma_start(vec[:], vecs).then_inc(consts_in, 16)
                    sp.dma_start(wsm[:], wsmall).then_inc(consts_in, 16)
            sp.dma_start(x[:], x_in).then_inc(x_loaded, 16)

            def stream(lo, hi):
                laps = (hi - lo) // R
                with sp.Fori(0, laps) as lap:
                    for n in range(lo, lo + R):
                        sp.wait_ge(slot_used, lap * R + (n - R + 1))
                        sp.dma_start(ring[:, n % R, :], wstream[ds(lap * R + n, 1)]
                                     .rearrange("a p n -> p (a n)")).then_inc(slot_in[n % R], 16)
                for n in range(lo + laps * R, hi):
                    sp.wait_ge(slot_used, n - R + 1)
                    sp.dma_start(ring[:, n % R, :], wstream[n]).then_inc(slot_in[n % R], 16)

            def key_page(b, j, first=False):
                page = sp.value_load(page_ids[0:1, ds(b * NPG + j, 1)], min_val=0, max_val=kcache.shape[0] - 1)
                if not first:
                    sp.wait_ge(k_used, b * NPG + (j - 3))
                sp.dma_start(kpg[:, j % 4, :], kcache[ds(page, 1)].rearrange("a p n -> p (a n)")) \
                    .then_inc(k_in[j % 4], 16)

            stream(R, S_MOE0 + 3 * NE)
            sp.wait_ge(ids_in, 16)
            for r in range(4):
                sp.wait_ge(state_out[r], 16 * NS * RH // 4)
            sp.wait_ge(sp_stored, 16 * RH)
            for j in range(4):
                key_page(0, j, True)
            stream(S_KV, S_MOE1 + 1)
            for j in range(4, NPG):
                key_page(0, j)
            with sp.Fori(0, NS - 1) as it:
                for j in range(NPG):
                    key_page(it + 1, j)
            stream(S_MOE1 + 1, SLOTS)

        @block.gpsimd
        def _(pool):
            pool.dma_start(page_ids[:], ptable).then_inc(ids_in, 16)
            pool.wait_ge(ids_in, 16)
            with pool.Fori(0, NPAGES) as j:
                page = pool.value_load(page_ids[0:1, ds(j, 1)], min_val=0, max_val=kcache.shape[0] - 1)
                pool.dma_start(past_lf.rearrange("p b g h -> p (b g) h")[:, ds(j, 1), :].rearrange("p a h -> p (a h)"),
                               lfcache[ds(page, 1)].rearrange("a p h -> p (a h)")).then_inc(lf_in, 16)
            def state_of(u):
                return u % NS * RH + u // NS

            for u in range(4):
                pool.dma_start(st[:, u, :, :], state[state_of(u)]).then_inc(state_in[u], 16)
            for u in range(NS * RH):
                moved(pool, ("vb", u))
                pool.dma_start(ss_out[state_of(u)], st[:, u % 4, :, :]).then_inc(state_out[u % 4], 16)
                nxt = u + 3
                if 4 <= nxt < NS * RH:
                    pool.wait_ge(state_out[nxt % 4], 16 * (nxt // 4))
                    old = nxt - 4
                    if old % NS == NS - 1:
                        result(pool, ("os", old // NS))
                    else:
                        pool.wait_ge(state_read, old // NS * (NS - 1) + old % NS + 1)
                    pool.dma_start(st[:, nxt % 4, :, :], state[state_of(nxt)]).then_inc(state_in[nxt % 4], 16)

            def page_of(j):
                return pool.value_load(page_ids[0:1, ds(j, 1)], min_val=0, max_val=kcache.shape[0] - 1)

            def load_page(ring_, cache, sems, r, page):
                pool.dma_start(ring_[:, r, :], cache[ds(page, 1)].rearrange("a p n -> p (a n)")).then_inc(sems[r], 16)

            for r in range(4):
                pool.wait_ge(state_out[r], 16 * NS * RH // 4)
            pool.wait_ge(x_ready, 1)
            pool.wait_ge(sp_stored, 16 * RH)
            for j in range(4):
                load_page(vpg, vcache, v_in, j, page_of(j))

            def store_windows(l):
                pool.wait_ge(windows_ready, l + 1)
                with pool.Fori(0, NE // 2) as it:
                    first = [pool.value_load(start_ids[0:1, ds(it * 2 + e, 1)], min_val=0, max_val=PICKS)
                             for e in range(2)]
                    for e in range(2):
                        moved(pool, ("Y", l, e, 0), it)
                        moved(pool, ("Y", l, e, 1), it)
                        pool.wait_ge(y_stored[1 - e], it * 16 + 16 * (l * (NE // 2) + e))
                        pool.dma_start(y_rows[ds(first[e], WIN)], y_sb[:, e, :]).then_inc(y_stored[e], 16)
                for e in range(2):
                    pool.wait_ge(y_stored[e], 16 * (l + 1) * (NE // 2))
                with pool.If(further(pool, l) > 0):
                    with pool.Fori(0, XW) as i:
                        gu = pool.value_load(extra_ids[0:1, ds(i, 1)], min_val=0, max_val=GU_LAST)
                        down = pool.value_load(extra_ids[0:1, ds(i + XW, 1)], min_val=0, max_val=DN_LAST)
                        to = pool.value_load(start_ids[0:1, ds(i + NE, 1)], min_val=0, max_val=PICKS)
                        base = (S_MOE0, S_MOE1)[l]
                        pool.wait_ge(far_product[l], i * 3)
                        for j in range(2):
                            pool.dma_start(far_w[j], wstream[ds(gu + (base + j), 1)].rearrange("a p n -> p (a n)")) \
                                .then_inc(far_in[l], 16)
                        pool.wait_ge(far_product[l], i * 3 + 1)
                        pool.dma_start(far_w[0], wstream[ds(down + base, 1)].rearrange("a p n -> p (a n)")) \
                            .then_inc(far_in[l], 16)
                        pool.wait_ge(far_moved[l], i * 4 + 4)
                        pool.dma_start(y_rows[ds(to, WIN)], y_sb[:, 0, :]).then_inc(far_stored[l], 16)
                        pool.wait_ge(far_stored[l], i * 16 + 16)
                pool.wait_ge(xw_ready, (l + 1) * (NE + 2))
                for c, rows in enumerate(PROWS):
                    pool.dma_start(y_sorted[0:rows, c, :], y_rows[c * P:c * P + rows]).then_inc(y_in[c], 16)

            store_windows(0)
            def values_of(b, j, tag=None, it=None):
                page = page_of(b * NPG + j)
                if j >= 4:
                    pool.wait_ge(v_used, b * (NPG - 1) + (j - 3))
                elif j < 3:
                    pool.wait_ge(v_used, b * (NPG - 1) + (j + 5 - (NPG - 1)))
                else:
                    result(pool, ("pv", 1, tag), it)
                load_page(vpg, vcache, v_in, j % 4, page)

            def next_values(tag, b, it=None):
                for j in range(NPG):
                    if j < 4:
                        values_of(b - 1, 4 + j)
                    else:
                        values_of(b, j - 4, tag, it)

            with pool.Fori(0, NS - 2) as it:
                next_values("mid", it + 1, it)
            next_values("end", NS - 1)
            for j in range(4, NPG):
                values_of(NS - 1, j)
            store_windows(1)
            for r in range(4):
                pool.wait_ge(state_out[r], 16 * NS * RH // 4)

        @block.tensor
        def _(pe):
            first_of_slot = [False]

            def mm(out, w, rhs, start, stop, done=None):
                ins = nc.tensor.matmul(out, w, rhs, start=start, stop=stop, skip_group_check=True)
                if first_of_slot[0]:
                    ins.then_inc(slot_used, 1)
                    first_of_slot[0] = False
                elif done is not None:
                    ins.then_inc(done, 1)

            def turned(out, rows, n, waits, done=None):
                if waits:
                    ins = nc.tensor.matmul(out, rows, ident[0:n, 0:n], start=True, stop=True)
                else:
                    ins = nc.tensor.transpose(out, rows, ident[0:n, 0:n])
                if done is not None:
                    ins.then_inc(done, 1)

            def take_slot(n, it=None, laps=1):
                if it is None:
                    pe.wait_ge(slot_in[n % R], 16 * (n // R + 1))
                else:
                    pe.wait_ge(slot_in[n % R], it * (16 * laps) + 16 * (n // R + 1))
                first_of_slot[0] = n > 0

            def begin(key, it=None):
                b, n = turn(key, it)
                if it is not None or n > 0:
                    pe.wait_ge(drained[b], n)
                return bank[b], filled[b]

            def rms(r):
                ps, full = begin(("rms", r))
                pe.wait_ge(squared, r + 1)
                for k in range(KT):
                    mm(ps[:, 0:T], ones, xn[:, k, :], k == 0, k == KT - 1, full if k == KT - 1 else None)

            def columns(key, n, m, src, it=None, k0=0, kn=KT):
                w = slot(n)
                ps, full = begin(key, it)
                for k in range(KT):
                    mm(ps[:, 0:T], w[:, k, m * P:(m + 1) * P], src[:, k, :], k == 0, k == KT - 1,
                       full if k == KT - 1 else None)

            def mod_rows(key, n, it=None, blocks=range(KT)):
                w = slot(n)
                b, _ = turn(key, it)
                ps, full = begin(key, it) if blocks[0] == 0 else (bank[b], filled[b])
                for k in blocks:
                    mm(ps[0:NC, 0:256], cs[:, k, :], w[:, k, :], k == 0, k == KT - 1,
                       full if k == KT - 1 else None)

            def mod_turn(key, buf, ps, tile, done=None, it=None):
                moved(pe, key, it)
                for m in range(2):
                    turned(ps[:, (tile + m) * NC:(tile + m + 1) * NC], mrow[0:NC, buf, m * P:(m + 1) * P], NC,
                           m == 0, done if m else None)

            pe.wait_ge(cond_ready, 1)

            def mod0_lap(it):
                for r in range(R):
                    pe.wait_ge(slot_in[r], it * 16 + 16)
                    first_of_slot[0] = not (isinstance(it, int) and r == 0)
                    mod_rows(("row0", r), r, it)
                    if r == 0 and isinstance(it, int):
                        pe.wait_ge(consts_in, 48)
                    if r == 0:
                        ps, full = begin("mod0", it)
                    else:
                        mod_turn(("row0", r - 1), (r - 1) % 2, ps, 2 * (r - 1), None, it)
                mod_turn(("row0", R - 1), (R - 1) % 2, ps, 2 * (R - 1), full, it)

            mod0_lap(0)
            with pe.Fori(1, 24 // R) as it:
                mod0_lap(it)

            rms(0)
            pe.wait_ge(h_ready, 1)
            mod1_ps, mod1_full = begin("mod1")

            def mod1_slot(i):
                take_slot(S_RET + 2 * i + 1)
                mod_rows(("row1", i), S_RET + 2 * i + 1)
                if i:
                    mod1_turn(i - 1)

            def mod1_turn(i):
                mod_turn(("row1", i), i % 2, mod1_ps, 2 * i, mod1_full if i == 23 else None)

            def values(key, skey, n, src, i):
                w = slot(n)
                for c in range(2):
                    ps, full = begin((key, i, c))
                    for k in range(KT):
                        mm(ps[:, 0:256], src[:, k, c * P:(c + 1) * P], w[:, k, :], k == 0, k == KT - 1,
                           full if k == KT - 1 else None)
                ps, full = begin((skey, i))
                for k in range(KT):
                    mm(ps[0:NS, 0:256], src[:, k, TP:T], w[:, k, :], k == 0, k == KT - 1,
                       full if k == KT - 1 else None)

            for i in range(8):
                take_slot(S_RET + 2 * i)
                for m in range(2):
                    columns(("qk", i, m), S_RET + 2 * i, m, h)
                mod1_slot(i)
            for i in range(8):
                take_slot(S_RET + 2 * (8 + i))
                values("v", "vs", S_RET + 2 * (8 + i), h, i)
                mod1_slot(8 + i)

            pe.wait_ge(past_ready, 1)
            lfv = past_lf.rearrange("p b g h -> p (b g h)")
            prev = past_pre.rearrange("p b g h -> p (b g h)")
            for i in range(2):
                ps, full = begin(("past", i))
                mm(ps[:], c_("upto")[:, 0:P], lfv[:, i * 512:(i + 1) * 512], True, False)
                mm(ps[:], ones, prev[:, i * 512:(i + 1) * 512], False, True, full)
            ps, full = begin("past_total")
            mm(ps[:, 0:NS * FH], ones, past_sum.rearrange("p b h -> p (b h)"), True, True, full)

            def head_scores(hd):
                for s in range(2):
                    moved(pe, ("qk", hd, s))
                    moved(pe, ("qk", 4 + hd, s))
                ps, full = begin(("ra", hd))
                for s in range(2):
                    mm(ps[:, 0:TP], qk[:, 8 + 2 * hd + s, 0:P], qk[:, 2 * hd + s, 0:TP], s == 0, s == 1)
                for s in range(2):
                    mm(ps[:, TP:TP + P], qk[:, 8 + 2 * hd + s, P:TP], qk[:, 2 * hd + s, P:TP], s == 0, s == 1,
                       full if s == 1 else None)
                ps, full = begin(("rk", hd))
                for c in range(2):
                    for s in range(2):
                        ins = nc.tensor.transpose(ps[:, (2 * c + s) * P:(2 * c + s + 1) * P],
                                                  qk[:, 8 + 2 * hd + s, c * P:(c + 1) * P], ident)
                ins.then_inc(full, 1)

            def head_output(hd):
                moved(pe, ("ra", hd))
                for c in range(2):
                    for i in (2 * hd, 2 * hd + 1):
                        moved(pe, ("v", i, c))
                sc = at_sb[:, hd % 2, :]
                for v in range(4):
                    ps, full = begin(("ro", hd, v))
                    col = slice(hd * RV + v * P, hd * RV + (v + 1) * P)
                    mm(ps[:, 0:TP], vtok[:, 0, col], sc[:, 0:TP], True, False)
                    mm(ps[:, P:TP], vtok[:, 1, col], sc[:, TP:TP + P], False, True, full)
                moved(pe, ("rk", hd))
                for s in range(2):
                    ps, full = begin(("rs", hd, s))
                    for c in range(2):
                        mm(ps[:], ktok[:, hd % 2, c, s * P:(s + 1) * P], vtok[:, c, hd * RV:(hd + 1) * RV], c == 0, c == 1,
                           full if c == 1 else None)

            head_scores(0)
            for hd in range(RH):
                if hd + 1 < RH:
                    head_scores(hd + 1)
                head_output(hd)

            def value_rows(u):
                hd, b = u // NS, u % NS
                ps, full = begin(("vb", u))
                mm(ps[:], bc(ident[0:NS, b:b + 1], [NS, P]), vrow[:, hd * RV:(hd + 1) * RV], True, True, full)

            for i in range(8):
                moved(pe, ("vs", i))
            pe.wait_ge(qz_ready, 1)

            def read_state(u):
                hd, b = u // NS, u % NS
                if b == 0:
                    begin(("os", hd))
                ps, full = bank[X1], filled[X1]
                moved(pe, ("vb", u))
                for s in range(2):
                    mm(ps[0:NS, :], qz[:, s, hd, b * NS:(b + 1) * NS], st[:, u % 4, s, :], b == 0 and s == 0,
                       b == NS - 1 and s == 1, None if s == 0 else full if b == NS - 1 else state_read)

            def outputs_turn(hd):
                moved(pe, ("os", hd))
                ps, full = begin(("osT", hd))
                for t in range(4):
                    ins = nc.tensor.transpose(ps[:, t * NS:(t + 1) * NS], osb[0:NS, t * P:(t + 1) * P],
                                              ident[0:NS, 0:NS])
                ins.then_inc(full, 1)

            for i in range(8):
                n = S_RET + 2 * (16 + i)
                value_rows(4 * i)
                take_slot(n)
                columns(("g", i, 0), n, 0, h)
                if i and i % 2 == 0:
                    outputs_turn(i // 2 - 1)
                read_state(4 * i)
                value_rows(4 * i + 1)
                columns(("g", i, 1), n, 1, h)
                read_state(4 * i + 1)
                value_rows(4 * i + 2)
                take_slot(n + 1)
                mod_rows(("row1", 16 + i), n + 1, None, range(0, 4))
                read_state(4 * i + 2)
                value_rows(4 * i + 3)
                mod_rows(("row1", 16 + i), n + 1, None, range(4, 8))
                mod1_turn(15 + i)
                read_state(4 * i + 3)
            mod1_turn(23)
            outputs_turn(RH - 1)

            for hd in range(RH):
                pe.wait_ge(o_squared, hd + 1)
                ps, full = begin(("gn", hd))
                for t in range(4):
                    mm(ps[:, 0:T], ones, qk[:, 4 * hd + t, :], t == 0, t == 3, full if t == 3 else None)

            pe.wait_ge(o_ready, RH)
            kv_ps, kv_full = begin("kvmod")
            for n in range(4):
                outs = []
                for half in range(2):
                    j = S_RO + 2 * (2 * n + half)
                    take_slot(j)
                    w = slot(j)
                    for m in range(2):
                        if half == 0:
                            outs.append(begin(("rout", n, m)))
                        ps, full = outs[m]
                        for k in range(KT):
                            mm(ps[:, 0:T], w[:, k, m * P:(m + 1) * P], oret[:, half * KT + k, :],
                               half == 0 and k == 0, half == 1 and k == KT - 1,
                               full if half == 1 and k == KT - 1 else None)
                    take_slot(j + 1)
                    i = 2 * n + half
                    mod_rows(("row2", i), j + 1)
                    if i:
                        mod_turn(("row2", i - 1), (i - 1) % 2, kv_ps, 2 * (i - 1))
            mod_turn(("row2", 7), 1, kv_ps, 14, kv_full)

            def moe(l, base):
                rms(1 + 2 * l)
                pe.wait_ge(h_ready, 2 + 3 * l)
                ps, full = begin(("logits", l))
                for k in range(KT):
                    mm(ps[0:36, 0:T], w_r[l][:, k, :], h[:, k, :], k == 0, k == KT - 1,
                       full if k == KT - 1 else None)
                moved(pe, ("logits", l))
                ps, full = begin(("logitsT", l))
                for c in range(3):
                    n = min(P, T - c * P)
                    ins = nc.tensor.transpose(ps[0:n, c * 36:(c + 1) * 36], lgT[:, c * P:c * P + n],
                                              ident[0:36, 0:36])
                ins.then_inc(full, 1)
                for c, n in enumerate(TROWS):
                    for i in range(2):
                        ps, full = begin(("ht", l, c, i))
                        for k in range(4):
                            ins = nc.tensor.transpose(ps[0:n, k * P:(k + 1) * P], h[:, 4 * i + k, c * P:c * P + n],
                                                      ident)
                        ins.then_inc(full, 1)
                pe.wait_ge(chosen_ready, l + 1)
                ps, full = begin(("count", l))
                for c, n in enumerate(TROWS):
                    mm(ps[0:NE, 0:P], chosen[0:n, 2, c, :], ones[0:n, :], c == 0, c == 2, full if c == 2 else None)
                moved(pe, ("count", l))
                ps, full = begin(("place", l))
                before = c_("before", NE)
                for c, n in enumerate(TROWS):
                    out = ps[0:n, c * NE:(c + 1) * NE]
                    for b in range(c):
                        mm(out, ones[:, 0:n], chosen[:, 2, b, :], b == 0, False)
                    mm(out, c_("upto", n)[:, 0:n], chosen[0:n, 2, c, :], c == 0, False)
                    mm(out, count_T[:, 0:n], before[:, 0:NE], False, True)
                mm(ps[:, 3 * NE:5 * NE], count_T, before, True, True, full)
                pe.wait_ge(pick_ready, l + 1)
                for c in range(3):
                    for i in range(2):
                        moved(pe, ("ht", l, c, i))
                for k in range(KT):
                    for i in range(2):
                        ps, full = begin(("sorted", l, k, i))
                        for c, n in enumerate(TROWS):
                            mm(ps[:, 0:T], h_tok[0:n, c, k * P:(k + 1) * P], pick[0:n, c, i * T:(i + 1) * T],
                               c == 0, c == 2, full if c == 2 else None)

                def turn_window(e, it):
                    ps, full = begin(("aT", l, e), it)
                    moved(pe, ("GU", l, e), it)
                    for m in range(2):
                        ins = nc.tensor.transpose(ps[:, m * P:(m + 1) * P], aff[:, e, m * P:(m + 1) * P], ident)
                    ins.then_inc(full, 1)

                with pe.Fori(0, NE // 2) as it:
                    for e in range(2):
                        ps, full = begin(("GU", l, e), it)
                        pe.wait_ge(xw_ready, it * 2 + (l * (NE + 2) + e + 1))
                        for j in range(2):
                            n = base + 2 * e + j
                            take_slot(n, it)
                            w = slot(n, 4)
                            for k in range(4):
                                mm(ps[:], xw[:, e, 4 * j + k, :], w[:, k, :], j + k == 0, j * k == 3,
                                   full if j * k == 3 else None)
                            if e == 1 and j == 0:
                                turn_window(0, it)
                    for e in range(2):
                        n = base + 4 + e
                        take_slot(n, it)
                        w = slot(n, 2)
                        moved(pe, ("aT", l, e), it)
                        for i in range(2):
                            ps, full = begin(("Y", l, e, i), it)
                            for q in range(2):
                                mm(ps[:], aff_T[:, e, q, :], w[:, q, i * 512:(i + 1) * 512], q == 0, q == 1,
                                   full if q else None)
                            if e == 0 and i == 0:
                                turn_window(1, it)
                with pe.If(further(pe, l) > 0):
                    for key in (("GU", l, 0), ("aT", l, 0), ("Y", l, 0, 0), ("Y", l, 0, 1)):
                        moved(pe, key, NE // 2 - 1)
                    with pe.Fori(0, XW) as i:
                        pe.wait_ge(far_moved[l], i * 4 + 1)
                        pe.wait_ge(far_in[l], i * 48 + 32)
                        for k in range(KT):
                            w = far_w[k // 4].rearrange("p (k c) -> p k c", k=4)
                            mm(bank[0][:], xw[:, 0, k, :], w[:, k % 4, :], k == 0, k == KT - 1,
                               far_product[l] if k == KT - 1 else None)
                        pe.wait_ge(far_moved[l], i * 4 + 2)
                        for m in range(2):
                            ins = nc.tensor.transpose(bank[2][:, m * P:(m + 1) * P], aff[:, 0, m * P:(m + 1) * P], ident)
                        ins.then_inc(far_product[l], 1)
                        pe.wait_ge(far_moved[l], i * 4 + 3)
                        pe.wait_ge(far_in[l], i * 48 + 48)
                        w = far_w[0].rearrange("p (k c) -> p k c", k=2)
                        for n in range(2):
                            for q in range(2):
                                mm(bank[4 + n][:], aff_T[:, 0, q, :], w[:, q, n * 512:(n + 1) * 512], q == 0, q == 1,
                                   far_product[l] if n * q else None)
                    pe.wait_ge(far_moved[l], 4 * XW)
                pe.wait_ge(pick_g_ready, l + 1)
                for s, rows in enumerate(PROWS):
                    ps, full = begin(("gT", l, s))
                    for c, n in enumerate(TROWS):
                        ins = nc.tensor.transpose(ps[0:rows, c * P:c * P + n], pick_g[0:n, c, s * P:s * P + rows],
                                                  ident[0:n, 0:n])
                    ins.then_inc(full, 1)
                for s in range(PC):
                    moved(pe, ("gT", l, s))
                outs = [begin(("sum", l, k)) for k in range(KT)]
                for s, rows in enumerate(PROWS):
                    pe.wait_ge(y_in[s], 16 * (l + 1))
                    for k in range(KT):
                        ps, full = outs[k]
                        mm(ps[:, 0:T], y_sorted[0:rows, s, k * P:(k + 1) * P], pick_gT[0:rows, s, :], s == 0,
                           s == PC - 1, full if s == PC - 1 else None)

            moe(0, S_MOE0)

            rms(2)
            pe.wait_ge(h_ready, 3)
            ps, full = begin("flogit")
            for k in range(KT):
                mm(ps[0:FH, 0:T], w_f[:, k, :], n2[:, k, :], k == 0, k == KT - 1, full if k == KT - 1 else None)
            for i in range(4):
                take_slot(S_KV + i)
                for m in range(2):
                    columns(("fk", i, m), S_KV + i, m, n2)
            pe.wait_ge(logf_ready, 1)
            ps, full = begin("logfT")
            for c in range(2):
                ins = nc.tensor.transpose(ps[:, c * FH:(c + 1) * FH], fz[:, 1, c * P:(c + 1) * P], ident[0:FH, 0:FH])
            ins.then_inc(full, 1)
            for i in range(4):
                take_slot(S_KV + 4 + i)
                if i == 0:
                    moved(pe, "logfT")
                    ps, full = begin("F")
                    nc.tensor.matmul(ps[0:FH, 0:TP], lf_tok[:, 0, :], c_("upto"), start=True, stop=False,
                                     skip_group_check=True)
                    nc.tensor.matmul(ps[0:FH, P:TP], lf_tok[:, 1, :], c_("upto")[:, 0:P], start=False, stop=True,
                                     skip_group_check=True).then_inc(full, 1)
                values("fv", "fvs", S_KV + 4 + i, n2, i)
            pe.wait_ge(h_ready, 4)
            for i in range(4):
                take_slot(S_FQ + i)
                for m in range(2):
                    columns(("fq", i, m), S_FQ + i, m, h)
            pe.wait_ge(diag_ready, 1)
            ps, full = begin("own_F")
            mm(ps[:, 0:NS * FH], ones[0:FH, :], lf_diag.rearrange("p b h -> p (b h)"), True, True, full)
            pe.wait_ge(own_ready, 1)
            ps, full = begin("own_score")
            for r, name in enumerate(("half0", "half1")):
                mm(ps[:, r * 64:(r + 1) * 64], c_(name), own.rearrange("p t b -> p (t b)"), True, True,
                   full if r else None)
            for i in range(4):
                moved(pe, ("fvs", i))
            ps, full = begin("fvsT")
            for t in range(KT):
                ins = nc.tensor.transpose(ps[:, t * NS:(t + 1) * NS], q_one[:, t * P:(t + 1) * P],
                                          ident[0:NS, 0:NS])
            ins.then_inc(full, 1)
            for i in range(2):
                ps, full = begin(("qrow", i))
                for t in range(4):
                    ins = nc.tensor.transpose(ps[0:NS, t * P:(t + 1) * P], fq[:, 4 * i + t, TP:T], ident)
                ins.then_inc(full, 1)

            def query_everywhere(tag, b, it=None):
                pe.wait_ge(one_ready, b + 1)
                for i in range(2):
                    ps, full = begin(("qb", i, tag), it)
                    mm(ps[:], ones[0:NS, :], q_one[:, i * 512:(i + 1) * 512], True, True, full)

            query_everywhere("pre", 0)

            def window(tag, b, it=None):
                def value_page(j):
                    if tag == "first":
                        return
                    if j == 0:
                        pe.wait_ge(pd_ready, b)
                        begin(("pv", 0, tag), it)
                        begin(("pv", 1, tag), it)
                    pe.wait_ge(v_in[j % 4], b * 32 + (16 * (j // 4 + 1) - 32))
                    for i in range(2):
                        bk = at[("pv", i, tag)][0]
                        mm(bank[bk][0:FH, :], pD[:, j * FH:(j + 1) * FH], vpg[:, j % 4, i * 512:(i + 1) * 512],
                           j == 0, j == NPG - 1, filled[bk] if j == NPG - 1 else v_used if i else None)

                def head_scores(hh):
                    if tag == "last":
                        return
                    pe.wait_ge(staged, b * 3 + 3)
                    pe.wait_ge(negF_ready, b + 1)
                    rows = slice(64 * hh, 64 * hh + 64)
                    ps, full = begin(("ps", hh, tag), it)
                    for c in range(2):
                        cols = slice(0, P) if c == 0 else slice(P, 3 * P)
                        keys = slice(0, (c + 1) * P)
                        mm(ps[:, cols], q_st[rows, c * P:(c + 1) * P], k_st[rows, keys], True, False)
                        mm(ps[:, cols], ones[0:FH, :], negF[:, hh, keys], False, True, full if c else None)

                def head_turn(hh):
                    if tag == "last":
                        return
                    ps, full = begin(("pT", hh, tag), it)
                    pe.wait_ge(p_ready, b * 2 + (hh + 1))
                    for i in range(3):
                        ins = nc.tensor.transpose(ps[:, i * P:(i + 1) * P], p_sb[:, hh, i * P:(i + 1) * P], ident)
                    ins.then_inc(full, 1)

                def head_values(hh):
                    if tag == "last":
                        return
                    moved(pe, ("pT", hh, tag), it)
                    ps, full = begin(("po", hh, tag), it)
                    rows = slice(64 * hh, 64 * hh + 64)
                    mm(ps[rows, 0:TP], v_st[:, 0, rows], pT_sb[:, hh, 0:TP], True, False)
                    mm(ps[rows, P:TP], v_st[:, 1, rows], pT_sb[:, hh, TP:3 * P], False, True, full)

                value_page(0)
                head_scores(0)
                value_page(1)
                head_scores(1)
                value_page(2)
                value_page(3)
                head_turn(0)
                value_page(4)
                head_turn(1)
                head_values(0)
                value_page(5)
                head_values(1)
                value_page(6)
                value_page(7)
                if tag != "last":
                    query_everywhere(tag, b + 1, it)
                    ps, full = begin(("mxT", tag), it)
                    pe.wait_ge(mxp_ready, b + 1)
                    nc.tensor.transpose(ps[0:FH, 0:P], mxp, ident).then_inc(full, 1)
                    pe.wait_ge(mxd_ready, b + 1)
                    ps, full = begin(("mxb", tag), it)
                    mm(ps[:, 0:FH], ones[0:FH, :], mxd, True, True, full)
                    pe.wait_ge(psm_ready, b + 1)
                    ps, full = begin(("den", tag), it)
                    mm(ps[:, 0:FH], ones, psm, True, True, full)
                if tag != "first":
                    moved(pe, ("pv", 0, tag), it)
                    moved(pe, ("pv", 1, tag), it)
                    ps, full = begin(("oT", tag), it)
                    for t in range(KT):
                        turned(ps[:, t * FH:(t + 1) * FH], o_row[:, t * P:(t + 1) * P], FH, t == 0,
                               full if t == KT - 1 else None)

            window("first", 0)
            with pe.Fori(0, NS - 2) as it:
                window("mid", it + 1, it)
            window("end", NS - 1)
            window("last", NS)

            pe.wait_ge(sample_done, NS)
            for hh in range(2):
                moved(pe, ("po", hh, "end"))
            for n in range(4):
                take_slot(S_FO + n)
                for m in range(2):
                    columns(("fout", n, m), S_FO + n, m, fo)
            moe(1, S_MOE1)
            rms(4)

        @block.scalar
        def _(act):
            def copy(out, in_, scale=None):
                if scale is None:
                    return nc.scalar.activation(out, in_, ACT.Copy)
                return nc.scalar.activation(out, in_, ACT.Copy, scale=scale)

            act.wait_ge(cond_in, 16)
            nc.scalar.activation(cs[:], cs[:], ACT.Silu).then_inc(cond_ready, 1)
            act.wait_ge(consts_in, 48)
            eps = c_("eps")

            def mod_rows(key, buf, it=None):
                ps = result(act, key, it)
                copy(mrow[0:NC, buf, :], ps[0:NC, 0:256]).then_inc(free(key), 1)

            with act.Fori(0, 24 // R) as it:
                for r in range(R):
                    mod_rows(("row0", r), r % 2, it)

            def rms(r):
                if r == 0:
                    act.wait_ge(x_loaded, 16)
                else:
                    act.wait_ge(x_ready, r)
                nc.scalar.activation(xn[:], x[:], ACT.Square).then_inc(squared, 1)
                ps = result(act, ("rms", r))
                nc.scalar.activation(root[:], ps[:, 0:T], ACT.Sqrt, bias=eps, scale=1.0 / D) \
                    .then_inc(free(("rms", r)), 1)

            rms(0)
            for i in range(8):
                mod_rows(("row1", i), i % 2)
            for i in range(8):
                for c in range(2):
                    ps = result(act, ("v", i, c))
                    copy(vtok[:, c, i * 256:(i + 1) * 256], ps[:, 0:256]).then_inc(free(("v", i, c)), 1)
                mod_rows(("row1", 8 + i), i % 2)
            for hd in range(RH):
                for v in range(4):
                    ps = result(act, ("ro", hd, v))
                    copy(oret[:, 4 * hd + v, 0:TP], ps[:, 0:TP]).then_inc(free(("ro", hd, v)), 1)
                if hd:
                    act.wait_ge(sp_stored, 16 * hd)
                for s in range(2):
                    ps = result(act, ("rs", hd, s))
                    copy(sp_sb[:, s, :], ps[:]).then_inc(free(("rs", hd, s)), 1)
                moved(act, ("rs", hd, 1))
                act.dma_start(sp_out[hd], sp_sb).then_inc(sp_stored, 16)

            def scale_state(u):
                act.wait_ge(state_in[u % 4], 16 * (u // 4 + 1))
                copy(st[:, u % 4, :, :], st[:, u % 4, :, :], GAMMA[u // NS]).then_inc(state_scaled, 1)

            for i in range(8):
                for m in range(2):
                    scale_state(4 * i + 2 * m)
                    scale_state(4 * i + 2 * m + 1)
                    ps = result(act, ("g", i, m))
                    nc.scalar.activation(gsil[:, 2 * i + m, :], ps[:, 0:T], ACT.Silu) \
                        .then_inc(free(("g", i, m)), 1)
                mod_rows(("row1", 16 + i), i % 2)
                if i % 2:
                    ps = result(act, ("os", i // 2))
                    copy(osb[0:NS, :], ps[0:NS, :]).then_inc(free(("os", i // 2)), 1)
            moved(act, ("osT", RH - 1))
            moved(act, ("ro", RH - 1, 3))
            for hd in range(RH):
                nc.scalar.activation(qk[:, 4 * hd:4 * hd + 4, :], oret[:, 4 * hd:4 * hd + 4, :], ACT.Square) \
                    .then_inc(o_squared, 1)
            for hd in range(RH):
                ps = result(act, ("gn", hd))
                nc.scalar.activation(rot[:, hd, :], ps[:, 0:T], ACT.Sqrt, bias=eps, scale=1.0 / RV) \
                    .then_inc(free(("gn", hd)), 1)

            for i in range(8):
                mod_rows(("row2", i), i % 2)

            def moe(l):
                rms(1 + 2 * l)
                ps = result(act, ("logits", l))
                copy(lgT, ps[0:36, 0:T]).then_inc(free(("logits", l)), 1)
                for c, n in enumerate(TROWS):
                    for i in range(2):
                        ps = result(act, ("ht", l, c, i))
                        copy(h_tok[0:n, c, i * 512:(i + 1) * 512], ps[0:n, :]).then_inc(free(("ht", l, c, i)), 1)
                ps = result(act, ("count", l))
                copy(count_T, ps[0:NE, 0:P]).then_inc(free(("count", l)), 1)
                act.wait_ge(route_x, l + 1)
                nc.scalar.activation(r4[:, 4, :, :], r4[:, 0, :, :], ACT.Exp)
                nc.scalar.activation(r1[:, 7, :], r1[:, 6, :], ACT.Exp).then_inc(route_e, 1)
                for k in range(KT):
                    for i in range(2):
                        ps = result(act, ("sorted", l, k, i))
                        copy(x_sorted[:, k, i * T:(i + 1) * T], ps[:, 0:T]).then_inc(free(("sorted", l, k, i)), 1)

                def half_out(e, it):
                    ps = result(act, ("Y", l, e, 0), it)
                    act.wait_ge(y_stored[e], it * 16 + 16 * l * (NE // 2))
                    copy(y_sb[:, e, 0:512], ps[:]).then_inc(free(("Y", l, e, 0)), 1)

                def window_turned(e, it):
                    ps = result(act, ("aT", l, e), it)
                    copy(aff_T[:, e, :, :], ps[:, 0:2 * P].rearrange("p (m n) -> p m n", m=2)) \
                        .then_inc(free(("aT", l, e)), 1)

                with act.Fori(0, NE // 2) as it:
                    for e in range(2):
                        ps = result(act, ("GU", l, e), it)
                        nc.scalar.activation(act_g[:, e, :], ps[:, 0:FF], ACT.Silu).then_inc(silu_ready, 1)
                        if e == 0:
                            window_turned(0, it)
                    half_out(0, it)
                    window_turned(1, it)
                    half_out(1, it)
                with act.If(further(act, l) > 0):
                    with act.Fori(0, XW) as i:
                        act.wait_ge(far_product[l], i * 3 + 1)
                        nc.scalar.activation(act_g[:, 0, :], bank[0][:, 0:FF], ACT.Silu).then_inc(far_silu[l], 1)
                for s, rows in enumerate(PROWS):
                    ps = result(act, ("gT", l, s))
                    copy(pick_gT[0:rows, s, :], ps[0:rows, 0:T]).then_inc(free(("gT", l, s)), 1)

            moe(0)

            rms(2)
            act.wait_ge(f_neg, 1)
            nc.scalar.activation(fz[:, 2, :], fz[:, 1, :], ACT.Exp).then_inc(f_exp, 1)
            act.wait_ge(f_exp, 1)
            nc.scalar.activation(fz[:, 3, :], fz[:, 2, :], ACT.Ln, bias=1.0).then_inc(f_exp, 1)
            for i in range(4):
                for m in range(2):
                    ps = result(act, ("fk", i, m))
                    copy(fk[:, 2 * i + m, :], ps[:, 0:T]).then_inc(free(("fk", i, m)), 1)
            act.wait_ge(logf_ready, 1)
            act.dma_start(lf_out, fz[:, 1, :]).then_inc(lf_stored, 16)
            moved(act, ("fk", 3, 0))
            moved(act, ("fk", 3, 1))
            act.dma_start(k_out, fk).then_inc(stored, 16)
            for i in range(4):
                for c in range(2):
                    ps = result(act, ("fv", i, c))
                    copy(fv[:, c, i * 256:(i + 1) * 256], ps[:, 0:256]).then_inc(free(("fv", i, c)), 1)
            moved(act, ("fv", 3, 0))
            moved(act, ("fv", 3, 1))
            act.dma_start(vp_out, fv).then_inc(stored, 16)
            moved(act, ("fvs", 2))
            moved(act, ("fvs", 3))
            act.dma_start(vs_out, q_one).then_inc(vs_stored, 16)
            for i in range(4):
                for m in range(2):
                    ps = result(act, ("fq", i, m))
                    copy(fq[:, 2 * i + m, :], ps[:, 0:T], HD ** -0.5).then_inc(free(("fq", i, m)), 1)
            moved(act, ("fq", 3, 0))
            moved(act, ("fq", 3, 1))

            def query_everywhere(tag, it=None):
                for i in range(2):
                    ps = result(act, ("qb", i, tag), it)
                    copy(qb[:, i * 512:(i + 1) * 512], ps[:]).then_inc(free(("qb", i, tag)), 1)

            query_everywhere("pre")

            def window(tag, b, it=None):
                if tag != "last":
                    copy(q_st, fq[:, ds(b, 1), 0:TP].rearrange("p a n -> p (a n)")).then_inc(staged, 1)
                    copy(k_st, fk[:, ds(b, 1), 0:TP].rearrange("p a n -> p (a n)")).then_inc(staged, 1)
                    copy(v_st, fv[:, :, ds(b * P, P)]).then_inc(staged, 1)
                    for hh in range(2):
                        act.wait_ge(neg_max, b * 2 + (hh + 1))
                        nc.scalar.activation(p_sb[:, hh, 0:P], s_sb[:, hh, 0:P], ACT.Exp, bias=hneg[:, hh, 0:1],
                                             accum_out=hsum[:, hh, 0:1])
                        nc.scalar.activation(p_sb[:, hh, P:3 * P], s_sb[:, hh, P:3 * P], ACT.Exp,
                                             bias=hneg[:, hh, 1:2], accum_out=hsum[:, hh, 1:2]).then_inc(p_raw, 1)
                    for hh in range(2):
                        ps = result(act, ("pT", hh, tag), it)
                        copy(pT_sb[:, hh, :], ps[:, 0:3 * P]).then_inc(free(("pT", hh, tag)), 1)
                    for hh in range(2):
                        rows = slice(64 * hh, 64 * hh + 64)
                        ps = result(act, ("po", hh, tag), it)
                        copy(fo[rows, ds(b, 1), 0:TP].rearrange("p a n -> p (a n)"), ps[rows, 0:TP]) \
                            .then_inc(free(("po", hh, tag)), 1)
                if tag != "last":
                    act.wait_ge(k_used, b * NPG + NPG)
                    query_everywhere(tag, it)
                    act.wait_ge(shifted, b + 1)
                    nc.scalar.activation(pE, sF, ACT.Exp)
                    nc.scalar.activation(pO, sO, ACT.Exp).then_inc(pE_ready, 1)
                if tag != "first":
                    for i in range(2):
                        ps = result(act, ("pv", i, tag), it)
                        copy(o_row[:, i * 512:(i + 1) * 512], ps[0:FH, :]).then_inc(free(("pv", i, tag)), 1)
                if tag != "last":
                    act.wait_ge(pE_ready, b + 1)
                    copy(pD, pE).then_inc(pd_ready, 1)

            window("first", 0)
            with act.Fori(0, NS - 2) as it:
                window("mid", it + 1, it)
            window("end", NS - 1)
            window("last", NS)

            moe(1)
            rms(4)
            act.wait_ge(h_ready, 6)
            act.dma_start(y_out, h[:]).then_inc(stored, 16)
            act.wait_ge(stored, 16 * 3)
            act.wait_ge(lf_stored, 16)

        @block.vector
        def _(dve):
            own_steps = Steps(dve, dve_steps)
            step, wait = own_steps.step, own_steps.wait
            tt, stt, tsc = nc.vector.tensor_tensor, nc.vector.scalar_tensor_tensor, nc.vector.tensor_scalar

            dve.wait_ge(consts_in, 48)
            def add_bias(key, out, tiles, v0):
                ps = result(dve, key)
                tt(out, ps[:, 0:tiles * NC].rearrange("p (t c) -> p t c", c=NC),
                   bc(vec[:, v0:v0 + tiles].unsqueeze(2), [P, tiles, NC]), ALU.add).then_inc(free(key), 1)

            with dve.Fori(0, 24 // R) as it:
                ps = result(dve, "mod0", it)
                tiles = 2 * R
                tt(mod[0][:, ds(it * tiles, tiles), :], ps[:, 0:tiles * NC].rearrange("p (t c) -> p t c", c=NC),
                   bc(vec[:, ds(it * tiles, tiles)].unsqueeze(2), [P, tiles, NC]), ALU.add) \
                    .then_inc(free("mod0"), 1)

            def normalise(r):
                moved(dve, ("rms", r))
                step(nc.vector.reciprocal(rstd[:], root[:]))
                wait()
                step(tt(xn[:], x[:], bc(rstd[:].unsqueeze(1), [P, KT, T]), ALU.mult))

            def modulate(out, cf, g, table, shift, scale):
                sh, sc = table[:, 8 * shift:8 * shift + 8, :], table[:, 8 * scale:8 * scale + 8, :]
                step(stt(cf[:], sc, 1.0, bc(gain[g].unsqueeze(2), [P, KT, NC]), ALU.add, ALU.mult))
                wait()
                step(tt(out[:, :, TP:T], xn[:, :, TP:T], cf[:, :, 1:NC], ALU.mult))
                for k in range(KT):
                    tsc(out[:, k, 0:TP], xn[:, k, 0:TP], cf[:, k, 0:1], sh[:, k, 0:1], ALU.mult, ALU.add)
                wait()
                tt(out[:, :, TP:T], out[:, :, TP:T], sh[:, :, 1:NC], ALU.add).then_inc(h_ready, 1)

            moved(dve, "mod0", 24 // R - 1)
            normalise(0)
            modulate(h, coef, G_MIX0, mod[0], SH1, SC1)

            for i in range(8):
                cos, sin = (c_("cosq"), c_("sinq")) if i < 4 else (c_("cosk"), c_("sink"))
                ps0 = result(dve, ("qk", i, 0))
                ps1 = result(dve, ("qk", i, 1))
                if i:
                    moved(dve, ("qk", i - 1, 0))
                    moved(dve, ("qk", i - 1, 1))
                step(tt(rot[:, 0, :], ps0[:, 0:T], cos, ALU.mult))
                step(tt(rot[:, 1, :], ps1[:, 0:T], sin, ALU.mult))
                step(tt(rot[:, 2, :], ps0[:, 0:T], sin, ALU.mult))
                step(tt(rot[:, 3, :], ps1[:, 0:T], cos, ALU.mult))
                wait()
                tt(qk[:, 2 * i, :], rot[:, 0, :], rot[:, 1, :], ALU.subtract).then_inc(free(("qk", i, 0)), 1)
                tt(qk[:, 2 * i + 1, :], rot[:, 2, :], rot[:, 3, :], ALU.add).then_inc(free(("qk", i, 1)), 1)
            for i in range(8):
                ps = result(dve, ("vs", i))
                nc.vector.tensor_copy(vrow[:, i * 256:(i + 1) * 256], ps[0:NS, 0:256]) \
                    .then_inc(free(("vs", i)), 1)
            step(nc.vector.memset(past_pre[:, :, 0, :], 0.0))
            dve.wait_ge(lf_in, 16 * NPAGES)
            for g in range(1, NPG):
                wait()
                step(tt(past_pre[:, :, g, :], past_pre[:, :, g - 1, :], past_lf[:, :, g - 1, :], ALU.add))
            wait()
            tt(past_sum, past_pre[:, :, NPG - 1, :], past_lf[:, :, NPG - 1, :], ALU.add).then_inc(past_ready, 1)
            flat_F = past_F[:, :, :].rearrange("p b c -> p (b c)")
            for i in range(2):
                ps = result(dve, ("past", i))
                nc.vector.tensor_copy(flat_F[:, i * 512:(i + 1) * 512], ps[:]).then_inc(free(("past", i)), 1)
            ps = result(dve, "past_total")
            nc.vector.tensor_copy(past_tot[:], ps[:, 0:NS * FH]).then_inc(free("past_total"), 1)
            step(nc.vector.memset(qz, 0.0))
            wait()
            for hd in range(RH):
                for s in range(2):
                    ins = nc.vector.tensor_copy(qz[:, s, hd, 0:NS * NS:NS + 1], qk[:, 2 * hd + s, TP:T])
            ins.then_inc(qz_ready, 1)
            for hd in range(RH):
                ps = result(dve, ("ra", hd))
                dec = c_("decay")[:, hd * TP:(hd + 1) * TP]
                tt(at_sb[:, hd % 2, 0:TP], ps[:, 0:TP], dec, ALU.mult)
                tt(at_sb[:, hd % 2, TP:TP + P], ps[:, TP:TP + P], dec[:, 0:P], ALU.mult) \
                    .then_inc(free(("ra", hd)), 1)
                ps = result(dve, ("rk", hd))
                for c in range(2):
                    kd = c_("kdec")[:, c * RH + hd:c * RH + hd + 1]
                    ins = tsc(ktok[:, hd % 2, c, :], ps[:, c * RK:(c + 1) * RK], kd, None, ALU.mult)
                ins.then_inc(free(("rk", hd)), 1)
            def samples_out(hd):
                ps = result(dve, ("osT", hd))
                nc.vector.tensor_copy(oret[:, 4 * hd:4 * hd + 4, TP:T],
                                      ps[:, 0:4 * NS].rearrange("p (t b) -> p t b", b=NS)) \
                    .then_inc(free(("osT", hd)), 1)

            for u in range(NS * RH):
                hd, b = u // NS, u % NS
                if hd and b == 1:
                    samples_out(hd - 1)
                ps = result(dve, ("vb", u))
                dve.wait_ge(state_scaled, u + 1)
                for s in range(2):
                    ins = stt(st[:, u % 4, s, :], ps[:], qk[:, 8 + 2 * hd + s, TP + b:TP + b + 1],
                              st[:, u % 4, s, :], ALU.mult, ALU.add)
                ins.then_inc(free(("vb", u)), 1)
            samples_out(RH - 1)
            add_bias("mod1", mod[1][:], 48, V_BMOD + 48)
            moved(dve, ("g", 7, 0))
            moved(dve, ("g", 7, 1))
            for hd in range(RH):
                tiles = slice(4 * hd, 4 * hd + 4)
                moved(dve, ("gn", hd))
                step(nc.vector.reciprocal(rot[:, hd, :], rot[:, hd, :]))
                wait()
                step(tt(oret[:, tiles, :], oret[:, tiles, :], bc(rot[:, hd:hd + 1, :], [P, 4, T]), ALU.mult))
                wait()
                tt(oret[:, tiles, :], oret[:, tiles, :], gsil[:, tiles, :], ALU.mult).then_inc(o_ready, 1)

            def residual(name, gate):
                for n in range(4):
                    for m in range(2):
                        t = 2 * n + m
                        ps = result(dve, (name, n, m))
                        stt(x[:, t, 0:TP], ps[:, 0:TP], gate[:, t, 0:1], x[:, t, 0:TP], ALU.mult, ALU.add)
                        tt(ms[:, t, :], ps[:, TP:T], gate[:, t, 1:NC], ALU.mult).then_inc(free((name, n, m)), 1)
                moved(dve, (name, 3, 0))
                moved(dve, (name, 3, 1))
                tt(x[:, :, TP:T], x[:, :, TP:T], ms[:], ALU.add).then_inc(x_ready, 1)

            residual("rout", mod[0][:, 8 * GT1:8 * GT1 + 8, :])
            add_bias("kvmod", kvmod[:], 16, V_BKV)

            def first_max(v, most, is_max, weight, first, best):
                n = v.shape[2]
                step(nc.vector.tensor_reduce(best[0], v, AX, ALU.max))
                wait()
                step(tt(is_max, v, bc(best[0].unsqueeze(2), [P, 3, n]), ALU.is_equal))
                wait()
                step(tt(weight, is_max, bc(first.unsqueeze(1), [P, 3, n]), ALU.mult))
                wait()
                step(nc.vector.tensor_reduce(best[1], weight, AX, ALU.max))
                wait()
                step(tt(most, weight, bc(best[1].unsqueeze(2), [P, 3, n]), ALU.is_equal))
                wait()

            def moe(l):
                normalise(1 + 2 * l)
                if l == 1:
                    dve.wait_ge(stored, 32)
                    dve.wait_ge(lf_stored, 16)
                step(nc.vector.memset(lg, 0.0))
                step(nc.vector.memset(place, 0.0))
                step(nc.vector.memset(x_sorted[:, :, PICKS:], 0.0))
                modulate(h, coef, G_FFN0 + l, mod[l], SH2, SC2)
                ps = result(dve, ("logitsT", l))
                nc.vector.tensor_copy(lg[:, 0:2, :], ps[:, 0:72].rearrange("p (c n) -> p c n", c=2))
                nc.vector.tensor_copy(lg[0:NS, 2, :], ps[0:NS, 72:108]).then_inc(free(("logitsT", l)), 1)
                moved(dve, ("logitsT", l))
                grp = lg[:, :, 0:NG]
                le = lg[:, :, NG:36]
                group = r4[:, 3, :, :]
                first_max(grp, group, r4[:, 1, :, :], r4[:, 2, :, :], c_("first4"), (r1[:, 0, :], r1[:, 1, :]))
                step(tt(r4[:, 0, :, :], grp, bc(r1[:, 0, :].unsqueeze(2), [P, 3, NG]), ALU.subtract))
                for c in range(3):
                    step(tt(le4[:, c, :, :], le[:, c, :].rearrange("p (g e) -> p e g", g=NG),
                            bc(group[:, c:c + 1, :], [P, EG, NG]), ALU.mult))
                wait()
                sel = r8[:, 0, :, :]
                step(nc.vector.tensor_reduce(sel, le4, AX, ALU.add))
                wait()
                one, two = r8[:, 3, :, :], r8[:, 7, :, :]
                first_max(sel, one, r8[:, 1, :, :], r8[:, 2, :, :], c_("first8"), (r1[:, 2, :], r1[:, 3, :]))
                step(stt(r8[:, 4, :, :], one, NEG, sel, ALU.mult, ALU.add))
                wait()
                first_max(r8[:, 4, :, :], two, r8[:, 5, :, :], r8[:, 6, :, :], c_("first8"),
                          (r1[:, 4, :], r1[:, 5, :]))
                tt(r1[:, 6, :], r1[:, 4, :], r1[:, 2, :], ALU.subtract).then_inc(route_x, 1)
                for i, choice in enumerate((one, two)):
                    for c in range(3):
                        step(tt(chosen[:, i, c, :].rearrange("p (g e) -> p g e", g=NG),
                                bc(group[:, c, :].unsqueeze(2), [P, NG, EG]),
                                bc(choice[:, c:c + 1, :], [P, NG, EG]), ALU.mult))
                wait()
                tt(chosen[:, 2, :, :], chosen[:, 0, :, :], chosen[:, 1, :, :], ALU.add).then_inc(chosen_ready, 1)
                ps = result(dve, ("place", l))
                step(nc.vector.tensor_copy(place[:, 0:2, :], ps[:, 0:2 * NE].rearrange("p (c n) -> p c n", c=2)))
                step(nc.vector.tensor_copy(place[0:NS, 2, :], ps[0:NS, 2 * NE:3 * NE]))
                nc.vector.tensor_copy(first_n, ps[0:1, 3 * NE:5 * NE]).then_inc(free(("place", l)), 1)
                moved(dve, ("place", l))
                for i in range(2):
                    step(tt(where[:, i, :, :], chosen[:, i, :, :], place, ALU.mult))
                wait()
                step(nc.vector.tensor_reduce(place_of, where, AX, ALU.add))
                wait()
                for c, n in enumerate(TROWS):
                    step(tsc(pick[0:n, c, :], c_("place", n), place_of[0:n, 0, c:c + 1], None, ALU.is_equal))
                wait()
                for c, n in enumerate(TROWS):
                    ins = stt(pick[0:n, c, :], c_("place", n), place_of[0:n, 1, c:c + 1], pick[0:n, c, :],
                              ALU.is_equal, ALU.add)
                ins.then_inc(pick_ready, 1)

                first, number = first_n[:, 0:NE], first_n[:, NE:2 * NE]
                step(tsc(over[:, 0:NE], number, WIN + 0.5, None, ALU.is_gt))
                step(tsc(over[:, NE:2 * NE], number, 2 * WIN + 0.5, None, ALU.is_gt))
                step(tt(rest[:, 0:NE], first, number, ALU.add))
                step(tsc(rest[:, NE:2 * NE], first, 2.0 * WIN, None, ALU.add))
                step(nc.vector.tensor_copy(starts[:, 0:NE], first))
                wait()
                step(tsc(rest, rest, -1.0, float(PICKS + WIN), ALU.mult, ALU.add))
                for i in range(2):
                    step(tt(keys[:, 1 + i, :], over, c_("back", 1)[:, i * 2 * NE:(i + 1) * 2 * NE], ALU.mult))
                wait()
                step(tt(keys[:, 0, :], over, rest, ALU.mult))
                wait()
                for i in range(3):
                    step(nc.vector.max(top[:, i, :], keys[:, i, :]))
                wait()
                step(tsc(starts[:, NE:NW], top[:, 0, 0:XW], -1.0, float(PICKS), ALU.mult, ALU.add))
                step(tsc(extra[:, 0:XW], top[:, 1, 0:XW], -1.0, float(GU_LAST), ALU.mult, ALU.add))
                step(tsc(extra[:, XW:2 * XW], top[:, 2, 0:XW], -1.0, float(DN_LAST), ALU.mult, ALU.add))
                step(nc.vector.tensor_copy(extra[:, 2 * XW:2 * XW + 1], top[:, 0, 0:1]))
                wait()
                step(nc.vector.tensor_copy(extra_ids[:], extra))
                nc.vector.tensor_copy(start_ids[:], starts).then_inc(windows_ready, 1)
                dve.wait_ge(route_e, l + 1)
                step(nc.vector.tensor_reduce(r1[:, 0, :], r4[:, 4, :, :], AX, ALU.add))
                wait()
                step(stt(r1[:, 1, :], r1[:, 7, :], 1.0, r1[:, 0, :], ALU.add, ALU.mult))
                wait()
                step(nc.vector.reciprocal(r1[:, 2, :], r1[:, 1, :]))
                wait()
                step(tt(r1[:, 3, :], r1[:, 2, :], r1[:, 7, :], ALU.mult))
                wait()
                for i in range(2):
                    result(dve, ("sorted", l, KT - 1, i))
                for c, n in enumerate(TROWS):
                    for i in range(2):
                        out = pick_g if i == 0 else pick_two
                        step(tsc(out[0:n, c, :], c_("place", n), place_of[0:n, i, c:c + 1],
                                 r1[0:n, 2 + i, c:c + 1], ALU.is_equal, ALU.mult))
                wait()
                for c, n in enumerate(TROWS):
                    ins = tt(pick_g[0:n, c, :], pick_g[0:n, c, :], pick_two[0:n, c, :], ALU.add)
                ins.then_inc(pick_g_ready, 1)

                def take_window(e, start):
                    nc.vector.tensor_copy(xw[:, e, :, :], x_sorted[:, :, ds(start, WIN)]).then_inc(xw_ready, 1)

                def start_of(w):
                    return dve.value_load(start_ids[0:1, w], min_val=0, max_val=PICKS)

                dve.wait_ge(windows_ready, l + 1)
                starts_01 = [start_of(slice(e, e + 1)) for e in range(2)]
                for k in range(KT - 4, KT):
                    for i in range(2):
                        moved(dve, ("sorted", l, k, i))
                for e in range(2):
                    take_window(e, starts_01[e])
                with dve.Fori(0, NE // 2) as it:
                    nxt = [start_of(ds(it * 2 + (2 + e), 1)) for e in range(2)]
                    for e in range(2):
                        ps = result(dve, ("GU", l, e), it)
                        dve.wait_ge(silu_ready, it * 2 + (l * NE + e + 1))
                        tt(aff[:, e, :], ps[:, FF:2 * FF], act_g[:, e, :], ALU.mult) \
                            .then_inc(free(("GU", l, e)), 1)
                        take_window(e, nxt[e])
                    for e in range(2):
                        ps = result(dve, ("Y", l, e, 1), it)
                        dve.wait_ge(y_stored[e], it * 16 + 16 * l * (NE // 2))
                        nc.vector.tensor_copy(y_sb[:, e, 512:D], ps[:]).then_inc(free(("Y", l, e, 1)), 1)
                with dve.If(further(dve, l) > 0):
                    dve.wait_ge(y_stored[0], 16 * (l + 1) * (NE // 2))
                    with dve.Fori(0, XW) as i:
                        start = start_of(ds(i + NE, 1))
                        nc.vector.tensor_copy(xw[:, 0, :, :], x_sorted[:, :, ds(start, WIN)]).then_inc(far_moved[l], 1)
                        dve.wait_ge(far_product[l], i * 3 + 1)
                        dve.wait_ge(far_silu[l], i + 1)
                        tt(aff[:, 0, :], bank[0][:, FF:2 * FF], act_g[:, 0, :], ALU.mult).then_inc(far_moved[l], 1)
                        dve.wait_ge(far_product[l], i * 3 + 2)
                        nc.vector.tensor_copy(aff_T[:, 0, :, :], bank[2][:, 0:2 * P].rearrange("p (m n) -> p m n", m=2)) \
                            .then_inc(far_moved[l], 1)
                        dve.wait_ge(far_product[l], i * 3 + 3)
                        dve.wait_ge(far_stored[l], i * 16)
                        for n in range(2):
                            ins = nc.vector.tensor_copy(y_sb[:, 0, n * 512:(n + 1) * 512], bank[4 + n][:])
                        ins.then_inc(far_moved[l], 1)
                gate = mod[l][:, 8 * GT2:8 * GT2 + 8, :]
                for k in range(KT):
                    ps = result(dve, ("sum", l, k))
                    step(tt(ms[:, k, :], ps[:, TP:T], gate[:, k, 1:NC], ALU.mult))
                    stt(x[:, k, 0:TP], ps[:, 0:TP], gate[:, k, 0:1], x[:, k, 0:TP], ALU.mult, ALU.add) \
                        .then_inc(free(("sum", l, k)), 1)
                wait()
                tt(x[:, :, TP:T], x[:, :, TP:T], ms[:], ALU.add).then_inc(x_ready, 1)

            moe(0)

            normalise(2)
            modulate(n2, coef, G_KV, kvmod, 0, 1)
            modulate(h, coef2, G_MIX1, mod[1], SH1, SC1)
            ps = result(dve, "flogit")
            tsc(fz[:, 0, :], ps[0:FH, 0:T], vec[0:FH, V_BF:V_BF + 1], None, ALU.add).then_inc(free("flogit"), 1)
            moved(dve, "flogit")
            stt(fz[:, 1, :], fz[:, 0, :], -1.0, fz[:, 0, :], ALU.mult, ALU.min).then_inc(f_neg, 1)
            dve.wait_ge(f_exp, 2)
            stt(fz[:, 1, :], fz[:, 0, :], 0.0, fz[:, 3, :], ALU.min, ALU.subtract).then_inc(logf_ready, 1)
            dve.wait_ge(logf_ready, 1)
            tt(lf_diag, bc(ident[0:FH, 0:FH].unsqueeze(1), [FH, NS, FH]),
               bc(fz[:, 1, TP:T].unsqueeze(2), [FH, NS, FH]), ALU.mult).then_inc(diag_ready, 1)
            ps = result(dve, "logfT")
            nc.vector.tensor_copy(lf_tok, ps[:, 0:2 * FH].rearrange("p (c n) -> p c n", c=2)) \
                .then_inc(free("logfT"), 1)
            ps = result(dve, "F")
            nc.vector.tensor_copy(Fsb, ps[0:FH, 0:TP]).then_inc(free("F"), 1)
            for i in range(4):
                ps = result(dve, ("fvs", i))
                nc.vector.tensor_copy(q_one[:, i * 256:(i + 1) * 256], ps[0:NS, 0:256]) \
                    .then_inc(free(("fvs", i)), 1)
            moved(dve, ("fk", 3, 0))
            moved(dve, ("fk", 3, 1))
            moved(dve, ("fq", 3, 0))
            moved(dve, ("fq", 3, 1))
            tt(own, fq[:, :, TP:T], fk[:, :, TP:T], ALU.mult).then_inc(own_ready, 1)
            ps = result(dve, "own_F")
            tt(s_own, ps[:, 0:NS * FH].rearrange("p (b h) -> p b h", b=NS),
               past_tot[:].rearrange("p (b h) -> p b h", b=NS), ALU.add).then_inc(free("own_F"), 1)
            moved(dve, "own_F")
            ps = result(dve, "own_score")
            for r in range(2):
                view = s_own.rearrange("p b (t r) -> p r b t", r=2)[:, r, :, :]
                ins = tt(view, ps[:, r * 64:(r + 1) * 64].rearrange("p (t b) -> p b t", t=KT), view, ALU.subtract)
            ins.then_inc(free("own_score"), 1)
            ps = result(dve, "fvsT")
            nc.vector.tensor_copy(fvs, ps[:, 0:KT * NS].rearrange("p (t b) -> p t b", b=NS)) \
                .then_inc(free("fvsT"), 1)
            for i in range(2):
                ps = result(dve, ("qrow", i))
                nc.vector.tensor_copy(q_row[:, i * 512:(i + 1) * 512], ps[0:NS, :]).then_inc(free(("qrow", i)), 1)
            for key in ("own_score", "F", "fvsT", ("qrow", 0), ("qrow", 1)):
                moved(dve, key)
            dve.wait_ge(vs_stored, 16)

            def one_query(b):
                tsc(q_one, q_row, ident[0:NS, ds(b, 1)], None, ALU.mult).then_inc(one_ready, 1)

            one_query(0)
            moved(dve, ("qb", 0, "pre"))
            moved(dve, ("qb", 1, "pre"))

            half = [slice(64 * r, 64 * r + 64) for r in range(2)]

            def by_half(a, r):
                return a[half[r]].rearrange("p (t r) -> p r t", r=2)[:, r, :]

            def window(tag, b, it=None):
                if tag != "first":
                    dve.wait_ge(pd_ready, b)
                    wait()
                    step(nc.vector.tensor_copy(pO1, pO))
                    wait()
                    step(nc.vector.tensor_copy(dinv1, dinv))
                if tag != "last":
                    for hh in range(2):
                        ins = tsc(negF[:, hh, :], Fsb, c_("negeye", FH)[:, ds(b * 2 + hh, 1)], None, ALU.mult)
                    ins.then_inc(negF_ready, 1)

                def multiply(j, b=b):
                    dve.wait_ge(k_in[j % 4], b * 32 + 16 * (j // 4 + 1))
                    tt(prod[:, j % 2, :], kpg[:, j % 4, :], qb, ALU.mult).then_inc(k_used, 1)

                def add_up(j, b=b):
                    dve.wait_ge(k_used, b * NPG + (j + 1))
                    step(nc.vector.tensor_reduce(sc[:, j * FH:(j + 1) * FH],
                                                 prod[:, j % 2, :].rearrange("p (h d) -> p h d", h=FH), AX, ALU.add))

                def head_max(hh):
                    ps = result(dve, ("ps", hh, tag), it)
                    tt(s_sb[:, hh, :], ps[:, 0:3 * P], c_("causal"), ALU.add).then_inc(free(("ps", hh, tag)), 1)
                    moved(dve, ("ps", hh, tag), it)
                    nc.vector.tensor_reduce(hmax[:, hh, 0:1], s_sb[:, hh, 0:P], AX, ALU.max)
                    step(nc.vector.tensor_reduce(hmax[:, hh, 1:2], s_sb[:, hh, P:3 * P], AX, ALU.max))
                    wait()
                    tsc(hneg[:, hh, :], hmax[:, hh, :], -1.0, None, ALU.mult).then_inc(neg_max, 1)

                def norm_p(hh):
                    dve.wait_ge(p_raw, b * 2 + (hh + 1))
                    step(nc.vector.reciprocal(hinv[:, hh, :], hsum[:, hh, :]))
                    wait()
                    tsc(p_sb[:, hh, 0:P], p_sb[:, hh, 0:P], hinv[:, hh, 0:1], None, ALU.mult)
                    tsc(p_sb[:, hh, P:3 * P], p_sb[:, hh, P:3 * P], hinv[:, hh, 1:2], None, ALU.mult) \
                        .then_inc(p_ready, 1)

                if tag != "last":
                    if tag == "first":
                        multiply(0)
                        add_up(0)
                    for j in range(1, NPG + 1):
                        if j < NPG:
                            if j > 1:
                                wait()
                            multiply(j)
                        if j > 1:
                            add_up(j - 1)
                        if j in (2, 3):
                            head_max(j - 2)
                        if j in (4, 5):
                            norm_p(j - 4)
                        if j == 5:
                            one_query(b + 1)
                    wait()
                    step(tt(sF, sc, past_F[:, ds(b, 1), :].rearrange("p a c -> p (a c)"), ALU.subtract))
                    wait()
                    nc.vector.tensor_reduce(mxp, sF.rearrange("p (g h) -> p h g", g=NPG), AX, ALU.max) \
                        .then_inc(mxp_ready, 1)
                    ps = result(dve, ("mxT", tag), it)
                    nc.vector.tensor_reduce(mx1, ps[0:FH, 0:P], AX, ALU.max).then_inc(free(("mxT", tag)), 1)
                    moved(dve, ("mxT", tag), it)
                    tsc(mxd, ident[0:FH, 0:FH], mx1, None, ALU.mult).then_inc(mxd_ready, 1)
                    if tag != "end":
                        for i in range(2):
                            moved(dve, ("qb", i, tag), it)
                        multiply(0, b + 1)
                    ps = result(dve, ("mxb", tag), it)
                    own_b = s_own[:, ds(b, 1), :].rearrange("p a h -> p (a h)")
                    tt(mx, ps[:, 0:FH], own_b, ALU.max).then_inc(free(("mxb", tag)), 1)
                    moved(dve, ("mxb", tag), it)
                    tt(sF.rearrange("p (g h) -> p g h", g=NPG), sF.rearrange("p (g h) -> p g h", g=NPG),
                       bc(mx.unsqueeze(1), [P, NPG, FH]), ALU.subtract)
                    tt(sO, own_b, mx, ALU.subtract).then_inc(shifted, 1)
                    if tag != "end":
                        add_up(0, b + 1)
                    dve.wait_ge(pE_ready, b + 1)
                    nc.vector.tensor_reduce(psm, pE.rearrange("p (g h) -> p h g", g=NPG), AX, ALU.add) \
                        .then_inc(psm_ready, 1)
                    ps = result(dve, ("den", tag), it)
                    tt(den, ps[:, 0:FH], pO, ALU.add).then_inc(free(("den", tag)), 1)
                    moved(dve, ("den", tag), it)
                    step(nc.vector.reciprocal(dinv, den))
                if tag != "first":
                    for r in range(2):
                        step(tt(oO[half[r]], by_half(pO1, r),
                                fvs[half[r], :, ds(b - 1, 1)].rearrange("p t a -> p (t a)"), ALU.mult))
                    ps = result(dve, ("oT", tag), it)
                    wait()
                    for r in range(2):
                        ins = tt(oS[half[r]], ps[half[r], r:r + (FH + 2) * (KT - 1) + 1:FH + 2], oO[half[r]], ALU.add)
                    ins.then_inc(free(("oT", tag)), 1)
                    moved(dve, ("oT", tag), it)
                    for r in range(2):
                        ins = tt(fo[half[r], :, ds(b + (TP - 1), 1)].rearrange("p t a -> p (t a)"), oS[half[r]],
                                 by_half(dinv1, r), ALU.mult)
                    ins.then_inc(sample_done, 1)

            window("first", 0)
            with dve.Fori(0, NS - 2) as it:
                own_steps.enter(it, 18)
                window("mid", it + 1, it)
                own_steps.leave(NS - 2)
            window("end", NS - 1)
            window("last", NS)

            residual("fout", mod[1][:, 8 * GT1:8 * GT1 + 8, :])
            moe(1)
            normalise(4)
            wait()
            tt(h[:], xn[:], bc(gain[G_FINAL].unsqueeze(2), [P, KT, T]), ALU.mult).then_inc(h_ready, 1)


def constants():
    c = np.zeros((P, N_CONST), np.float32)

    def put(name, value):
        a, n = CONST[name]
        c[:, a:a + n] = value

    i = np.arange(P)
    put("ident", np.eye(P))
    put("ones", 1.0)
    put("half0", (i < 64)[:, None])
    put("half1", (i >= 64)[:, None])
    inv = np.float32(10000.0) ** (-i.astype(np.float32) / np.float32(P))
    pos = np.concatenate([np.arange(TP), np.full(NS, PAST)]).astype(np.float32)
    angle = (pos[None, :] * inv.astype(np.float32)[:, None]).astype(np.float32).astype(np.float64)
    for name, f in (("cos", np.cos), ("sin", np.sin)):
        put(name + "q", f(angle))
        put(name + "k", f(angle).astype(np.float32) * np.float32(RK ** -0.5))
    log_gamma = np.log(np.array(GAMMA, np.float32)).astype(np.float64)
    rel = np.arange(TP)[None, :] - i[:, None]
    for hd in range(RH):
        a = CONST["decay"][0] + hd * TP
        c[:, a:a + TP] = np.where(rel >= 0, np.exp(log_gamma[hd] * np.maximum(rel, 0)), 0.0)
        for k in range(2):
            c[:, CONST["kdec"][0] + k * RH + hd] = np.exp(log_gamma[hd] * (TP - 1 - k * P - i))
    put("upto", rel >= 0)
    future = np.where(i[None, :] <= i[:, None], 0.0, NEG)
    put("causal", np.concatenate([future, np.zeros((P, P)), future], 1))
    c[0:FH, CONST["negeye"][0]:CONST["negeye"][0] + FH] = -np.eye(FH)
    put("eps", EPS)
    put("first4", NG - np.arange(NG))
    put("first8", EG - np.arange(EG))
    put("place", 1 + np.arange(PICKS))
    e = np.arange(NE)
    a = CONST["before"][0]
    c[0:NE, a:a + 2 * NE] = np.concatenate([e[:, None] < e[None, :], np.eye(NE)], 1)
    gu, dn = GU_LAST - np.array(GU_SLOT), DN_LAST - np.array(DN_SLOT)
    put("back", np.concatenate([gu, gu, dn, dn]))
    return c


def features(a):
    return np.ascontiguousarray(a.reshape(a.shape[0], -1, P).transpose(2, 1, 0))


def column_slots(w):
    return w.reshape(KT, P, -1, 256).transpose(2, 1, 0, 3).reshape(-1, P, SW)


def weight_stream(w_mod, w_kvmod, w_ret_in, w_ret_out, w_kv, w_fq, w_fo, w_gate, w_up, w_down):
    s = np.empty((SLOTS, P, SW), np.float32)
    s[S_MOD0:S_MOD0 + 24] = column_slots(w_mod[0])
    s[S_RET:S_RET + 48:2] = column_slots(w_ret_in)
    s[S_RET + 1:S_RET + 48:2] = column_slots(w_mod[1])
    s[S_RO:S_RO + 16:2] = w_ret_out.reshape(2, KT, P, 4, 256).transpose(3, 0, 2, 1, 4).reshape(8, P, SW)
    s[S_RO + 1:S_RO + 16:2] = column_slots(w_kvmod)
    s[S_KV:S_KV + 8] = column_slots(w_kv)
    s[S_FQ:S_FQ + 4] = column_slots(w_fq)
    s[S_FO:S_FO + 4] = column_slots(w_fo)
    for l, base in ((0, S_MOE0), (1, S_MOE1)):
        m = s[base:base + 3 * NE].reshape(NE // 2, 6, P, SW)
        gu = np.stack([w_gate[l].reshape(2, 4, P, NE // 2, 2, FF), w_up[l].reshape(2, 4, P, NE // 2, 2, FF)], 5)
        m[:, 0:4] = gu.transpose(3, 4, 0, 2, 1, 5, 6).reshape(NE // 2, 4, P, SW)
        m[:, 4:6] = w_down[l].reshape(NE // 2, 2, 2, P, D).transpose(0, 1, 3, 2, 4).reshape(NE // 2, 2, P, SW)
    return s


def kernel(x_prompt, x_sample, c_prompt, c_sample, state_ret, cache_k, cache_v, cache_logf, page_table,
           w_mod, b_mod, g_mix, g_ffn, w_ret_in, w_ret_out, g_kv, w_kvmod, b_kvmod, w_kv, w_f, b_f,
           w_fq, w_fo, w_rg, w_re, w_e_gate, w_e_up, w_e_down, g_final):
    import concourse.bacc as bacc
    from concourse.bass_utils import run_bass_kernel_spmd

    a = {k: np.asarray(v) for k, v in locals().items() if k not in ("bacc", "run_bass_kernel_spmd")}
    pool = a["cache_k"].shape[0]
    vectors = np.zeros((P, N_VEC), np.float32)
    vectors[:, V_BMOD:V_BMOD + 96] = a["b_mod"].reshape(96, P).T
    vectors[:, V_BKV:V_BKV + 16] = a["b_kvmod"].reshape(16, P).T
    gains = (a["g_mix"][0], a["g_mix"][1], a["g_ffn"][0], a["g_ffn"][1], a["g_kv"], a["g_final"])
    vectors[:, V_GAIN:V_GAIN + 48] = np.concatenate(gains).reshape(48, P).T
    vectors[0:FH, V_BF] = a["b_f"]
    small = [a["w_f"].reshape(KT, P, FH).transpose(1, 0, 2).reshape(P, -1)]
    for l in range(2):
        both = np.concatenate([a["w_rg"][l], a["w_re"][l]], 1)
        small.append(both.reshape(KT, P, 36).transpose(1, 0, 2).reshape(P, -1))
    ins = {
        "consts": constants(),
        "x_in": features(np.concatenate([a["x_prompt"][0], a["x_sample"][:, 0]])),
        "c_in": features(np.concatenate([a["c_prompt"], a["c_sample"]])),
        "vecs": vectors,
        "wsmall": np.concatenate(small, 1),
        "wstream": weight_stream(a["w_mod"], a["w_kvmod"], a["w_ret_in"][0], a["w_ret_out"][0], a["w_kv"],
                                 a["w_fq"][0], a["w_fo"][0], a["w_e_gate"], a["w_e_up"], a["w_e_down"]),
        "kcache": a["cache_k"].reshape(pool, PAGE, D),
        "vcache": a["cache_v"].reshape(pool, PAGE, D),
        "lfcache": a["cache_logf"],
        "ptable": a["page_table"].reshape(1, NPAGES),
        "state": a["state_ret"].reshape(NS * RH, 2, P, RV).transpose(0, 2, 1, 3),
    }
    outs = {
        "y_out": (P, KT, T), "sp_out": (RH, P, 2, RV), "ss_out": (NS * RH, P, 2, RV), "k_out": (P, KT, T),
        "vp_out": (P, 2, D), "vs_out": (NS, D), "lf_out": (FH, T),
    }
    nc = bacc.Bacc("TRN2", target_bir_lowering=False, num_devices=1)
    arrays, args = {}, []
    for name, v in ins.items():
        v = np.ascontiguousarray(v)
        arrays[name] = v
        args.append(nc.dram_tensor(name, v.shape, mybir.dt.from_np(v.dtype), kind="ExternalInput").ap())
    for name, shape in outs.items():
        args.append(nc.dram_tensor(name, shape, F32, kind="ExternalOutput").ap())
    build(nc, *args)
    r = run_bass_kernel_spmd(nc, [arrays], core_ids=[0]).results[0]

    y = r["y_out"].transpose(2, 1, 0).reshape(T, D)
    k = r["k_out"].transpose(2, 1, 0).reshape(T, FH, HD)
    vp = r["vp_out"].transpose(1, 0, 2).reshape(1, TP, FH, HD)
    vs = r["vs_out"].reshape(NS, 1, FH, HD)
    lf = r["lf_out"].T
    sp = r["sp_out"].transpose(0, 2, 1, 3).reshape(1, 1, RH, RK, RV)
    ss = r["ss_out"].transpose(0, 2, 1, 3).reshape(1, NS, RH, RK, RV)
    return (y[None, :TP], y[TP:, None], sp, ss, k[None, :TP], vp, lf[None, :TP], k[TP:, None], vs, lf[TP:, None])
```
